# Optimizing a Trainium2 kernel written in Bass

```python
import jax, jax.numpy as jnp
from jax import lax
import numpy as np

D_MODEL = 1024
BATCH = 1
SEQ = 512
DEPTH = 1
DEC_BATCH = 1
DEC_SEQ = 1024
PAST_LEN = 128

HEAD_DIM = 64
HQ_A = 8
HKV_A = 2
H_B = 8
D_MIX = (HQ_A + H_B) * HEAD_DIM
SPLITS = (HQ_A * HEAD_DIM,
          HQ_A * HEAD_DIM + HKV_A * HEAD_DIM,
          HQ_A * HEAD_DIM + 2 * HKV_A * HEAD_DIM,
          HQ_A * HEAD_DIM + 2 * HKV_A * HEAD_DIM + H_B * HEAD_DIM,
          HQ_A * HEAD_DIM + 2 * HKV_A * HEAD_DIM + 2 * H_B * HEAD_DIM)
D_IN = HQ_A * HEAD_DIM + 2 * HKV_A * HEAD_DIM + 3 * H_B * HEAD_DIM
WINDOW = 128
BLK = 128
ROPE_THETA = 500000.0
ROT_DIM = HEAD_DIM // 4
GRID_W = 64
NA_ROWS = 8
NA_COLS = 16
NA_QROWS = 2
N_COLBLK = GRID_W // NA_COLS
KEY_COLS = 2 * NA_COLS
N_EXPERTS = 16
CAP_FACTOR = 2
D_EXPERT = 2 * D_MODEL
RMS_EPS = 1e-6
NEG_INF = -1e30

kernel_name = "hymba_window_natten_ec_moe_encoder"

def _rmsnorm(x, g):
    xf = x.astype(jnp.float32)
    y = xf * lax.rsqrt(jnp.mean(xf * xf, axis=-1, keepdims=True) + RMS_EPS)
    return (y * g.astype(jnp.float32)).astype(x.dtype)

def _partial_rotary(x):
    S = x.shape[1]
    half = ROT_DIM // 2
    inv_freq = jnp.float32(ROPE_THETA) ** (-(jnp.arange(half, dtype=jnp.float32) * 2.0) / ROT_DIM)
    ang = jnp.arange(S, dtype=jnp.float32)[:, None] * inv_freq[None, :]
    cos = jnp.cos(ang)[None, :, None, :]
    sin = jnp.sin(ang)[None, :, None, :]
    xf = x.astype(jnp.float32)
    x1 = xf[..., :half]
    x2 = xf[..., half:ROT_DIM]
    out = jnp.concatenate([x1 * cos - x2 * sin, x2 * cos + x1 * sin, xf[..., ROT_DIM:]], axis=-1)
    return out.astype(x.dtype)

def _window_attention(q, k, v, sink):
    B, S = q.shape[0], q.shape[1]
    nb = S // BLK
    grp = HQ_A // HKV_A
    qb = q.reshape(B, nb, BLK, HKV_A, grp, HEAD_DIM)
    pad = ((0, 0), (BLK, BLK), (0, 0), (0, 0))
    kp = jnp.pad(k, pad).reshape(B, nb + 2, BLK, HKV_A, HEAD_DIM)
    vp = jnp.pad(v, pad).reshape(B, nb + 2, BLK, HKV_A, HEAD_DIM)
    kw = jnp.concatenate([kp[:, :-2], kp[:, 1:-1], kp[:, 2:]], axis=2)
    vw = jnp.concatenate([vp[:, :-2], vp[:, 1:-1], vp[:, 2:]], axis=2)
    s = jnp.einsum('bnqhgd,bnkhd->bnhgqk', qb, kw).astype(jnp.float32) * (HEAD_DIM ** -0.5)
    qi = jnp.arange(BLK)[:, None]
    kj = jnp.arange(3 * BLK)[None, :]
    kpos = (jnp.arange(nb)[:, None, None] - 1) * BLK + kj[None]
    valid = (jnp.abs(kj - BLK - qi) <= WINDOW)[None] & (kpos >= 0) & (kpos < S)
    s = jnp.where(valid[None, :, None, None], s, NEG_INF)
    sb = sink.astype(jnp.float32).reshape(1, 1, HKV_A, grp, 1, 1)
    m = jnp.maximum(jnp.max(s, axis=-1, keepdims=True), sb)
    p = jnp.exp(s - m)
    denom = jnp.sum(p, axis=-1, keepdims=True) + jnp.exp(sb - m)
    o = jnp.einsum('bnhgqk,bnkhd->bnqhgd', (p / denom).astype(v.dtype), vw)
    return o.reshape(B, S, HQ_A * HEAD_DIM)

def _neighbourhood_attention(q, k, v, rpb):
    B, S = q.shape[0], q.shape[1]
    rows = S // GRID_W
    kr = min(NA_ROWS, rows)
    qr = NA_QROWS
    krb = min(kr + qr - 1, rows)
    nrb = rows // qr
    qg = q.reshape(B, rows, GRID_W, H_B, HEAD_DIM)
    kg = k.reshape(B, rows, GRID_W, H_B, HEAD_DIM)
    vg = v.reshape(B, rows, GRID_W, H_B, HEAD_DIM)
    qc = np.arange(GRID_W).reshape(N_COLBLK, NA_COLS)
    kc0 = np.clip(np.arange(N_COLBLK) * NA_COLS - NA_COLS // 2, 0, GRID_W - KEY_COLS)
    kc = kc0[:, None] + np.arange(KEY_COLS)[None, :]
    cs = np.clip(qc - NA_COLS // 2, 0, GRID_W - NA_COLS)
    col_ok = (kc[:, None, :] >= cs[:, :, None]) & (kc[:, None, :] < cs[:, :, None] + NA_COLS)
    cidx = np.clip(kc[:, None, :] - qc[:, :, None] + NA_COLS - 1, 0, 2 * NA_COLS - 2)
    nkeys = krb * KEY_COLS
    scale = HEAD_DIM ** -0.5

    def row_block(rb):
        r0 = rb * qr
        qrows = r0 + jnp.arange(qr)
        rs = jnp.clip(qrows - kr // 2, 0, rows - kr)
        kstart = jnp.clip(r0 - kr // 2, 0, rows - krb)
        krows = kstart + jnp.arange(krb)
        qb = lax.dynamic_slice_in_dim(qg, r0, qr, axis=1).reshape(B, qr, N_COLBLK, NA_COLS, H_B, HEAD_DIM)
        kb = lax.dynamic_slice_in_dim(kg, kstart, krb, axis=1)[:, :, kc]
        vb = lax.dynamic_slice_in_dim(vg, kstart, krb, axis=1)[:, :, kc]
        kb = kb.transpose(0, 2, 1, 3, 4, 5).reshape(B, N_COLBLK, nkeys, H_B, HEAD_DIM)
        vb = vb.transpose(0, 2, 1, 3, 4, 5).reshape(B, N_COLBLK, nkeys, H_B, HEAD_DIM)
        row_ok = (krows[None, :] >= rs[:, None]) & (krows[None, :] < rs[:, None] + kr)
        ridx = jnp.clip(krows[None, :] - qrows[:, None] + NA_ROWS - 1, 0, 2 * NA_ROWS - 2)
        valid = (row_ok[None, :, None, :, None] & col_ok[:, None, :, None, :]).reshape(
            N_COLBLK, qr, NA_COLS, nkeys)
        bias = rpb.astype(jnp.float32)[:, ridx[None, :, None, :, None], cidx[:, None, :, None, :]]
        bias = bias.reshape(H_B, N_COLBLK, qr, NA_COLS, nkeys)
        s = jnp.einsum('brjchd,bjkhd->bhjrck', qb, kb).astype(jnp.float32) * scale + bias[None]
        s = jnp.where(valid[None, None], s, NEG_INF)
        p = jax.nn.softmax(s, axis=-1).astype(v.dtype)
        o = jnp.einsum('bhjrck,bjkhd->brjchd', p, vb)
        return o.reshape(B, qr, GRID_W, H_B * HEAD_DIM)

    out = lax.map(row_block, jnp.arange(nrb))
    return out.transpose(1, 0, 2, 3, 4).reshape(B, S, H_B * HEAD_DIM)

def _mixers(hn, w_in, g_out_a, g_out_b, sink_a, rpb_b, w_out):
    B, S = hn.shape[0], hn.shape[1]
    proj = jnp.einsum('bsd,de->bse', hn, w_in)
    qa, ka, va, qb, kb, vb = jnp.split(proj, list(SPLITS), axis=-1)
    qa = _partial_rotary(qa.reshape(B, S, HQ_A, HEAD_DIM))
    ka = _partial_rotary(ka.reshape(B, S, HKV_A, HEAD_DIM))
    va = va.reshape(B, S, HKV_A, HEAD_DIM)
    oa = _window_attention(qa, ka, va, sink_a)
    ob = _neighbourhood_attention(qb.reshape(B, S, H_B, HEAD_DIM), kb.reshape(B, S, H_B, HEAD_DIM),
                                  vb.reshape(B, S, H_B, HEAD_DIM), rpb_b)
    merged = jnp.concatenate([_rmsnorm(oa, g_out_a), _rmsnorm(ob, g_out_b)], axis=-1)
    return jnp.einsum('bse,ed->bsd', merged, w_out)

def _expert_choice_ffn(h, w_router, w_gate, w_up, w_down):
    N, D = h.shape
    cap = CAP_FACTOR * N // N_EXPERTS
    aff = jax.nn.softmax(jnp.einsum('nd,de->ne', h, w_router).astype(jnp.float32), axis=-1)
    gate, idx = lax.top_k(aff.T, cap)
    xe = h[idx]
    hid = jax.nn.silu(jnp.einsum('ecd,edf->ecf', xe, w_gate)) * jnp.einsum('ecd,edf->ecf', xe, w_up)
    ye = jnp.einsum('ecf,efd->ecd', hid, w_down) * gate[..., None].astype(h.dtype)
    return jnp.zeros_like(h).at[idx.reshape(-1)].add(ye.reshape(-1, D))

def _encoder_layer(x, g_attn, w_in, g_out_a, g_out_b, sink_a, rpb_b, w_out,
                   g_ffn, w_router, w_gate, w_up, w_down):
    B, S, D = x.shape
    x = x + _mixers(_rmsnorm(x, g_attn), w_in, g_out_a, g_out_b, sink_a, rpb_b, w_out)
    h = _rmsnorm(x, g_ffn).reshape(B * S, D)
    return x + _expert_choice_ffn(h, w_router, w_gate, w_up, w_down).reshape(B, S, D)

def setup_inputs(seed: int = 0) -> dict:
    key = jax.random.key(seed)
    ks = jax.random.split(key, 16)
    f32 = jnp.float32
    nrm = lambda k, shape, s: jax.random.normal(k, shape, f32) * s
    return {
        "x_prompt": nrm(ks[0], (BATCH, SEQ, D_MODEL), 1.0),
        "x_sample": nrm(ks[1], (DEC_BATCH, DEC_SEQ, D_MODEL), 1.0),
        "g_attn": 1.0 + nrm(ks[2], (DEPTH, D_MODEL), 0.01),
        "w_in": nrm(ks[3], (DEPTH, D_MODEL, D_IN), D_MODEL ** -0.5),
        "g_out_a": 1.0 + nrm(ks[4], (DEPTH, HQ_A * HEAD_DIM), 0.01),
        "g_out_b": 1.0 + nrm(ks[5], (DEPTH, H_B * HEAD_DIM), 0.01),
        "sink_a": nrm(ks[6], (DEPTH, HQ_A), 0.5),
        "rpb_b": nrm(ks[7], (DEPTH, H_B, 2 * NA_ROWS - 1, 2 * NA_COLS - 1), 0.1),
        "w_out": nrm(ks[8], (DEPTH, D_MIX, D_MODEL), D_MIX ** -0.5),
        "g_ffn": 1.0 + nrm(ks[9], (DEPTH, D_MODEL), 0.01),
        "w_router": nrm(ks[10], (DEPTH, D_MODEL, N_EXPERTS), D_MODEL ** -0.5),
        "w_gate": nrm(ks[11], (DEPTH, N_EXPERTS, D_MODEL, D_EXPERT), D_MODEL ** -0.5),
        "w_up": nrm(ks[12], (DEPTH, N_EXPERTS, D_MODEL, D_EXPERT), D_MODEL ** -0.5),
        "w_down": nrm(ks[13], (DEPTH, N_EXPERTS, D_EXPERT, D_MODEL), D_EXPERT ** -0.5),
        "g_final": 1.0 + nrm(ks[14], (D_MODEL,), 0.01),
    }

def reference(x_prompt, x_sample, g_attn, w_in, g_out_a, g_out_b, sink_a, rpb_b, w_out,
              g_ffn, w_router, w_gate, w_up, w_down, g_final):
    h_p = x_prompt
    h_s = x_sample
    for l in range(DEPTH):
        h_p = _encoder_layer(h_p, g_attn[l], w_in[l], g_out_a[l], g_out_b[l], sink_a[l], rpb_b[l], w_out[l],
                             g_ffn[l], w_router[l], w_gate[l], w_up[l], w_down[l])
        h_s = _encoder_layer(h_s, g_attn[l], w_in[l], g_out_a[l], g_out_b[l], sink_a[l], rpb_b[l], w_out[l],
                             g_ffn[l], w_router[l], w_gate[l], w_up[l], w_down[l])
    y_prompt = _rmsnorm(h_p, g_final)
    y_sample = _rmsnorm(h_s, g_final)
    return (y_prompt, y_sample)


_drawn_inputs = setup_inputs


def setup_inputs(seed=0):
    import zlib

    import numpy as np

    out = dict(_drawn_inputs(seed))
    spreads = {}
    factors = {'g_attn': 3.62,
     'g_out_a': 7.271,
     'g_out_b': 17.638,
     'sink_a': 64.0,
     'g_ffn': 6.211,
     'g_final': 32.886}
    for name, (base, spread) in spreads.items():
        noise = np.random.default_rng([zlib.crc32(name.encode()), seed]).standard_normal(out[name].shape)
        drawn = base * np.exp(spread * noise) if base else spread * noise
        out[name] = __import__('jax').numpy.asarray(drawn.astype(out[name].dtype))
    for name, factor in factors.items():
        out[name] = (out[name] * factor).astype(out[name].dtype)
    return out
```

```python
import numpy as np
from contextlib import ExitStack
import concourse.bass as bass
from concourse import mybir

F32 = mybir.dt.float32
F32R = mybir.dt.float32r
BF16 = mybir.dt.bfloat16
U32 = mybir.dt.uint32
ACT = mybir.ActivationFunctionType
ALU = mybir.AluOpType
AX = mybir.AxisListType

P = 128
D = 1024
DT = D // P
S_TOK, P_TOK = 1024, 512
TOK = S_TOK + P_TOK
TILES = TOK // P
S_TILES = S_TOK // P
GROUP = 512
G_TILES = GROUP // P
GROUPS = TOK // GROUP
HD = 64
ROT_HALF = 8
GRID_W = 64
KEY_ROWS = 8
QA, KA, QB, KB = 4, 1, 4, 4
V_CHUNKS = 5
ROTATED = QA + KA
CHUNKS = QA + KA + QB + KB + V_CHUNKS
FIRST_V = CHUNKS - V_CHUNKS
EPS = 1e-6
SCALE = float(HD) ** -0.5
NEG = -1e30
EXPERTS = 16
DF = 2048
FT = DF // P
S_CAP, P_CAP = 2 * S_TOK // EXPERTS, 2 * P_TOK // EXPERTS
CAP = S_CAP + P_CAP
PROMPT_AT = 32


class Heads:

    def __init__(self, q, k, v):
        self.q, self.k, self.v = q, k, v


class Route:

    def __init__(self, rows, gates, index):
        self.rows, self.gates, self.index = rows, gates, index


def buffers(nc, ctx):
    def sb(name, shape, dt=F32):
        return ctx.enter_context(nc.sbuf_tensor(name, shape, dt))

    def ps(name, shape, dt=F32):
        return ctx.enter_context(nc.psum_tensor(name, shape, dt))

    def sem(name):
        return ctx.enter_context(nc.semaphore(name))

    return sb, ps, sem


def three_pass(nc, out, stationary, moving, first, last):
    (sh, sl), (mh, ml) = stationary, moving
    nc.tensor.matmul(out, sh, mh, start=first, stop=False)
    nc.tensor.matmul(out, sh, ml, start=False, stop=False)
    return nc.tensor.matmul(out, sl, mh, start=False, stop=last)


START = 1
REFINE = 6


def inverse_root(dve, step, done, ss, rt, tmp, out, scale):
    mean, sq, corr = tmp
    dve.reciprocal(out, rt).then_inc(step, 1)
    dve.tensor_scalar(mean, ss, scale, EPS, ALU.mult, ALU.add).then_inc(step, 1)
    dve.wait_ge(step, done + 2)
    dve.tensor_tensor(sq, out, out, ALU.mult).then_inc(step, 1)
    dve.wait_ge(step, done + 3)
    dve.tensor_tensor(corr, sq, mean, ALU.mult).then_inc(step, 1)
    dve.wait_ge(step, done + 4)
    dve.tensor_scalar(sq, corr, -0.5, 1.5, ALU.mult, ALU.add).then_inc(step, 1)
    dve.wait_ge(step, done + 5)
    dve.tensor_tensor(out, out, sq, ALU.mult).then_inc(step, 1)
    dve.wait_ge(step, done + 6)


def project(nc, d, keep):
    ctx = ExitStack()
    with ctx:
        sb, ps, sem = buffers(nc, ctx)
        X_SLOTS, W_SLOTS, AHEAD = 2, 3, 2
        x = sb("pj_x", [P, X_SLOTS, D])
        xn = sb("pj_xn", [P, D])
        junk = sb("pj_junk", [P, D], BF16)
        gain = sb("pj_gain", [P, D])
        eps = sb("pj_eps", [P, 1])
        ss = sb("pj_ss", [P, G_TILES])
        rt = sb("pj_rt", [P, G_TILES])
        rs = sb("pj_rs", [P, G_TILES])
        tmp = sb("pj_tmp", [P, 3])
        ident = sb("pj_ident", [P, P])
        rot = sb("pj_rot", [P, P])
        x_hi = sb("pj_x_hi", [P, DT, GROUP], F32R)
        x_lo = sb("pj_x_lo", [P, DT, GROUP], F32R)
        w = sb("pj_w", [P, W_SLOTS, D])
        w_hi = sb("pj_w_hi", [P, W_SLOTS, DT, P], F32R)
        w_lo = sb("pj_w_lo", [P, W_SLOTS, DT, P], F32R)
        cos = sb("pj_cos", [P, GROUP])
        sin = sb("pj_sin", [P, GROUP])
        raw = sb("pj_raw", [P, 2, GROUP])
        turned = sb("pj_turned", [P, GROUP])
        bank = [ps(f"pj_ps{i}", [P, 512]) for i in range(8)]

        const_in = sem("pj_const_in")
        eps_set = sem("pj_eps_set")
        x_in = [sem(f"pj_x_in{i}") for i in range(X_SLOTS)]
        w_in = [sem(f"pj_w_in{i}") for i in range(W_SLOTS)]
        table_in = sem("pj_table_in")
        squared = sem("pj_squared")
        root = sem("pj_root")
        refined = sem("pj_refined")
        normed = sem("pj_normed")
        transposed = sem("pj_transposed")
        hi_x = sem("pj_hi_x")
        lo_x = sem("pj_lo_x")
        hi_w = sem("pj_hi_w")
        lo_w = sem("pj_lo_w")
        chunk_done = sem("pj_chunk_done")
        taken = sem("pj_taken")
        swapped = sem("pj_swapped")
        rot_a = sem("pj_rot_a")
        rot_b = sem("pj_rot_b")
        rotated = sem("pj_rotated")
        block = ctx.enter_context(nc.Block())

        @block.sync
        def _(sp):
            for dst, src in ((gain, d["g_attn"]), (ident, d["ident"]), (rot, d["rot"])):
                sp.dma_start(dst[:], src).then_inc(const_in, 16)
            with sp.Fori(0, GROUPS) as g:
                for t in range(X_SLOTS):
                    sp.wait_ge(normed, g * G_TILES + t + 1)
                    sp.dma_start(x[:, t % X_SLOTS, :], d["x"][g, t]).then_inc(x_in[t % X_SLOTS], 16)
                for n in range(W_SLOTS):
                    sp.wait_ge(lo_w, g * CHUNKS + n + 1)
                    sp.dma_start(w[:, n % W_SLOTS, :], d["w_in"][n]).then_inc(w_in[n % W_SLOTS], 16)
                for t in range(X_SLOTS, G_TILES):
                    sp.wait_ge(normed, g * G_TILES + t + 1)
                    sp.dma_start(x[:, t % X_SLOTS, :], d["x"][g, t]).then_inc(x_in[t % X_SLOTS], 16)
                sp.wait_ge(rotated, g * ROTATED + 1)
                sp.dma_start(cos[:], d["cos"][g]).then_inc(table_in, 16)
                sp.dma_start(sin[:], d["sin"][g]).then_inc(table_in, 16)
                for n in range(W_SLOTS, CHUNKS):
                    sp.wait_ge(lo_w, g * CHUNKS + n + 1)
                    sp.dma_start(w[:, n % W_SLOTS, :], d["w_in"][n]).then_inc(w_in[n % W_SLOTS], 16)

        @block.gpsimd
        def _(pool):
            pool.memset(eps[:], EPS).then_inc(eps_set, 1)

        @block.scalar
        def _(act):
            act.wait_ge(eps_set, 1)
            act.sem_inc(taken, 2)
            act.sem_inc(squared, START)
            with act.Fori(0, GROUPS) as g:
                def split(n):
                    act.wait_ge(w_in[n % W_SLOTS], g * (16 * CHUNKS // W_SLOTS) + 16 * (n // W_SLOTS + 1))
                    act.activation(w_hi[:, n % W_SLOTS, :, :].rearrange("p j c -> p (j c)"),
                                   w[:, n % W_SLOTS, :], ACT.Copy).then_inc(hi_w, 1)

                for t in range(G_TILES):
                    act.wait_ge(x_in[t % X_SLOTS], g * (16 * G_TILES // X_SLOTS) + 16 * (t // X_SLOTS + 1))
                    act.wait_ge(squared, g * G_TILES + t + START)
                    act.activation(junk[:], x[:, t % X_SLOTS, :], ACT.Square,
                                   accum_out=ss[:, t:t + 1]).then_inc(squared, 1)
                    act.wait_ge(squared, g * G_TILES + t + 1 + START)
                    act.activation(rt[:, t:t + 1], ss[:, t:t + 1], ACT.Sqrt, bias=eps[:, 0:1],
                                   scale=1.0 / D).then_inc(root, 1)
                    if t == 1:
                        split(0)
                    if t == 2:
                        split(1)
                for t in range(G_TILES):
                    for h in range(2):
                        act.wait_ge(transposed, g * (2 * G_TILES) + 2 * t + h + 1 + START)
                        act.activation(x_hi[:, 4 * h:4 * h + 4, t * P:(t + 1) * P],
                                       bank[2 * (t % 2) + h][:].rearrange("p (j c) -> p j c", j=4),
                                       ACT.Copy).then_inc(hi_x, 1)
                for n in range(CHUNKS + 1):
                    if n > 0:
                        act.wait_ge(chunk_done, g * CHUNKS + n)
                    if n + AHEAD < CHUNKS and n + AHEAD >= 2:
                        split(n + AHEAD)
                    if n == 0:
                        continue
                    q = n - 1
                    src = bank[4 + q % 2][:]
                    if q < ROTATED:
                        if q >= 2:
                            act.wait_ge(rotated, g * ROTATED + q)
                        act.activation(raw[:, q % 2, :], src, ACT.Copy,
                                       scale=SCALE if q < QA else 1.0).then_inc(taken, 1)
                    elif q < ROTATED + QB:
                        act.activation(keep.q[:, QA + q - ROTATED, bass.ds(g * GROUP, GROUP)], src,
                                       ACT.Copy, scale=SCALE).then_inc(taken, 1)
                    elif q < FIRST_V:
                        act.activation(keep.k[:, KA + q - ROTATED - QB, bass.ds(g * GROUP, GROUP)], src,
                                       ACT.Copy).then_inc(taken, 1)
                    else:
                        v0 = (q - FIRST_V) * P
                        act.activation(keep.v[:, bass.ds(g * G_TILES, G_TILES), v0:v0 + P],
                                       src.rearrange("p (t c) -> p t c", t=G_TILES),
                                       ACT.Copy).then_inc(taken, 1)

        @block.vector
        def _(dve):
            dve.wait_ge(const_in, 48)
            dve.sem_inc(normed, X_SLOTS)
            dve.sem_inc(lo_w, W_SLOTS)
            dve.sem_inc(rotated, 1)
            dve.sem_inc(transposed, START)
            with dve.Fori(0, GROUPS) as g:
                def split(n):
                    dve.wait_ge(hi_w, g * CHUNKS + n + 1)
                    dve.tensor_tensor(w_lo[:, n % W_SLOTS, :, :].rearrange("p j c -> p (j c)"),
                                      w[:, n % W_SLOTS, :],
                                      w_hi[:, n % W_SLOTS, :, :].rearrange("p j c -> p (j c)").bitcast(F32),
                                      ALU.subtract).then_inc(lo_w, 1)

                def norm(t):
                    dve.wait_ge(root, g * G_TILES + t + 1)
                    inverse_root(dve, refined, (g * G_TILES + t) * REFINE, ss[:, t:t + 1], rt[:, t:t + 1],
                                 [tmp[:, i:i + 1] for i in range(3)], rs[:, t:t + 1], 1.0 / D)
                    dve.wait_ge(transposed, g * (2 * G_TILES) + 2 * t + START)
                    dve.scalar_tensor_tensor(out=xn[:], in0=x[:, t % X_SLOTS, :], scalar=rs[:, t:t + 1],
                                             in1=gain[:], op0=ALU.mult, op1=ALU.mult).then_inc(normed, 1)

                def low(t):
                    for h in range(2):
                        dve.wait_ge(hi_x, g * (2 * G_TILES) + 2 * t + h + 1)
                        dst = x_lo[:, 4 * h:4 * h + 4, t * P:(t + 1) * P]
                        dve.tensor_tensor(dst, bank[2 * (t % 2) + h][:].rearrange("p (j c) -> p j c", j=4),
                                          x_hi[:, 4 * h:4 * h + 4, t * P:(t + 1) * P].bitcast(F32),
                                          ALU.subtract).then_inc(lo_x, 1)

                norm(0)
                norm(1)
                split(0)
                norm(2)
                low(0)
                split(1)
                norm(3)
                for t in range(1, G_TILES):
                    low(t)
                for n in range(CHUNKS + 1):
                    if n + AHEAD < CHUNKS:
                        split(n + AHEAD)
                    q = n - 2
                    if 0 <= q < ROTATED:
                        if q == 0:
                            dve.wait_ge(table_in, g * 32 + 32)
                        dve.wait_ge(swapped, g * ROTATED + q + 1)
                        dve.tensor_tensor(turned[:], bank[6 + q % 2][:], sin[:], ALU.mult).then_inc(rot_a, 1)
                        dve.tensor_tensor(raw[:, q % 2, :], raw[:, q % 2, :], cos[:],
                                          ALU.mult).then_inc(rot_b, 1)
                        dve.wait_ge(rot_a, g * ROTATED + q + 1)
                        dve.wait_ge(rot_b, g * ROTATED + q + 1)
                        dst = (keep.q[:, q, bass.ds(g * GROUP, GROUP)] if q < QA
                               else keep.k[:, 0, bass.ds(g * GROUP, GROUP)])
                        dve.tensor_tensor(dst, raw[:, q % 2, :], turned[:], ALU.add).then_inc(rotated, 1)
                        dve.wait_ge(rotated, g * ROTATED + q + 2)

        @block.tensor
        def _(pe):
            pe.wait_ge(const_in, 48)
            with pe.Fori(0, GROUPS) as g:
                for t in range(G_TILES):
                    pe.wait_ge(normed, g * G_TILES + t + 1 + X_SLOTS)
                    for h in range(2):
                        if t >= 2:
                            pe.wait_ge(lo_x, g * (2 * G_TILES) + 2 * (t - 2) + h + 1)
                        for j in range(4):
                            c0 = (4 * h + j) * P
                            last = nc.tensor.transpose(bank[2 * (t % 2) + h][:, j * P:(j + 1) * P],
                                                       xn[:, c0:c0 + P], ident[:])
                        last.then_inc(transposed, 1)
                for n in range(CHUNKS):
                    pe.wait_ge(lo_w, g * CHUNKS + n + 1 + W_SLOTS)
                    pe.wait_ge(taken, g * CHUNKS + n + 1)
                    if n == 0:
                        pe.wait_ge(lo_x, (g + 1) * (2 * G_TILES))
                    s = n % W_SLOTS
                    if n < FIRST_V:
                        for j in range(DT):
                            last = three_pass(nc, bank[4 + n % 2][:], (w_hi[:, s, j, :], w_lo[:, s, j, :]),
                                              (x_hi[:, j, :], x_lo[:, j, :]), j == 0, j == DT - 1)
                    else:
                        for t in range(G_TILES):
                            c = slice(t * P, (t + 1) * P)
                            for j in range(DT):
                                last = three_pass(nc, bank[4 + n % 2][:, c], (x_hi[:, j, c], x_lo[:, j, c]),
                                                  (w_hi[:, s, j, :], w_lo[:, s, j, :]), j == 0, j == DT - 1)
                    last.then_inc(chunk_done, 1)
                    q = n - 1
                    if 0 <= q < ROTATED:
                        pe.wait_ge(taken, g * CHUNKS + q + 3)
                        if q >= 2:
                            pe.wait_ge(rotated, g * ROTATED + q)
                        nc.tensor.matmul(bank[6 + q % 2][:], rot[:], raw[:, q % 2, :], start=True,
                                         stop=True).then_inc(swapped, 1)


WINDOW_KEYS = 3 * P
NEAR_ROWS = KEY_ROWS + 1
NEAR_KEYS = NEAR_ROWS * GRID_W
DELTAS = 14
PAIRS = 4


def attention_units():
    window, near = [], []
    for first, tiles in ((0, S_TILES), (S_TILES, TILES - S_TILES)):
        for b in range(tiles):
            lo, hi = max(b - 1, 0), min(b + 1, tiles - 1)
            window.append((True, first + b, first + lo, (hi - lo + 1) * P, (lo - b + 1) * P))
            rows = 2 * tiles
            if 2 * b >= KEY_ROWS // 2 and 2 * b + 1 <= rows - KEY_ROWS // 2 and rows > KEY_ROWS:
                near.append((False, first + b, first + b - 2, NEAR_KEYS, None))
            else:
                lo = 0 if 2 * b < KEY_ROWS // 2 or rows == KEY_ROWS else (rows - KEY_ROWS) // 2
                near.append((False, first + b, first + lo, KEY_ROWS * GRID_W, 2 * (lo - b) + 6))
    return window + near


def attend(nc, d, keep):
    ctx = ExitStack()
    with ctx:
        sb, ps, sem = buffers(nc, ctx)
        blocks = attention_units()
        units = [(*blk, pair, bi) for bi, blk in enumerate(blocks) for pair in range(PAIRS)]
        N = len(units)
        N_WINDOW = N // 2
        PROBS, STATS, FLIPS, BANKS, OUTS = 6, 4, 6, 2, 2

        groups, first_group = [], []
        for u, (window, _, _, keys, *_) in enumerate(units):
            first_group.append(len(groups))
            full = keys // P
            for h in range(2):
                groups.append((u, [(h, i, P, i * P) for i in range(full)]))
            if keys % P:
                groups.append((u, [(h, full, keys % P, h * P) for h in range(2)]))
        first_group.append(len(groups))

        bias = sb("at_bias", [P, 2 * PAIRS, DELTAS, GRID_W])
        inner = sb("at_inner", [P, 2 * PAIRS, NEAR_KEYS])
        col_mask = sb("at_col_mask", [P, GRID_W])
        row_mask = sb("at_row_mask", [P, NEAR_KEYS])
        band = sb("at_band", [P, WINDOW_KEYS])
        sink = sb("at_sink", [P, 2 * PAIRS])
        neg_sink = sb("at_neg_sink", [P, 2 * PAIRS])
        ident = sb("at_ident", [P, P])
        probs = sb("at_probs", [P, PROBS, NEAR_KEYS])
        flipped = sb("at_flipped", [P, FLIPS, 512])
        o = sb("at_o", [P, 2, 512])
        top, neg_top, at_sink, e_sink, sums, den, rden = (
            sb(f"at_{n}", [P, STATS, 2]) for n in ("top", "neg_top", "at_sink", "e_sink", "sums", "den", "rden"))
        score = [ps(f"at_score{h}", [P, 1024]) for h in range(2)]
        flip_ps = [ps(f"at_flip{i}", [P, 512]) for i in range(BANKS)]
        out_ps = [ps(f"at_out{i}", [P, 512]) for i in range(OUTS)]

        const_in = sem("at_const_in")
        bias_in = sem("at_bias_in")
        negated = sem("at_negated")
        masked = sem("at_masked")
        scored = sem("at_scored")
        added = sem("at_added")
        bounded = sem("at_bounded")
        sink_at = sem("at_sink_at")
        exped = sem("at_exped")
        sink_exped = sem("at_sink_exped")
        summed = sem("at_summed")
        inverted = sem("at_inverted")
        flipped_ps = sem("at_flipped_ps")
        copied = [sem("at_copied_act"), sem("at_copied_dve")]
        weighed = sem("at_weighed")
        scaled = sem("at_scaled")
        stored = [sem(f"at_stored{i}") for i in range(2)]
        block = ctx.enter_context(nc.Block())

        def copies(engine, upto):
            return (upto + 1 - engine) // 2

        def copy_groups(eng, engine, v):
            for g in range(first_group[v], first_group[v + 1]):
                if g % 2 != engine:
                    continue
                eng.wait_ge(flipped_ps, g + 1)
                if g >= FLIPS:
                    eng.wait_ge(weighed, groups[g - FLIPS][0] + 1)
                items = groups[g][1]
                rows, width = items[0][2], len(items) * P
                dst, src = flipped[0:rows, g % FLIPS, 0:width], flip_ps[g % BANKS][0:rows, 0:width]
                if engine == 0:
                    nc.scalar.activation(dst, src, ACT.Copy).then_inc(copied[0], 1)
                else:
                    nc.vector.tensor_copy(dst, src).then_inc(copied[1], 1)

        @block.sync
        def _(sp):
            sp.dma_start(ident[:], d["ident"]).then_inc(const_in, 16)
            sp.dma_start(band[:], d["band"]).then_inc(const_in, 16)
            sp.dma_start(sink[:], d["sink"]).then_inc(const_in, 16)
            sp.dma_start(col_mask[:], d["col_mask"]).then_inc(bias_in, 16)
            sp.dma_start(row_mask[:], d["row_mask"]).then_inc(bias_in, 16)
            for r in range(2):
                sp.dma_start(bias[r * GRID_W:(r + 1) * GRID_W, :, :, :],
                             d["rpb"][:, :, 1 - r:1 - r + DELTAS, :]).then_inc(bias_in, 16)
            for bi, (window, tile, *_) in enumerate(blocks):
                sp.wait_ge(scaled, PAIRS * (bi + 1))
                c0 = 0 if window else 512
                sp.dma_start(d["o"][tile][:, c0:c0 + 512], o[:, bi % 2, :]).then_inc(stored[bi % 2], 16)
            for i in range(2):
                sp.wait_ge(stored[i], 16 * len(blocks) // 2)

        @block.gpsimd
        def _(pool):
            pool.wait_ge(bias_in, 64)
            flat = bias[:].rearrange("p h r c -> p (h r) c")
            pool.tensor_tensor(flat, flat, col_mask[:].unsqueeze(1).broadcast_to([P, 2 * PAIRS * DELTAS, GRID_W]),
                               ALU.add).then_inc(masked, 1)
            pool.wait_ge(masked, 1)
            rows = bias[:, :, 2:2 + NEAR_ROWS, :].rearrange("p h r c -> p h (r c)")
            pool.tensor_tensor(inner[:], rows, row_mask[:].unsqueeze(1).broadcast_to([P, 2 * PAIRS, NEAR_KEYS]),
                               ALU.add).then_inc(masked, 1)

        @block.scalar
        def _(act):
            for u in range(N + 1):
                if u < N:
                    window, r = units[u][0], u % STATS
                    act.wait_ge(bounded, u + 1)
                    for h in range(2):
                        p = probs[:, (2 * u + h) % PROBS, 0:units[u][3]]
                        act.activation(p, p, ACT.Exp, bias=neg_top[:, r, h:h + 1],
                                       accum_out=sums[:, r, h:h + 1]).then_inc(exped, 1)
                    if window:
                        act.wait_ge(sink_at, u + 1)
                        act.activation(e_sink[:, r, :], at_sink[:, r, :], ACT.Exp).then_inc(sink_exped, 1)
                if u >= 1:
                    copy_groups(act, 0, u - 1)

        @block.vector
        def _(dve):
            dve.wait_ge(const_in, 48)
            dve.tensor_scalar(neg_sink[:], sink[:], -1.0, None, ALU.mult).then_inc(negated, 1)
            dve.wait_ge(negated, 1)
            for u in range(N + 2):
                if u < N:
                    window, tile, key0, keys, off, pair, bi = units[u]
                    r = u % STATS
                    if u == N_WINDOW:
                        dve.wait_ge(masked, 2)
                    for h in range(2):
                        dve.wait_ge(scored, 2 * u + h + 1)
                        if 2 * u + h >= PROBS:
                            dve.wait_ge(flipped_ps, first_group[u - PROBS // 2 + 1])
                        if window:
                            add = band[:, off:off + keys]
                        elif off is None:
                            add = inner[:, 2 * pair + h, :]
                        else:
                            add = bias[:, 2 * pair + h, off:off + KEY_ROWS, :].rearrange("p r c -> p (r c)")
                        dve.tensor_tensor_reduce(out=probs[:, (2 * u + h) % PROBS, 0:keys],
                                                 in0=score[h][:, 0:keys], in1=add, scale=1.0, scalar=-3.0e38,
                                                 op0=ALU.add, op1=ALU.max,
                                                 accum_out=top[:, r, h:h + 1]).then_inc(added, 1)
                    dve.wait_ge(added, 2 * u + 2)
                    if window:
                        mine = neg_sink[:, 2 * pair:2 * pair + 2]
                        dve.scalar_tensor_tensor(out=neg_top[:, r, :], in0=top[:, r, :], scalar=-1.0, in1=mine,
                                                 op0=ALU.mult, op1=ALU.min).then_inc(bounded, 1)
                        dve.wait_ge(bounded, u + 1)
                        dve.tensor_tensor(at_sink[:, r, :], neg_top[:, r, :], mine,
                                          ALU.subtract).then_inc(sink_at, 1)
                    else:
                        dve.tensor_scalar(neg_top[:, r, :], top[:, r, :], -1.0, None,
                                          ALU.mult).then_inc(bounded, 1)
                if 1 <= u < N + 1:
                    v, r = u - 1, (u - 1) % STATS
                    dve.wait_ge(exped, 2 * v + 2)
                    total = sums
                    if units[v][0]:
                        dve.wait_ge(sink_exped, v + 1)
                        dve.tensor_tensor(den[:, r, :], sums[:, r, :], e_sink[:, r, :],
                                          ALU.add).then_inc(summed, 1)
                        dve.wait_ge(summed, v + 1)
                        total = den
                    dve.reciprocal(rden[:, r, :], total[:, r, :]).then_inc(inverted, 1)
                    copy_groups(dve, 1, v)
                if u >= 2:
                    v, r = u - 2, (u - 2) % STATS
                    window, _, _, _, _, pair, bi = units[v]
                    dve.wait_ge(weighed, v + 1)
                    dve.wait_ge(inverted, v + 1)
                    if pair == 0 and bi >= 2:
                        dve.wait_ge(stored[bi % 2], 16 * (bi // 2))
                    if window:
                        dst = o[:, bi % 2, :].rearrange("p (h c e) -> p h c e", h=2, c=PAIRS)[:, :, pair, :]
                    else:
                        dst = o[:, bi % 2, pair * P:(pair + 1) * P].rearrange("p (h e) -> p h e", h=2)
                    dve.tensor_tensor(dst, out_ps[v % OUTS][:, 0:P].rearrange("p (h e) -> p h e", h=2),
                                      rden[:, r, :].unsqueeze(2).broadcast_to([P, 2, HD]),
                                      ALU.mult).then_inc(scaled, 1)

        @block.tensor
        def _(pe):
            pe.wait_ge(const_in, 48)

            def transpose(g):
                v, items = groups[g]
                pe.wait_ge(exped, 2 * v + items[-1][0] + 1)
                if g >= BANKS:
                    e = (g - BANKS) % 2
                    pe.wait_ge(copied[e], copies(e, g - BANKS + 1))
                for h, i, rows, col in items:
                    last = nc.tensor.transpose(flip_ps[g % BANKS][0:rows, col:col + P],
                                               probs[:, (2 * v + h) % PROBS, i * P:i * P + rows], ident[:])
                last.then_inc(flipped_ps, 1)

            for u in range(N + 2):
                if u < N:
                    window, tile, key0, keys, off, pair, bi = units[u]
                    q0, k0 = tile * P, key0 * P
                    for h in range(2):
                        if u >= 1:
                            pe.wait_ge(added, 2 * (u - 1) + h + 1)
                        rows = slice(h * HD, (h + 1) * HD)
                        qc, kc = (pair, 0) if window else (QA + pair, KA + pair)
                        for c in range(0, keys, 512):
                            w = min(512, keys - c)
                            last = nc.tensor.matmul(score[h][:, c:c + w], keep.q[rows, qc, q0:q0 + P],
                                                    keep.k[rows, kc, k0 + c:k0 + c + w], start=True, stop=True)
                        last.then_inc(scored, 1)
                mine = range(first_group[u - 1], first_group[u]) if 1 <= u < N + 1 else []
                for g in mine[:BANKS]:
                    transpose(g)
                if u >= 2:
                    v = u - 2
                    window, tile, key0, keys, off, pair, bi = units[v]
                    for e in range(2):
                        pe.wait_ge(copied[e], copies(e, first_group[v + 1]))
                    if v >= OUTS:
                        pe.wait_ge(scaled, v - OUTS + 1)
                    for h in range(2):
                        products = [(i, rows, g % FLIPS, col) for g in range(first_group[v], first_group[v + 1])
                                    for hh, i, rows, col in groups[g][1] if hh == h]
                        c0 = h * HD if window else P + pair * P + h * HD
                        for n, (i, rows, slot, col) in enumerate(products):
                            last = nc.tensor.matmul(out_ps[v % OUTS][:, h * HD:(h + 1) * HD], flipped[0:rows, slot, col:col + P],
                                                    keep.v[0:rows, key0 + i, c0:c0 + HD], start=n == 0,
                                                    stop=n == len(products) - 1)
                    last.then_inc(weighed, 1)
                for g in mine[BANKS:]:
                    transpose(g)


def mix(nc, d, route):
    ctx = ExitStack()
    with ctx:
        sb, ps, sem = buffers(nc, ctx)
        HALF = D // 2
        w = sb("mx_w", [P, DT, D])
        w_hi = sb("mx_w_hi", [P, DT, D], F32R)
        w_lo = sb("mx_w_lo", [P, DT, D], F32R)
        w_router = sb("mx_w_router", [P, DT, EXPERTS])
        gain_out = sb("mx_gain_out", [P, D])
        gain_ffn = sb("mx_gain_ffn", [P, D])
        ident = sb("mx_ident", [P, P])
        eps = sb("mx_eps", [P, 1])
        o = sb("mx_o", [P, 2, D])
        x = sb("mx_x", [P, 2, D])
        x2 = sb("mx_x2", [P, 2, D])
        h = sb("mx_h", [P, 2, D])
        merged = sb("mx_merged", [P, D])
        m_hi = sb("mx_m_hi", [P, 2, DT, P], F32R)
        m_lo = sb("mx_m_lo", [P, 2, DT, P], F32R)
        ht = sb("mx_ht", [P, DT, P])
        junk = sb("mx_junk", [P, D], BF16)
        ss1, rt1, rs1 = (sb(f"mx_{n}1", [P, 2]) for n in ("ss", "rt", "rs"))
        ss2, rt2, rs2 = (sb(f"mx_{n}2", [P, 1]) for n in ("ss", "rt", "rs"))
        tmp1, tmp2 = sb("mx_tmp1", [P, 3, 2]), sb("mx_tmp2", [P, 3, 1])
        neg_top, e_sum, e_inv = (sb(f"mx_{n}", [P, 1]) for n in ("neg_top", "e_sum", "e_inv"))
        e_aff, aff = sb("mx_e_aff", [P, EXPERTS]), sb("mx_aff", [P, 2, EXPERTS])
        bank = [ps(f"mx_ps{i}", [P, 512]) for i in range(8)]

        const_in = sem("mx_const_in")
        w_in = [sem(f"mx_w_in{i}") for i in range(DT)]
        ready = sem("mx_ready")
        o_in = [sem(f"mx_o_in{i}") for i in range(2)]
        x_in = [sem(f"mx_x_in{i}") for i in range(2)]
        hi_w, lo_w = sem("mx_hi_w"), sem("mx_lo_w")
        squared = sem("mx_squared")
        root1, root2 = sem("mx_root1"), sem("mx_root2")
        refined = sem("mx_refined")
        normed1, normed2 = sem("mx_normed1"), sem("mx_normed2")
        turned1, turned2 = sem("mx_turned1"), sem("mx_turned2")
        hi_m, lo_m = sem("mx_hi_m"), sem("mx_lo_m")
        projected = sem("mx_projected")
        summed = sem("mx_summed")
        ht_copied = sem("mx_ht_copied")
        routed = sem("mx_routed")
        topped, exped, inverted, shared = (sem(f"mx_{n}") for n in ("topped", "exped", "inverted", "shared"))
        aff_turned, rowed = sem("mx_aff_turned"), sem("mx_rowed")
        x2_out = [sem(f"mx_x2_out{i}") for i in range(2)]
        h_out = [sem(f"mx_h_out{i}") for i in range(2)]
        block = ctx.enter_context(nc.Block())

        @block.sync
        def _(sp):
            def load(t):
                if t >= 2:
                    sp.wait_ge(normed1, 2 * (t - 1))
                sp.dma_start(o[:, t % 2, :], d["o"][t]).then_inc(o_in[t % 2], 16)
                if t >= 2:
                    sp.wait_ge(summed, 2 * (t - 1))
                sp.dma_start(x[:, t % 2, :], d["x_tiles"][t]).then_inc(x_in[t % 2], 16)

            sp.dma_start(gain_out[:], d["g_out"]).then_inc(const_in, 16)
            sp.dma_start(ident[:], d["ident"]).then_inc(const_in, 16)
            load(0)
            for j in range(DT):
                sp.dma_start(w[:, j, :], d["w_out"][j]).then_inc(w_in[j], 16)
            sp.dma_start(gain_ffn[:], d["g_ffn"]).then_inc(const_in, 16)
            sp.dma_start(w_router[:], d["w_router"]).then_inc(const_in, 16)
            load(1)
            for t in range(TILES):
                if t + 2 < TILES:
                    load(t + 2)
                sp.wait_ge(summed, 2 * (t + 1))
                sp.dma_start(d["acc_tiles"][t], x2[:, t % 2, :]).then_inc(x2_out[t % 2], 16)
                sp.wait_ge(normed2, t + 1)
                sp.dma_start(d["h_tiles"][t], h[:, t % 2, :]).then_inc(h_out[t % 2], 16)
            for i in range(2):
                sp.wait_ge(x2_out[i], 16 * TILES // 2)
                sp.wait_ge(h_out[i], 16 * TILES // 2)

        @block.gpsimd
        def _(pool):
            pool.memset(eps[:], EPS).then_inc(ready, 1)
            pool.memset(route.rows[:, 0, :], -1.0).then_inc(ready, 1)

        @block.scalar
        def _(act):
            squares = 0

            def square(src, dst):
                nonlocal squares
                act.wait_ge(squared, squares)
                act.activation(junk[:, 0:src.shape[-1]], src, ACT.Square, accum_out=dst).then_inc(squared, 1)
                squares += 1

            act.wait_ge(ready, 2)
            for s in range(-1, TILES + 2):
                t = s - 1
                if 0 <= t < TILES:
                    act.wait_ge(summed, 2 * (t + 1))
                    square(x2[:, t % 2, :], ss2[:])
                    act.wait_ge(squared, squares)
                    act.activation(rt2[:], ss2[:], ACT.Sqrt, bias=eps[:], scale=1.0 / D).then_inc(root2, 1)
                t = s + 1
                if t < TILES:
                    act.wait_ge(o_in[t % 2], 16 * (t // 2 + 1))
                    for k in range(2):
                        square(o[:, t % 2, k * HALF:(k + 1) * HALF], ss1[:, k:k + 1])
                    act.wait_ge(squared, squares)
                    act.activation(rt1[:], ss1[:], ACT.Sqrt, bias=eps[:], scale=1.0 / HALF).then_inc(root1, 1)
                    if t == 0:
                        for j in range(DT):
                            act.wait_ge(w_in[j], 16)
                            act.activation(w_hi[:, j, :], w[:, j, :], ACT.Copy).then_inc(hi_w, 1)
                    for k in range(2):
                        act.wait_ge(turned1, 2 * t + k + 1)
                        if t >= 2:
                            act.wait_ge(projected, t - 1)
                        act.activation(m_hi[:, t % 2, 4 * k:4 * k + 4, :].rearrange("p j c -> p (j c)"),
                                       bank[k][:], ACT.Copy).then_inc(hi_m, 1)
                t = s - 1
                if 0 <= t < TILES:
                    for k in range(2):
                        act.wait_ge(turned2, 2 * t + k + 1)
                        if t >= 1:
                            act.wait_ge(routed, t)
                        act.activation(ht[:, 4 * k:4 * k + 4, :].rearrange("p j c -> p (j c)"),
                                       bank[4 + k][:], ACT.Copy).then_inc(ht_copied, 1)
                    act.wait_ge(topped, t + 1)
                    act.activation(e_aff[:], bank[6][:, 0:EXPERTS], ACT.Exp, bias=neg_top[:],
                                   accum_out=e_sum[:]).then_inc(exped, 1)
                t = s - 2
                if 0 <= t < TILES:
                    act.wait_ge(aff_turned, t + 1)
                    row, col = (0, t * P) if t < S_TILES else (PROMPT_AT, (t - S_TILES) * P)
                    act.activation(route.rows[row:row + EXPERTS, 0, col:col + P], bank[7][0:EXPERTS, 0:P],
                                   ACT.Copy).then_inc(rowed, 1)

        @block.vector
        def _(dve):
            refines = 0
            dve.wait_ge(const_in, 64)
            for s in range(-1, TILES + 1):
                t = s - 1
                if 0 <= t < TILES:
                    dve.wait_ge(x_in[t % 2], 16 * (t // 2 + 1))
                    if t >= 2:
                        dve.wait_ge(x2_out[t % 2], 16 * (t // 2))
                    dve.wait_ge(projected, t + 1)
                    for k in range(2):
                        c = slice(k * HALF, (k + 1) * HALF)
                        dve.tensor_tensor(x2[:, t % 2, c], bank[2 + k][:], x[:, t % 2, c],
                                          ALU.add).then_inc(summed, 1)
                    dve.wait_ge(root2, t + 1)
                    inverse_root(dve, refined, refines, ss2[:], rt2[:], [tmp2[:, i, :] for i in range(3)],
                                 rs2[:], 1.0 / D)
                    refines += REFINE
                    if t >= 2:
                        dve.wait_ge(h_out[t % 2], 16 * (t // 2))
                        dve.wait_ge(turned2, 2 * (t - 1))
                    dve.scalar_tensor_tensor(out=h[:, t % 2, :], in0=x2[:, t % 2, :], scalar=rs2[:],
                                             in1=gain_ffn[:], op0=ALU.mult, op1=ALU.mult).then_inc(normed2, 1)
                t = s + 1
                if t < TILES:
                    dve.wait_ge(root1, t + 1)
                    inverse_root(dve, refined, refines, ss1[:], rt1[:], [tmp1[:, i, :] for i in range(3)],
                                 rs1[:], 1.0 / HALF)
                    refines += REFINE
                    for k in range(2):
                        c = slice(k * HALF, (k + 1) * HALF)
                        dve.wait_ge(turned1, 2 * t)
                        dve.scalar_tensor_tensor(out=merged[:, c], in0=o[:, t % 2, c], scalar=rs1[:, k:k + 1],
                                                 in1=gain_out[:, c], op0=ALU.mult,
                                                 op1=ALU.mult).then_inc(normed1, 1)
                    if t == 0:
                        for j in range(DT):
                            dve.wait_ge(hi_w, j + 1)
                            dve.tensor_tensor(w_lo[:, j, :], w[:, j, :], w_hi[:, j, :].bitcast(F32),
                                              ALU.subtract).then_inc(lo_w, 1)
                    for k in range(2):
                        dve.wait_ge(hi_m, 2 * t + k + 1)
                        jj = slice(4 * k, 4 * k + 4)
                        dve.tensor_tensor(m_lo[:, t % 2, jj, :].rearrange("p j c -> p (j c)"), bank[k][:],
                                          m_hi[:, t % 2, jj, :].rearrange("p j c -> p (j c)").bitcast(F32),
                                          ALU.subtract).then_inc(lo_m, 1)
                t = s - 1
                if 0 <= t < TILES:
                    dve.wait_ge(routed, t + 1)
                    dve.tensor_reduce(neg_top[:], bank[6][:, 0:EXPERTS], AX.X, ALU.max,
                                      negate=True).then_inc(topped, 1)
                    dve.wait_ge(exped, t + 1)
                    dve.reciprocal(e_inv[:], e_sum[:]).then_inc(inverted, 1)
                    dve.wait_ge(inverted, t + 1)
                    if t >= 2:
                        dve.wait_ge(aff_turned, t - 1)
                    dve.tensor_scalar(aff[:, t % 2, :], e_aff[:], e_inv[:], None, ALU.mult).then_inc(shared, 1)

        @block.tensor
        def _(pe):
            pe.wait_ge(const_in, 64)
            for s in range(-1, TILES + 2):
                t = s
                if 0 <= t < TILES:
                    pe.wait_ge(lo_m, 2 * (t + 1))
                    if t >= 1:
                        pe.wait_ge(summed, 2 * t)
                    for k in range(2):
                        c = slice(k * HALF, (k + 1) * HALF)
                        for j in range(DT):
                            pe.wait_ge(lo_w, j + 1)
                            last = three_pass(nc, bank[2 + k][:], (m_hi[:, t % 2, j, :], m_lo[:, t % 2, j, :]),
                                              (w_hi[:, j, c], w_lo[:, j, c]), j == 0, j == DT - 1)
                    last.then_inc(projected, 1)
                t = s + 1
                if t < TILES:
                    for k in range(2):
                        pe.wait_ge(normed1, 2 * t + k + 1)
                        if t >= 1:
                            pe.wait_ge(lo_m, 2 * (t - 1) + k + 1)
                        for j in range(4):
                            c0 = (4 * k + j) * P
                            last = nc.tensor.transpose(bank[k][:, j * P:(j + 1) * P], merged[:, c0:c0 + P],
                                                       ident[:])
                        last.then_inc(turned1, 1)
                t = s - 1
                if 0 <= t < TILES:
                    pe.wait_ge(normed2, t + 1)
                    for k in range(2):
                        if t >= 1:
                            pe.wait_ge(ht_copied, 2 * (t - 1) + k + 1)
                        for j in range(4):
                            c0 = (4 * k + j) * P
                            last = nc.tensor.transpose(bank[4 + k][:, j * P:(j + 1) * P], h[:, t % 2, c0:c0 + P],
                                                       ident[:])
                        last.then_inc(turned2, 1)
                    pe.wait_ge(ht_copied, 2 * (t + 1))
                    if t >= 1:
                        pe.wait_ge(exped, t)
                    for j in range(DT):
                        last = nc.tensor.matmul(bank[6][:, 0:EXPERTS], ht[:, j, :], w_router[:, j, :],
                                                start=j == 0, stop=j == DT - 1)
                    last.then_inc(routed, 1)
                t = s - 2
                if 0 <= t < TILES:
                    pe.wait_ge(shared, t + 1)
                    if t >= 1:
                        pe.wait_ge(rowed, t)
                    nc.tensor.transpose(bank[7][0:EXPERTS, 0:P], aff[:, t % 2, :],
                                        ident[:]).then_inc(aff_turned, 1)


def choose(nc, d, route):
    ctx = ExitStack()
    with ctx:
        sb, ps, sem = buffers(nc, ctx)
        ROWS = PROMPT_AT + EXPERTS
        best = sb("ch_best", [ROWS, S_CAP])
        at = sb("ch_at", [ROWS, S_CAP], U32)
        at_f = sb("ch_at_f", [ROWS, S_CAP])
        ident = sb("ch_ident", [P, P])
        bank = [ps(f"ch_ps{i}", [P, 512]) for i in range(2)]
        const_in = sem("ch_const_in")
        found, placed, dropped = sem("ch_found"), sem("ch_placed"), sem("ch_dropped")
        floated, turned, done = sem("ch_floated"), sem("ch_turned"), sem("ch_done")
        block = ctx.enter_context(nc.Block())

        @block.sync
        def _(sp):
            sp.dma_start(ident[:], d["ident"]).then_inc(const_in, 16)

        @block.vector
        def _(dve):
            for r in range(S_CAP // 8):
                rows, other = route.rows[:, r % 2, :], route.rows[:, 1 - r % 2, :]
                c = slice(8 * r, 8 * r + 8)
                dve.wait_ge(dropped, r)
                dve.max(best[:, c], rows).then_inc(found, 1)
                dve.wait_ge(found, r + 1)
                dve.max_index(at[:, c], best[:, c], rows).then_inc(placed, 1)
                dve.match_replace(other, best[:, c], rows, -2.0).then_inc(dropped, 1)
            dve.wait_ge(placed, S_CAP // 8)
            dve.tensor_copy(at_f[:], at[:]).then_inc(floated, 1)
            dve.wait_ge(turned, 2)
            dve.tensor_copy(route.gates[:, 0, :], bank[0][:, 0:EXPERTS]).then_inc(done, 1)
            dve.tensor_copy(route.gates[:, 1, :], bank[0][:, PROMPT_AT:ROWS]).then_inc(done, 1)
            dve.tensor_copy(route.index[:, 0, 0:EXPERTS], bank[1][:, 0:EXPERTS]).then_inc(done, 1)
            dve.tensor_copy(route.index[:, 0, EXPERTS:], bank[1][:, 0:1]).then_inc(done, 1)
            dve.tensor_scalar(route.index[:, 1, 0:EXPERTS], bank[1][:, PROMPT_AT:ROWS], float(S_TOK), None,
                              ALU.add).then_inc(done, 1)
            dve.tensor_scalar(route.index[:, 1, EXPERTS:], bank[1][:, PROMPT_AT:PROMPT_AT + 1], float(S_TOK),
                              None, ALU.add).then_inc(done, 1)

        @block.tensor
        def _(pe):
            pe.wait_ge(const_in, 16)
            pe.wait_ge(found, S_CAP // 8)
            nc.tensor.transpose(bank[0][:, 0:ROWS], best[:], ident[0:ROWS, 0:ROWS]).then_inc(turned, 1)
            pe.wait_ge(floated, 1)
            nc.tensor.transpose(bank[1][:, 0:ROWS], at_f[:], ident[0:ROWS, 0:ROWS]).then_inc(turned, 1)


UP_CHUNKS = 2 * (FT // 2)
W_CHUNKS = UP_CHUNKS + DT
W_COLS = 2 * D


def experts(nc, d, route):
    ctx = ExitStack()
    with ctx:
        sb, ps, sem = buffers(nc, ctx)
        SLOTS, AHEAD = 4, 3
        PAIR = 2 * CAP
        w = sb("ex_w", [P, SLOTS, W_COLS])
        w_hi = sb("ex_w_hi", [P, SLOTS, W_COLS], F32R)
        w_lo = sb("ex_w_lo", [P, SLOTS, W_COLS], F32R)
        ident = sb("ex_ident", [P, P])
        x_s = sb("ex_x_s", [S_CAP, D])
        x_p = sb("ex_x_p", [P_CAP, D])
        x_hi = sb("ex_x_hi", [P, DT, CAP], F32R)
        x_lo = sb("ex_x_lo", [P, DT, CAP], F32R)
        silu = sb("ex_silu", [P, 2, PAIR])
        hid = sb("ex_hid", [P, 2, PAIR])
        h_hi = sb("ex_h_hi", [P, FT, CAP], F32R)
        h_lo = sb("ex_h_lo", [P, FT, CAP], F32R)
        y = sb("ex_y", [P, DT, CAP])
        y_s = sb("ex_y_s", [S_CAP, D])
        y_p = sb("ex_y_p", [P_CAP, D])
        gather_s = sb("ex_gather_s", [S_CAP, 1], U32)
        gather_p = sb("ex_gather_p", [P_CAP, 1], U32)
        scatter_s = sb("ex_scatter_s", [S_CAP, 1], U32)
        scatter_p = sb("ex_scatter_p", [P_CAP, 1], U32)
        gate_s = sb("ex_gate_s", [S_CAP, 1])
        gate_p = sb("ex_gate_p", [P_CAP, 1])
        bank = [ps(f"ex_ps{i}", [P, 512]) for i in range(8)]

        const_in = sem("ex_const_in")
        w_in = [sem(f"ex_w_in{i}") for i in range(SLOTS)]
        hi_w = sem("ex_hi_w")
        lo_w = sem("ex_lo_w")
        chunk_done = sem("ex_chunk_done")
        gated = sem("ex_gated")
        hidden = sem("ex_hidden")
        hi_h, lo_h = sem("ex_hi_h"), sem("ex_lo_h")
        y_copied = sem("ex_y_copied")
        x_turned, hi_x, lo_x = sem("ex_x_turned"), sem("ex_hi_x"), sem("ex_lo_x")
        y_turned = sem("ex_y_turned")
        s_scaled, p_scaled = sem("ex_s_scaled"), sem("ex_p_scaled")
        columns = sem("ex_columns")
        y_free = sem("ex_y_free")
        released = sem("ex_released")
        gathered = sem("ex_gathered")
        scattered_s, scattered_p = sem("ex_scattered_s"), sem("ex_scattered_p")
        block = ctx.enter_context(nc.Block())
        FILLS = DT // 2
        COPIES, FIRST_COPIES = 6, 2

        @block.sync
        def _(sp):
            sp.dma_start(ident[:], d["ident"]).then_inc(const_in, 16)
            with sp.Fori(0, EXPERTS) as e:
                for c in range(W_CHUNKS):
                    sp.wait_ge(lo_w, e * W_CHUNKS + c + 1)
                    sp.dma_start(w[:, c % SLOTS, :], d["w_experts"][e, c]).then_inc(w_in[c % SLOTS], 16)
            for c in range(AHEAD):
                sp.wait_ge(lo_w, EXPERTS * W_CHUNKS + c + 1)
                sp.dma_start(w[:, c % SLOTS, :], d["w_experts"][0, c]).then_inc(w_in[c % SLOTS], 16)

        @block.gpsimd
        def _(pool):
            def gather(e, copied):
                pool.tensor_copy(gather_s[:], route.index[:, 0, bass.ds(e, 1)]).then_inc(columns, 1)
                pool.tensor_copy(gather_p[:], route.index[0:P_CAP, 1, bass.ds(e, 1)]).then_inc(columns, 1)
                pool.wait_ge(columns, copied)
                pool.sem_inc(released, 1)
                for dst, at in ((x_s, gather_s), (x_p, gather_p)):
                    pool.indirect_dma_start(dst[:], None, d["h"],
                                            bass.IndirectOffsetOnAxis(at[:, 0:1], 0)).then_inc(gathered, 16)

            pool.sem_inc(y_free, START)
            gather(0, FIRST_COPIES)
            with pool.Fori(0, EXPERTS) as e:
                pool.wait_ge(x_turned, (e + 1) * FILLS)
                pool.wait_ge(gathered, (e + 1) * 32)
                gather(e + 1, FIRST_COPIES + e * COPIES + 2)
                pool.tensor_copy(scatter_s[:], route.index[:, 0, bass.ds(e, 1)]).then_inc(columns, 1)
                pool.tensor_copy(scatter_p[:], route.index[0:P_CAP, 1, bass.ds(e, 1)]).then_inc(columns, 1)
                pool.tensor_copy(gate_s[:], route.gates[:, 0, bass.ds(e, 1)]).then_inc(columns, 1)
                pool.tensor_copy(gate_p[:], route.gates[0:P_CAP, 1, bass.ds(e, 1)]).then_inc(columns, 1)
                pool.wait_ge(columns, FIRST_COPIES + (e + 1) * COPIES)
                pool.wait_ge(s_scaled, e * 2 + 2 + START)
                pool.sem_inc(released, 1)
                pool.indirect_dma_start(d["acc"], bass.IndirectOffsetOnAxis(scatter_s[:, 0:1], 0), y_s[:],
                                        None, compute_op=ALU.add).then_inc(scattered_s, 16)
                pool.wait_ge(p_scaled, e * 2 + 2 + START)
                pool.sem_inc(released, 1)
                pool.indirect_dma_start(d["acc"], bass.IndirectOffsetOnAxis(scatter_p[:, 0:1], 0), y_p[:],
                                        None, compute_op=ALU.add).then_inc(scattered_p, 16)
                pool.wait_ge(scattered_s, (e + 1) * 16)
                pool.wait_ge(scattered_p, (e + 1) * 16)
                pool.sem_inc(y_free, 1)
            pool.wait_ge(gathered, (EXPERTS + 1) * 32)

        @block.scalar
        def _(act):
            def split(n0, c):
                act.wait_ge(w_in[c % SLOTS], n0 * (16 // SLOTS) + 16 * (c // SLOTS + 1))
                act.activation(w_hi[:, c % SLOTS, :], w[:, c % SLOTS, :], ACT.Copy).then_inc(hi_w, 1)

            def turn(fills, i):
                act.wait_ge(x_turned, fills + i + 1)
                act.activation(x_hi[:, 2 * i:2 * i + 2, :].rearrange("p j c -> p (j c)"),
                               bank[6 + i % 2][:, 0:PAIR], ACT.Copy).then_inc(hi_x, 1)

            for c in range(AHEAD):
                split(0, c)
            for i in range(FILLS):
                turn(0, i)
            with act.Fori(0, EXPERTS) as e:
                pairs, tiles = e * (FT // 2), e * DT

                def finish(q):
                    p, i = q // 2, q - UP_CHUNKS
                    if q < UP_CHUNKS and q % 2 == 0:
                        if p >= 2:
                            act.wait_ge(hidden, pairs + p - 1)
                        act.activation(silu[:, p % 2, :], bank[q % 4][:, 0:PAIR], ACT.Silu).then_inc(gated, 1)
                    elif q < UP_CHUNKS:
                        act.wait_ge(hidden, pairs + p + 1)
                        act.activation(h_hi[:, 2 * p:2 * p + 2, :].rearrange("p j c -> p (j c)"),
                                       hid[:, p % 2, :], ACT.Copy).then_inc(hi_h, 1)
                    else:
                        act.activation(y[:, i, :], bank[4 + i % 2][:, 0:CAP], ACT.Copy).then_inc(y_copied, 1)
                        if 1 <= i <= FILLS:
                            turn((e + 1) * FILLS, i - 1)

                def scale(k):
                    act.wait_ge(y_turned, e * 4 + 2 * k + 1)
                    if k == 0:
                        act.wait_ge(columns, FIRST_COPIES + (e + 1) * COPIES)
                        act.wait_ge(y_free, e + START)
                    act.activation(y_s[:, 512 * k:512 * k + 512], bank[6][:], ACT.Copy,
                                   scale=gate_s[:, 0:1]).then_inc(s_scaled, 1)

                for c in range(W_CHUNKS):
                    act.wait_ge(chunk_done, e * W_CHUNKS + c + START)
                    split(e * W_CHUNKS, c + AHEAD)
                    if c > 0:
                        finish(c - 1)
                    if c == UP_CHUNKS + 5:
                        scale(0)
                act.wait_ge(chunk_done, (e + 1) * W_CHUNKS + START)
                finish(W_CHUNKS - 1)
                scale(1)

        @block.vector
        def _(dve):
            def split(n0, c):
                dve.wait_ge(hi_w, n0 + c + 1)
                dve.tensor_tensor(w_lo[:, c % SLOTS, :], w[:, c % SLOTS, :], w_hi[:, c % SLOTS, :].bitcast(F32),
                                  ALU.subtract).then_inc(lo_w, 1)

            def turn(fills, i):
                dve.wait_ge(hi_x, fills + i + 1)
                dst = x_lo[:, 2 * i:2 * i + 2, :].rearrange("p j c -> p (j c)")
                dve.tensor_tensor(dst, bank[6 + i % 2][:, 0:PAIR],
                                  x_hi[:, 2 * i:2 * i + 2, :].rearrange("p j c -> p (j c)").bitcast(F32),
                                  ALU.subtract).then_inc(lo_x, 1)

            dve.sem_inc(lo_w, SLOTS)
            for c in range(AHEAD):
                split(0, c)
            for i in range(FILLS):
                turn(0, i)
            with dve.Fori(0, EXPERTS) as e:
                pairs = e * (FT // 2)

                def scale(k):
                    dve.wait_ge(y_turned, e * 4 + 2 * k + 2)
                    if k == 0:
                        dve.wait_ge(columns, FIRST_COPIES + (e + 1) * COPIES)
                        dve.wait_ge(y_free, e + START)
                    dve.tensor_scalar(y_p[:, 512 * k:512 * k + 512], bank[7][0:P_CAP, :], gate_p[:, 0:1], None,
                                      ALU.mult).then_inc(p_scaled, 1)

                for c in range(W_CHUNKS):
                    q = c - 1
                    p = q // 2
                    up = 0 < q < UP_CHUNKS and q % 2 == 1
                    if up:
                        dve.wait_ge(chunk_done, e * W_CHUNKS + c + START)
                        dve.wait_ge(gated, pairs + p + 1)
                        if p >= 2:
                            dve.wait_ge(hi_h, pairs + p - 1)
                        dve.tensor_tensor(hid[:, p % 2, :], bank[q % 4][:, 0:PAIR], silu[:, p % 2, :],
                                          ALU.mult).then_inc(hidden, 1)
                    split(e * W_CHUNKS, c + AHEAD)
                    if up:
                        dve.wait_ge(hi_h, pairs + p + 1)
                        dve.tensor_tensor(h_lo[:, 2 * p:2 * p + 2, :].rearrange("p j c -> p (j c)"),
                                          hid[:, p % 2, :],
                                          h_hi[:, 2 * p:2 * p + 2, :].rearrange("p j c -> p (j c)").bitcast(F32),
                                          ALU.subtract).then_inc(lo_h, 1)
                    if UP_CHUNKS + 1 <= q <= UP_CHUNKS + FILLS:
                        turn((e + 1) * FILLS, q - UP_CHUNKS - 1)
                    if c == UP_CHUNKS + 5:
                        scale(0)
                scale(1)

        @block.tensor
        def _(pe):
            def turn(fills, i, arrived):
                pe.wait_ge(gathered, arrived)
                for j in range(2):
                    c = slice((2 * i + j) * P, (2 * i + j + 1) * P)
                    nc.tensor.transpose(bank[6 + i % 2][:, j * CAP:j * CAP + S_CAP], x_s[:, c], ident[:])
                    last = nc.tensor.transpose(bank[6 + i % 2][:, j * CAP + S_CAP:(j + 1) * CAP], x_p[:, c],
                                               ident[0:P_CAP, 0:P_CAP])
                last.then_inc(x_turned, 1)

            pe.wait_ge(const_in, 16)
            pe.sem_inc(chunk_done, START)
            pe.sem_inc(s_scaled, START)
            pe.sem_inc(p_scaled, START)
            for i in range(FILLS):
                if i >= 2:
                    pe.wait_ge(lo_x, i - 1)
                turn(0, i, 32)
            with pe.Fori(0, EXPERTS) as e:
                pairs, tiles = e * (FT // 2), e * DT

                def turn_back(k):
                    pe.wait_ge(y_copied, tiles + 4 * (k + 1))
                    for at, (c0, n) in enumerate(((0, S_CAP), (S_CAP, P_CAP))):
                        for j in range(4):
                            last = nc.tensor.transpose(bank[6 + at][0:n, j * P:(j + 1) * P],
                                                       y[:, 4 * k + j, c0:c0 + n], ident[:])
                        last.then_inc(y_turned, 1)

                pe.wait_ge(lo_x, (e + 1) * FILLS)
                for c in range(W_CHUNKS):
                    pe.wait_ge(lo_w, e * W_CHUNKS + c + 1 + SLOTS)
                    hi = w_hi[:, c % SLOTS, :]
                    lo = w_lo[:, c % SLOTS, :]
                    if c < UP_CHUNKS:
                        if c >= 4:
                            pe.wait_ge(hidden if c % 2 else gated, pairs + (c - 4) // 2 + 1)
                        for f in range(2):
                            out = bank[c % 4][:, f * CAP:(f + 1) * CAP]
                            for j in range(DT):
                                a = slice((2 * j + f) * P, (2 * j + f + 1) * P)
                                last = three_pass(nc, out, (hi[:, a], lo[:, a]), (x_hi[:, j, :], x_lo[:, j, :]),
                                                  j == 0, j == DT - 1)
                        last.then_inc(chunk_done, 1)
                        continue
                    i = c - UP_CHUNKS
                    if i == 0:
                        pe.wait_ge(lo_h, pairs + FT // 2 - 1)
                    if i >= 2:
                        pe.wait_ge(y_copied, tiles + i - 1)
                    for f in range(FT):
                        if i == 0 and f == FT - 2:
                            pe.wait_ge(lo_h, pairs + FT // 2)
                        a = slice(f * P, (f + 1) * P)
                        last = three_pass(nc, bank[4 + i % 2][:, 0:CAP], (hi[:, a], lo[:, a]),
                                          (h_hi[:, f, :], h_lo[:, f, :]), f == 0, f == FT - 1)
                    last.then_inc(chunk_done, 1)
                    if i < FILLS:
                        if i == 0:
                            pe.wait_ge(s_scaled, e * 2 + START)
                        elif i == 1:
                            pe.wait_ge(p_scaled, e * 2 + START)
                        else:
                            pe.wait_ge(lo_x, (e + 1) * FILLS + i - 1)
                        turn((e + 1) * FILLS, i, (e + 2) * 32)
                    if i == 4:
                        pe.wait_ge(lo_x, (e + 2) * FILLS)
                        turn_back(0)
                pe.wait_ge(s_scaled, e * 2 + 1 + START)
                pe.wait_ge(p_scaled, e * 2 + 1 + START)
                turn_back(1)


def finish(nc, d):
    ctx = ExitStack()
    with ctx:
        sb, ps, sem = buffers(nc, ctx)
        gain = sb("fi_gain", [P, D])
        eps = sb("fi_eps", [P, 1])
        x = sb("fi_x", [P, G_TILES, D])
        out = sb("fi_out", [P, G_TILES, D])
        junk = sb("fi_junk", [P, D], BF16)
        ss, rt, rs = (sb(f"fi_{n}", [P, G_TILES]) for n in ("ss", "rt", "rs"))
        tmp = sb("fi_tmp", [P, 3])
        const_in, eps_set = sem("fi_const_in"), sem("fi_eps_set")
        x_in = [sem(f"fi_x_in{i}") for i in range(G_TILES)]
        stored = [sem(f"fi_stored{i}") for i in range(G_TILES)]
        squared, root, refined = sem("fi_squared"), sem("fi_root"), sem("fi_refined")
        normed = sem("fi_normed")
        block = ctx.enter_context(nc.Block())

        @block.sync
        def _(sp):
            sp.dma_start(gain[:], d["g_final"]).then_inc(const_in, 16)
            with sp.Fori(0, GROUPS) as g:
                for t in range(G_TILES):
                    sp.wait_ge(normed, g * G_TILES + t + 1)
                    sp.dma_start(x[:, t, :], d["acc_groups"][g, t]).then_inc(x_in[t], 16)
                for t in range(G_TILES):
                    sp.wait_ge(normed, (g + 1) * G_TILES + t + 1)
                    sp.dma_start(d["out_groups"][g, t], out[:, t, :]).then_inc(stored[t], 16)
            for t in range(G_TILES):
                sp.wait_ge(stored[t], 16 * GROUPS + START)

        @block.gpsimd
        def _(pool):
            pool.memset(eps[:], EPS).then_inc(eps_set, 1)

        @block.scalar
        def _(act):
            act.wait_ge(eps_set, 1)
            act.sem_inc(squared, START)
            with act.Fori(0, GROUPS) as g:
                for t in range(G_TILES):
                    act.wait_ge(x_in[t], g * 16 + 16)
                    act.wait_ge(squared, g * G_TILES + t + START)
                    act.activation(junk[:], x[:, t, :], ACT.Square, accum_out=ss[:, t:t + 1]).then_inc(squared, 1)
                    act.wait_ge(squared, g * G_TILES + t + 1 + START)
                    act.activation(rt[:, t:t + 1], ss[:, t:t + 1], ACT.Sqrt, bias=eps[:],
                                   scale=1.0 / D).then_inc(root, 1)

        @block.vector
        def _(dve):
            dve.sem_inc(normed, G_TILES)
            for t in range(G_TILES):
                dve.sem_inc(stored[t], START)
            dve.wait_ge(const_in, 16)
            with dve.Fori(0, GROUPS) as g:
                for t in range(G_TILES):
                    dve.wait_ge(root, g * G_TILES + t + 1)
                    inverse_root(dve, refined, (g * G_TILES + t) * REFINE, ss[:, t:t + 1], rt[:, t:t + 1],
                                 [tmp[:, i:i + 1] for i in range(3)], rs[:, t:t + 1], 1.0 / D)
                    dve.wait_ge(stored[t], g * 16 + START)
                    dve.scalar_tensor_tensor(out=out[:, t, :], in0=x[:, t, :], scalar=rs[:, t:t + 1],
                                             in1=gain[:], op0=ALU.mult, op1=ALU.mult).then_inc(normed, 1)


def program(nc, d):
    d["o"] = nc.dram_tensor("o_scratch", [TILES, P, D], F32, kind="Internal").ap()
    d["h"] = nc.dram_tensor("h_scratch", [TOK, D], F32, kind="Internal").ap()
    d["acc"] = nc.dram_tensor("acc_scratch", [TOK, D], F32, kind="Internal").ap()
    d["x_tiles"] = d["x"].rearrange("g t p e -> (g t) p e")
    d["h_tiles"] = d["h"].rearrange("(t p) e -> t p e", p=P)
    d["acc_tiles"] = d["acc"].rearrange("(t p) e -> t p e", p=P)
    d["acc_groups"] = d["acc"].rearrange("(g t p) e -> g t p e", p=P, t=G_TILES)
    d["out_groups"] = d["out"].rearrange("(g t p) e -> g t p e", p=P, t=G_TILES)
    with ExitStack() as outer:
        sb, _, _ = buffers(nc, outer)
        keep = Heads(
            q=sb("q", [P, QA + QB, TOK]),
            k=sb("k", [P, KA + KB, TOK]),
            v=sb("v", [P, TILES, V_CHUNKS * P]),
        )
        project(nc, d, keep)
        attend(nc, d, keep)
    with ExitStack() as outer:
        sb, _, _ = buffers(nc, outer)
        route = Route(
            rows=sb("rows", [PROMPT_AT + EXPERTS, 2, S_TOK]),
            gates=sb("gates", [P, 2, EXPERTS]),
            index=sb("index", [P, 2, EXPERTS + 1], U32),
        )
        mix(nc, d, route)
        choose(nc, d, route)
        experts(nc, d, route)
    finish(nc, d)


def columns():
    qa0, ka0, va0 = 0, 512, 640
    qb0, kb0, vb0 = 768, 1280, 1792
    span = lambda a, n=P: list(range(a, a + n))
    out = [span(qa0 + HD * c, HD) + span(qa0 + HD * (c + 4), HD) for c in range(QA)]
    out += [span(ka0)]
    out += [span(qb0 + P * c) for c in range(QB)] + [span(kb0 + P * c) for c in range(KB)]
    out += [span(va0)] + [span(vb0 + P * c) for c in range(V_CHUNKS - 1)]
    return np.array(out)


def constants():
    c = {}
    inv = np.float32(500000.0) ** (-(np.arange(ROT_HALF, dtype=np.float32) * np.float32(2.0))
                                   / np.float32(2 * ROT_HALF))
    ang = (np.arange(S_TOK, dtype=np.float32)[:, None] * inv[None, :]).astype(np.float32)
    cos = np.ones((P, S_TOK), np.float32)
    sin = np.zeros((P, S_TOK), np.float32)
    rot = np.zeros((P, P), np.float32)
    for p in range(P):
        dd = p % HD
        if dd < 2 * ROT_HALF:
            cos[p] = np.cos(ang[:, dd % ROT_HALF])
            sin[p] = np.sin(ang[:, dd % ROT_HALF])
            if dd < ROT_HALF:
                rot[p + ROT_HALF, p] = -1.0
            else:
                rot[p - ROT_HALF, p] = 1.0
    c["cos"] = np.stack([cos[:, 0:512], cos[:, 512:1024], cos[:, 0:512]])
    c["sin"] = np.stack([sin[:, 0:512], sin[:, 512:1024], sin[:, 0:512]])
    c["rot"] = rot
    i, j = np.arange(P)[:, None], np.arange(3 * P)[None, :]
    c["band"] = np.where(np.abs(j - P - i) <= P, 0.0, NEG).astype(np.float32)
    qc, kc = np.arange(P)[:, None] % GRID_W, np.arange(GRID_W)[None, :]
    cs = np.clip(qc - 8, 0, GRID_W - 16)
    c["col_mask"] = np.where((kc >= cs) & (kc < cs + 16), 0.0, NEG).astype(np.float32)
    row_mask = np.zeros((P, NEAR_ROWS, GRID_W), np.float32)
    row_mask[GRID_W:, 0] = NEG
    row_mask[:GRID_W, NEAR_ROWS - 1] = NEG
    c["row_mask"] = row_mask.reshape(P, NEAR_KEYS)
    c["ident"] = np.eye(P, dtype=np.float32)
    return c


def layouts(i):
    a = {}
    x = np.concatenate([i["x_sample"][0], i["x_prompt"][0]])
    a["x"] = x.reshape(GROUPS, G_TILES, P, D)
    w = i["w_in"][0].reshape(DT, P, -1)[:, :, columns()]
    a["w_in"] = w.transpose(2, 1, 0, 3).reshape(CHUNKS, P, D)
    pad = np.pad(i["rpb_b"][0], ((0, 0), (0, 0), (GRID_W - 16, GRID_W - 16)))
    a["rpb"] = np.stack([pad[:, :, GRID_W - 1 - c:2 * GRID_W - 1 - c] for c in range(GRID_W)])
    order = [h for c in range(PAIRS) for h in (c, c + PAIRS)]
    a["sink"] = np.broadcast_to(i["sink_a"][0][order], (P, 2 * PAIRS))
    a["w_out"] = i["w_out"][0].reshape(DT, P, D)
    a["w_router"] = i["w_router"][0].reshape(DT, P, EXPERTS).transpose(1, 0, 2)
    up = np.stack([i["w_gate"][0], i["w_up"][0]], axis=1)
    up = up.reshape(EXPERTS, 2, DT, P, FT // 2, 2 * P).transpose(0, 4, 1, 3, 2, 5)
    down = i["w_down"][0].reshape(EXPERTS, FT, P, DT, P).transpose(0, 3, 2, 1, 4)
    a["w_experts"] = np.concatenate([up.reshape(EXPERTS, UP_CHUNKS, P, W_COLS),
                                     down.reshape(EXPERTS, DT, P, W_COLS)], axis=1)
    a["g_out"] = np.broadcast_to(np.concatenate([i["g_out_a"][0], i["g_out_b"][0]]), (P, D))
    a["g_ffn"] = np.broadcast_to(i["g_ffn"][0], (P, D))
    a["g_final"] = np.broadcast_to(i["g_final"], (P, D))
    a["g_attn"] = np.broadcast_to(i["g_attn"][0], (P, D))
    return a


def kernel(**inputs):
    import concourse.bacc as bacc
    from concourse.bass_utils import run_bass_kernel_spmd

    given = {name: np.asarray(value) for name, value in inputs.items()}
    arrays = {**layouts(given), **constants()}
    nc = bacc.Bacc("TRN2", target_bir_lowering=False, num_devices=1)
    feeds, d = {}, {}
    for name, value in arrays.items():
        value = np.ascontiguousarray(value)
        feeds[f"in_{name}"] = value
        d[name] = nc.dram_tensor(f"in_{name}", value.shape, mybir.dt.from_np(value.dtype),
                                 kind="ExternalInput").ap()
    d["out"] = nc.dram_tensor("out_0", [TOK, D], F32, kind="ExternalOutput").ap()
    program(nc, d)
    result = run_bass_kernel_spmd(nc, [feeds], core_ids=[0]).results[0]["out_0"]
    return result[S_TOK:].reshape(1, P_TOK, D), result[:S_TOK].reshape(1, S_TOK, D)
```

```python
import numpy as np
from contextlib import ExitStack
import concourse.bass as bass
from concourse import mybir

F32 = mybir.dt.float32
F32R = mybir.dt.float32r
BF16 = mybir.dt.bfloat16
U32 = mybir.dt.uint32
ACT = mybir.ActivationFunctionType
ALU = mybir.AluOpType
AX = mybir.AxisListType

P = 128
D = 1024
DT = D // P
S_TOK, P_TOK = 1024, 512
TOK = S_TOK + P_TOK
TILES = TOK // P
S_TILES = S_TOK // P
GROUP = 512
G_TILES = GROUP // P
GROUPS = TOK // GROUP
HD = 64
ROT_HALF = 8
GRID_W = 64
KEY_ROWS = 8
QA, KA, QB, KB = 4, 1, 4, 4
V_CHUNKS = 5
ROTATED = QA + KA
CHUNKS = QA + KA + QB + KB + V_CHUNKS
FIRST_V = CHUNKS - V_CHUNKS
AGAIN = [*range(ROTATED), *range(FIRST_V, CHUNKS)]
EPS = 1e-6
SCALE = float(HD) ** -0.5
NEG = -1e30
EXPERTS = 16
DF = 2048
FT = DF // P
S_CAP, P_CAP = 2 * S_TOK // EXPERTS, 2 * P_TOK // EXPERTS
CAP = S_CAP + P_CAP
PROMPT_AT = 32


class Heads:

    def __init__(self, q, k, v):
        self.q, self.k, self.v = q, k, v


class Route:

    def __init__(self, rows, gates, index):
        self.rows, self.gates, self.index = rows, gates, index


def buffers(nc, ctx):
    def sb(name, shape, dt=F32):
        return ctx.enter_context(nc.sbuf_tensor(name, shape, dt))

    def ps(name, shape, dt=F32):
        return ctx.enter_context(nc.psum_tensor(name, shape, dt))

    def sem(name):
        return ctx.enter_context(nc.semaphore(name))

    return sb, ps, sem


def three_pass(nc, out, stationary, moving, first, last):
    (sh, sl), (mh, ml) = stationary, moving
    nc.tensor.matmul(out, sh, mh, start=first, stop=False)
    nc.tensor.matmul(out, sh, ml, start=False, stop=False)
    return nc.tensor.matmul(out, sl, mh, start=False, stop=last)


START = 1
REFINE = 6


def inverse_root(dve, step, done, ss, rt, tmp, out, scale):
    mean, sq, corr = tmp
    dve.reciprocal(out, rt).then_inc(step, 1)
    dve.tensor_scalar(mean, ss, scale, EPS, ALU.mult, ALU.add).then_inc(step, 1)
    dve.wait_ge(step, done + 2)
    dve.tensor_tensor(sq, out, out, ALU.mult).then_inc(step, 1)
    dve.wait_ge(step, done + 3)
    dve.tensor_tensor(corr, sq, mean, ALU.mult).then_inc(step, 1)
    dve.wait_ge(step, done + 4)
    dve.tensor_scalar(sq, corr, -0.5, 1.5, ALU.mult, ALU.add).then_inc(step, 1)
    dve.wait_ge(step, done + 5)
    dve.tensor_tensor(out, out, sq, ALU.mult).then_inc(step, 1)
    dve.wait_ge(step, done + 6)


def project(nc, d, keep):
    ctx = ExitStack()
    with ctx:
        sb, ps, sem = buffers(nc, ctx)
        X_SLOTS, W_SLOTS, AHEAD = 2, 3, 2
        x = sb("pj_x", [P, X_SLOTS, D])
        xn = sb("pj_xn", [P, D])
        junk = sb("pj_junk", [P, D], BF16)
        gain = sb("pj_gain", [P, D])
        eps = sb("pj_eps", [P, 1])
        ss = sb("pj_ss", [P, G_TILES])
        rt = sb("pj_rt", [P, G_TILES])
        rs = sb("pj_rs", [P, G_TILES])
        tmp = sb("pj_tmp", [P, 3])
        ident = sb("pj_ident", [P, P])
        rot = sb("pj_rot", [P, P])
        x_hi = sb("pj_x_hi", [P, DT, GROUP], F32R)
        x_lo = sb("pj_x_lo", [P, DT, GROUP], F32R)
        w = sb("pj_w", [P, W_SLOTS, D])
        w_hi = sb("pj_w_hi", [P, W_SLOTS, DT, P], F32R)
        w_lo = sb("pj_w_lo", [P, W_SLOTS, DT, P], F32R)
        cos = sb("pj_cos", [P, GROUP])
        sin = sb("pj_sin", [P, GROUP])
        raw = sb("pj_raw", [P, 2, GROUP])
        turned = sb("pj_turned", [P, GROUP])
        bank = [ps(f"pj_ps{i}", [P, 512]) for i in range(8)]

        const_in = sem("pj_const_in")
        eps_set = sem("pj_eps_set")
        x_in = [sem(f"pj_x_in{i}") for i in range(X_SLOTS)]
        w_in = [sem(f"pj_w_in{i}") for i in range(W_SLOTS)]
        table_in = sem("pj_table_in")
        squared = sem("pj_squared")
        root = sem("pj_root")
        refined = sem("pj_refined")
        normed = sem("pj_normed")
        transposed = sem("pj_transposed")
        hi_x = sem("pj_hi_x")
        lo_x = sem("pj_lo_x")
        hi_w = sem("pj_hi_w")
        lo_w = sem("pj_lo_w")
        chunk_done = sem("pj_chunk_done")
        taken = sem("pj_taken")
        swapped = sem("pj_swapped")
        rotated = sem("pj_rotated")
        again_done = sem("pj_again_done")
        block = ctx.enter_context(nc.Block())

        @block.sync
        def _(sp):
            for dst, src in ((gain, d["g_attn"]), (ident, d["ident"]), (rot, d["rot"])):
                sp.dma_start(dst[:], src).then_inc(const_in, 16)
            with sp.Fori(0, GROUPS) as g:
                for t in range(X_SLOTS):
                    sp.wait_ge(normed, g * G_TILES + t + 1)
                    sp.dma_start(x[:, t % X_SLOTS, :], d["x"][g, t]).then_inc(x_in[t % X_SLOTS], 16)
                for n in range(W_SLOTS):
                    sp.wait_ge(lo_w, g * CHUNKS + n + 1)
                    sp.dma_start(w[:, n % W_SLOTS, :], d["w_in"][n]).then_inc(w_in[n % W_SLOTS], 16)
                for t in range(X_SLOTS, G_TILES):
                    sp.wait_ge(normed, g * G_TILES + t + 1)
                    sp.dma_start(x[:, t % X_SLOTS, :], d["x"][g, t]).then_inc(x_in[t % X_SLOTS], 16)
                sp.wait_ge(again_done, g * len(AGAIN) + 2)
                sp.dma_start(cos[:], d["cos"][g]).then_inc(table_in, 16)
                sp.dma_start(sin[:], d["sin"][g]).then_inc(table_in, 16)
                for n in range(W_SLOTS, CHUNKS):
                    sp.wait_ge(lo_w, g * CHUNKS + n + 1)
                    sp.dma_start(w[:, n % W_SLOTS, :], d["w_in"][n]).then_inc(w_in[n % W_SLOTS], 16)

        @block.gpsimd
        def _(pool):
            pool.memset(eps[:], EPS).then_inc(eps_set, 1)

        @block.scalar
        def _(act):
            act.wait_ge(eps_set, 1)
            act.sem_inc(taken, 2)
            act.sem_inc(squared, START)
            with act.Fori(0, GROUPS) as g:
                def split(n):
                    act.wait_ge(w_in[n % W_SLOTS], g * (16 * CHUNKS // W_SLOTS) + 16 * (n // W_SLOTS + 1))
                    act.activation(w_hi[:, n % W_SLOTS, :, :].rearrange("p j c -> p (j c)"),
                                   w[:, n % W_SLOTS, :], ACT.Copy).then_inc(hi_w, 1)

                for t in range(G_TILES):
                    act.wait_ge(x_in[t % X_SLOTS], g * (16 * G_TILES // X_SLOTS) + 16 * (t // X_SLOTS + 1))
                    act.wait_ge(squared, g * G_TILES + t + START)
                    act.activation(junk[:], x[:, t % X_SLOTS, :], ACT.Square,
                                   accum_out=ss[:, t:t + 1]).then_inc(squared, 1)
                    act.wait_ge(squared, g * G_TILES + t + 1 + START)
                    act.activation(rt[:, t:t + 1], ss[:, t:t + 1], ACT.Sqrt, bias=eps[:, 0:1],
                                   scale=1.0 / D).then_inc(root, 1)
                    if t == 1:
                        split(0)
                    if t == 2:
                        split(1)
                for t in range(G_TILES):
                    for h in range(2):
                        act.wait_ge(transposed, g * (2 * G_TILES) + 2 * t + h + 1 + START)
                        act.activation(x_hi[:, 4 * h:4 * h + 4, t * P:(t + 1) * P],
                                       bank[2 * (t % 2) + h][:].rearrange("p (j c) -> p j c", j=4),
                                       ACT.Copy).then_inc(hi_x, 1)
                for n in range(CHUNKS + 1):
                    if n > 0:
                        act.wait_ge(chunk_done, g * CHUNKS + n)
                    if n + AHEAD < CHUNKS and n + AHEAD >= 2:
                        split(n + AHEAD)
                    if n == 0:
                        continue
                    q = n - 1
                    src = bank[4 + q % 2][:]
                    if q in AGAIN:
                        m = AGAIN.index(q)
                        act.wait_ge(again_done, g * len(AGAIN) + m + 1)
                        act.activation(raw[:, m % 2, :], src, ACT.Copy,
                                       scale=SCALE if q < QA else 1.0).then_inc(taken, 1)
                    elif q < ROTATED + QB:
                        act.activation(keep.q[:, QA + q - ROTATED, bass.ds(g * GROUP, GROUP)], src,
                                       ACT.Copy, scale=SCALE).then_inc(taken, 1)
                    else:
                        act.activation(keep.k[:, KA + q - ROTATED - QB, bass.ds(g * GROUP, GROUP)], src,
                                       ACT.Copy).then_inc(taken, 1)

        @block.vector
        def _(dve):
            dve.wait_ge(const_in, 48)
            dve.sem_inc(normed, X_SLOTS)
            dve.sem_inc(lo_w, W_SLOTS)
            dve.sem_inc(again_done, 2)
            dve.sem_inc(transposed, START)
            with dve.Fori(0, GROUPS) as g:
                def split(n):
                    dve.wait_ge(hi_w, g * CHUNKS + n + 1)
                    dve.tensor_tensor(w_lo[:, n % W_SLOTS, :, :].rearrange("p j c -> p (j c)"),
                                      w[:, n % W_SLOTS, :],
                                      w_hi[:, n % W_SLOTS, :, :].rearrange("p j c -> p (j c)").bitcast(F32),
                                      ALU.subtract).then_inc(lo_w, 1)

                def norm(t):
                    dve.wait_ge(root, g * G_TILES + t + 1)
                    inverse_root(dve, refined, (g * G_TILES + t) * REFINE, ss[:, t:t + 1], rt[:, t:t + 1],
                                 [tmp[:, i:i + 1] for i in range(3)], rs[:, t:t + 1], 1.0 / D)
                    dve.wait_ge(transposed, g * (2 * G_TILES) + 2 * t + START)
                    dve.scalar_tensor_tensor(out=xn[:], in0=x[:, t % X_SLOTS, :], scalar=rs[:, t:t + 1],
                                             in1=gain[:], op0=ALU.mult, op1=ALU.mult).then_inc(normed, 1)

                def low(t):
                    for h in range(2):
                        dve.wait_ge(hi_x, g * (2 * G_TILES) + 2 * t + h + 1)
                        dst = x_lo[:, 4 * h:4 * h + 4, t * P:(t + 1) * P]
                        dve.tensor_tensor(dst, bank[2 * (t % 2) + h][:].rearrange("p (j c) -> p j c", j=4),
                                          x_hi[:, 4 * h:4 * h + 4, t * P:(t + 1) * P].bitcast(F32),
                                          ALU.subtract).then_inc(lo_x, 1)

                norm(0)
                norm(1)
                split(0)
                norm(2)
                low(0)
                split(1)
                norm(3)
                for t in range(1, G_TILES):
                    low(t)
                for n in range(CHUNKS + 2):
                    if n + AHEAD < CHUNKS:
                        split(n + AHEAD)
                    q = n - 2
                    if q not in AGAIN:
                        continue
                    m = AGAIN.index(q)
                    again = bank[6 + m % 2][:]
                    if q == 0:
                        dve.wait_ge(table_in, g * 32 + 32)
                    dve.wait_ge(swapped, g * len(AGAIN) + m + 1)
                    if q < ROTATED:
                        dve.tensor_tensor(turned[:], again, sin[:], ALU.mult).then_inc(rotated, 1)
                        dve.tensor_tensor(raw[:, m % 2, :], raw[:, m % 2, :], cos[:],
                                          ALU.mult).then_inc(rotated, 1)
                        dve.wait_ge(rotated, g * (2 * ROTATED) + 2 * q + 2)
                        dst = (keep.q[:, q, bass.ds(g * GROUP, GROUP)] if q < QA
                               else keep.k[:, 0, bass.ds(g * GROUP, GROUP)])
                        dve.tensor_tensor(dst, raw[:, m % 2, :], turned[:], ALU.add).then_inc(again_done, 1)
                        dve.wait_ge(again_done, g * len(AGAIN) + m + 3)
                    else:
                        v0 = (q - FIRST_V) * P
                        dve.tensor_copy(keep.v[:, bass.ds(g * G_TILES, G_TILES), v0:v0 + P],
                                        again.rearrange("p (t c) -> p t c", t=G_TILES)).then_inc(again_done, 1)

        @block.tensor
        def _(pe):
            pe.wait_ge(const_in, 48)
            with pe.Fori(0, GROUPS) as g:
                for t in range(G_TILES):
                    pe.wait_ge(normed, g * G_TILES + t + 1 + X_SLOTS)
                    for h in range(2):
                        if t >= 2:
                            pe.wait_ge(lo_x, g * (2 * G_TILES) + 2 * (t - 2) + h + 1)
                        for j in range(4):
                            c0 = (4 * h + j) * P
                            last = nc.tensor.transpose(bank[2 * (t % 2) + h][:, j * P:(j + 1) * P],
                                                       xn[:, c0:c0 + P], ident[:])
                        last.then_inc(transposed, 1)
                for n in range(CHUNKS + 1):
                    if n < CHUNKS:
                        pe.wait_ge(lo_w, g * CHUNKS + n + 1 + W_SLOTS)
                        pe.wait_ge(taken, g * CHUNKS + n + 1)
                        if n == 0:
                            pe.wait_ge(lo_x, (g + 1) * (2 * G_TILES))
                        s = n % W_SLOTS
                        for j in range(DT):
                            last = three_pass(nc, bank[4 + n % 2][:], (w_hi[:, s, j, :], w_lo[:, s, j, :]),
                                              (x_hi[:, j, :], x_lo[:, j, :]), j == 0, j == DT - 1)
                        last.then_inc(chunk_done, 1)
                    q = n - 1
                    if q not in AGAIN:
                        continue
                    m = AGAIN.index(q)
                    pe.wait_ge(taken, g * CHUNKS + q + 3)
                    pe.wait_ge(again_done, g * len(AGAIN) + m + 1)
                    if q < ROTATED:
                        last = nc.tensor.matmul(bank[6 + m % 2][:], rot[:], raw[:, m % 2, :], start=True,
                                                stop=True)
                    else:
                        for t in range(G_TILES):
                            c = slice(t * P, (t + 1) * P)
                            last = nc.tensor.transpose(bank[6 + m % 2][:, c], raw[:, m % 2, c], ident[:])
                    last.then_inc(swapped, 1)


WINDOW_KEYS = 3 * P
NEAR_ROWS = KEY_ROWS + 1
NEAR_KEYS = NEAR_ROWS * GRID_W
DELTAS = 14
PAIRS = 4


def attention_units():
    window, near = [], []
    for first, tiles in ((0, S_TILES), (S_TILES, TILES - S_TILES)):
        for b in range(tiles):
            lo, hi = max(b - 1, 0), min(b + 1, tiles - 1)
            window.append((True, first + b, first + lo, (hi - lo + 1) * P, (lo - b + 1) * P))
            rows = 2 * tiles
            if 2 * b >= KEY_ROWS // 2 and 2 * b + 1 <= rows - KEY_ROWS // 2 and rows > KEY_ROWS:
                near.append((False, first + b, first + b - 2, NEAR_KEYS, None))
            else:
                lo = 0 if 2 * b < KEY_ROWS // 2 or rows == KEY_ROWS else (rows - KEY_ROWS) // 2
                near.append((False, first + b, first + lo, KEY_ROWS * GRID_W, 2 * (lo - b) + 6))
    lead = 4
    turns = [b for pair in zip(window[lead:], near) for b in pair]
    return window[:lead] + turns + near[len(window) - lead:]


def attend(nc, d, keep):
    ctx = ExitStack()
    with ctx:
        sb, ps, sem = buffers(nc, ctx)
        blocks = attention_units()
        units = [(*blk, pair, bi) for bi, blk in enumerate(blocks) for pair in range(PAIRS)]
        N = len(units)
        window_units = [sum(x[0] for x in units[:u]) for u in range(N)]
        first_near = next(u for u in range(N) if not units[u][0])
        PROBS, STATS, FLIPS, BANKS, OUTS = 6, 4, 6, 2, 2

        groups, first_group = [], []
        for u, (window, _, _, keys, *_) in enumerate(units):
            first_group.append(len(groups))
            full = keys // P
            for h in range(2):
                groups.append((u, [(h, i, P, i * P) for i in range(full)]))
            if keys % P:
                groups.append((u, [(h, full, keys % P, h * P) for h in range(2)]))
        first_group.append(len(groups))

        bias = sb("at_bias", [P, 2 * PAIRS, DELTAS, GRID_W])
        inner = sb("at_inner", [P, 2 * PAIRS, NEAR_KEYS])
        col_mask = sb("at_col_mask", [P, GRID_W])
        row_mask = sb("at_row_mask", [P, NEAR_KEYS])
        band = sb("at_band", [P, WINDOW_KEYS])
        sink = sb("at_sink", [P, 2 * PAIRS])
        neg_sink = sb("at_neg_sink", [P, 2 * PAIRS])
        ident = sb("at_ident", [P, P])
        probs = sb("at_probs", [P, PROBS, NEAR_KEYS])
        flipped = sb("at_flipped", [P, FLIPS, 512])
        o = sb("at_o", [P, 2, 512])
        top, neg_top, at_sink, e_sink, sums, den, rden = (
            sb(f"at_{n}", [P, STATS, 2]) for n in ("top", "neg_top", "at_sink", "e_sink", "sums", "den", "rden"))
        score = [ps(f"at_score{h}", [P, 1024]) for h in range(2)]
        flip_ps = [ps(f"at_flip{i}", [P, 512]) for i in range(BANKS)]
        out_ps = [ps(f"at_out{i}", [P, 512]) for i in range(OUTS)]

        const_in = sem("at_const_in")
        bias_in = sem("at_bias_in")
        negated = sem("at_negated")
        masked = sem("at_masked")
        scored = sem("at_scored")
        added = sem("at_added")
        bounded = sem("at_bounded")
        sink_at = sem("at_sink_at")
        exped = sem("at_exped")
        sink_exped = sem("at_sink_exped")
        summed = sem("at_summed")
        inverted = sem("at_inverted")
        flipped_ps = sem("at_flipped_ps")
        copied = [sem("at_copied_act"), sem("at_copied_dve")]
        weighed = sem("at_weighed")
        scaled = sem("at_scaled")
        stored = [sem(f"at_stored{i}") for i in range(2)]
        block = ctx.enter_context(nc.Block())

        def copies(engine, upto):
            return (upto + 1 - engine) // 2

        def copy_groups(eng, engine, v):
            for g in range(first_group[v], first_group[v + 1]):
                if g % 2 != engine:
                    continue
                eng.wait_ge(flipped_ps, g + 1)
                if g >= FLIPS:
                    eng.wait_ge(weighed, groups[g - FLIPS][0] + 1)
                items = groups[g][1]
                rows, width = items[0][2], len(items) * P
                dst, src = flipped[0:rows, g % FLIPS, 0:width], flip_ps[g % BANKS][0:rows, 0:width]
                if engine == 0:
                    nc.scalar.activation(dst, src, ACT.Copy).then_inc(copied[0], 1)
                else:
                    nc.vector.tensor_copy(dst, src).then_inc(copied[1], 1)

        @block.sync
        def _(sp):
            sp.dma_start(ident[:], d["ident"]).then_inc(const_in, 16)
            sp.dma_start(band[:], d["band"]).then_inc(const_in, 16)
            sp.dma_start(sink[:], d["sink"]).then_inc(const_in, 16)
            sp.dma_start(col_mask[:], d["col_mask"]).then_inc(bias_in, 16)
            sp.dma_start(row_mask[:], d["row_mask"]).then_inc(bias_in, 16)
            for r in range(2):
                sp.dma_start(bias[r * GRID_W:(r + 1) * GRID_W, :, :, :],
                             d["rpb"][:, :, 1 - r:1 - r + DELTAS, :]).then_inc(bias_in, 16)
            for bi, (window, tile, *_) in enumerate(blocks):
                sp.wait_ge(scaled, PAIRS * (bi + 1))
                c0 = 0 if window else 512
                sp.dma_start(d["o"][tile][:, c0:c0 + 512], o[:, bi % 2, :]).then_inc(stored[bi % 2], 16)
            for i in range(2):
                sp.wait_ge(stored[i], 16 * len(blocks) // 2)

        @block.gpsimd
        def _(pool):
            pool.wait_ge(bias_in, 64)
            flat = bias[:].rearrange("p h r c -> p (h r) c")
            pool.tensor_tensor(flat, flat, col_mask[:].unsqueeze(1).broadcast_to([P, 2 * PAIRS * DELTAS, GRID_W]),
                               ALU.add).then_inc(masked, 1)
            pool.wait_ge(masked, 1)
            rows = bias[:, :, 2:2 + NEAR_ROWS, :].rearrange("p h r c -> p h (r c)")
            pool.tensor_tensor(inner[:], rows, row_mask[:].unsqueeze(1).broadcast_to([P, 2 * PAIRS, NEAR_KEYS]),
                               ALU.add).then_inc(masked, 1)

        @block.scalar
        def _(act):
            for u in range(N + 1):
                if u < N:
                    window, r = units[u][0], u % STATS
                    act.wait_ge(bounded, u + 1)
                    for h in range(2):
                        p = probs[:, (2 * u + h) % PROBS, 0:units[u][3]]
                        act.activation(p, p, ACT.Exp, bias=neg_top[:, r, h:h + 1],
                                       accum_out=sums[:, r, h:h + 1]).then_inc(exped, 1)
                    if window:
                        act.wait_ge(sink_at, window_units[u] + 1)
                        act.activation(e_sink[:, r, :], at_sink[:, r, :], ACT.Exp).then_inc(sink_exped, 1)
                if u >= 1:
                    copy_groups(act, 0, u - 1)

        @block.vector
        def _(dve):
            dve.wait_ge(const_in, 48)
            dve.tensor_scalar(neg_sink[:], sink[:], -1.0, None, ALU.mult).then_inc(negated, 1)
            dve.wait_ge(negated, 1)
            for u in range(N + 2):
                if u < N:
                    window, tile, key0, keys, off, pair, bi = units[u]
                    r = u % STATS
                    if u == first_near:
                        dve.wait_ge(masked, 2)
                    for h in range(2):
                        dve.wait_ge(scored, 2 * u + h + 1)
                        if 2 * u + h >= PROBS:
                            dve.wait_ge(flipped_ps, first_group[u - PROBS // 2 + 1])
                        if window:
                            add = band[:, off:off + keys]
                        elif off is None:
                            add = inner[:, 2 * pair + h, :]
                        else:
                            add = bias[:, 2 * pair + h, off:off + KEY_ROWS, :].rearrange("p r c -> p (r c)")
                        dve.tensor_tensor_reduce(out=probs[:, (2 * u + h) % PROBS, 0:keys],
                                                 in0=score[h][:, 0:keys], in1=add, scale=1.0, scalar=-3.0e38,
                                                 op0=ALU.add, op1=ALU.max,
                                                 accum_out=top[:, r, h:h + 1]).then_inc(added, 1)
                    dve.wait_ge(added, 2 * u + 2)
                    if window:
                        mine = neg_sink[:, 2 * pair:2 * pair + 2]
                        dve.scalar_tensor_tensor(out=neg_top[:, r, :], in0=top[:, r, :], scalar=-1.0, in1=mine,
                                                 op0=ALU.mult, op1=ALU.min).then_inc(bounded, 1)
                        dve.wait_ge(bounded, u + 1)
                        dve.tensor_tensor(at_sink[:, r, :], neg_top[:, r, :], mine,
                                          ALU.subtract).then_inc(sink_at, 1)
                    else:
                        dve.tensor_scalar(neg_top[:, r, :], top[:, r, :], -1.0, None,
                                          ALU.mult).then_inc(bounded, 1)
                if 1 <= u < N + 1:
                    v, r = u - 1, (u - 1) % STATS
                    dve.wait_ge(exped, 2 * v + 2)
                    total = sums
                    if units[v][0]:
                        dve.wait_ge(sink_exped, window_units[v] + 1)
                        dve.tensor_tensor(den[:, r, :], sums[:, r, :], e_sink[:, r, :],
                                          ALU.add).then_inc(summed, 1)
                        dve.wait_ge(summed, window_units[v] + 1)
                        total = den
                    dve.reciprocal(rden[:, r, :], total[:, r, :]).then_inc(inverted, 1)
                    copy_groups(dve, 1, v)
                if u >= 2:
                    v, r = u - 2, (u - 2) % STATS
                    window, _, _, _, _, pair, bi = units[v]
                    dve.wait_ge(weighed, v + 1)
                    dve.wait_ge(inverted, v + 1)
                    if pair == 0 and bi >= 2:
                        dve.wait_ge(stored[bi % 2], 16 * (bi // 2))
                    if window:
                        dst = o[:, bi % 2, :].rearrange("p (h c e) -> p h c e", h=2, c=PAIRS)[:, :, pair, :]
                    else:
                        dst = o[:, bi % 2, pair * P:(pair + 1) * P].rearrange("p (h e) -> p h e", h=2)
                    own = out_ps[v % OUTS][:, 0:2 * (P + HD)].rearrange("p (h x) -> p h x", h=2)[:, :, 0:HD]
                    dve.tensor_tensor(dst, own,
                                      rden[:, r, :].unsqueeze(2).broadcast_to([P, 2, HD]),
                                      ALU.mult).then_inc(scaled, 1)

        @block.tensor
        def _(pe):
            pe.wait_ge(const_in, 48)

            def transpose(g):
                v, items = groups[g]
                pe.wait_ge(exped, 2 * v + items[-1][0] + 1)
                if g >= BANKS:
                    e = (g - BANKS) % 2
                    pe.wait_ge(copied[e], copies(e, g - BANKS + 1))
                for h, i, rows, col in items:
                    last = nc.tensor.transpose(flip_ps[g % BANKS][0:rows, col:col + P],
                                               probs[:, (2 * v + h) % PROBS, i * P:i * P + rows], ident[:])
                last.then_inc(flipped_ps, 1)

            for u in range(N + 2):
                if u < N:
                    window, tile, key0, keys, off, pair, bi = units[u]
                    q0, k0 = tile * P, key0 * P
                    for h in range(2):
                        if u >= 1:
                            pe.wait_ge(added, 2 * (u - 1) + h + 1)
                        rows = slice(h * HD, (h + 1) * HD)
                        qc, kc = (pair, 0) if window else (QA + pair, KA + pair)
                        for c in range(0, keys, 512):
                            w = min(512, keys - c)
                            last = nc.tensor.matmul(score[h][:, c:c + w], keep.q[rows, qc, q0:q0 + P],
                                                    keep.k[rows, kc, k0 + c:k0 + c + w], start=True, stop=True)
                        last.then_inc(scored, 1)
                mine = range(first_group[u - 1], first_group[u]) if 1 <= u < N + 1 else []
                for g in mine[:BANKS]:
                    transpose(g)
                if u >= 2:
                    v = u - 2
                    window, tile, key0, keys, off, pair, bi = units[v]
                    for e in range(2):
                        pe.wait_ge(copied[e], copies(e, first_group[v + 1]))
                    if v >= OUTS:
                        pe.wait_ge(scaled, v - OUTS + 1)
                    for h in range(2):
                        products = [(i, rows, g % FLIPS, col) for g in range(first_group[v], first_group[v + 1])
                                    for hh, i, rows, col in groups[g][1] if hh == h]
                        c0 = 0 if window else P + pair * P
                        for n, (i, rows, slot, col) in enumerate(products):
                            last = nc.tensor.matmul(out_ps[v % OUTS][:, h * P:(h + 1) * P], flipped[0:rows, slot, col:col + P],
                                                    keep.v[0:rows, key0 + i, c0:c0 + P], start=n == 0,
                                                    stop=n == len(products) - 1)
                    last.then_inc(weighed, 1)
                for g in mine[BANKS:]:
                    transpose(g)


def mix(nc, d, route):
    ctx = ExitStack()
    with ctx:
        sb, ps, sem = buffers(nc, ctx)
        HALF = D // 2
        w = sb("mx_w", [P, DT, D])
        w_hi = sb("mx_w_hi", [P, DT, D], F32R)
        w_lo = sb("mx_w_lo", [P, DT, D], F32R)
        w_router = sb("mx_w_router", [P, DT, EXPERTS])
        gain_out = sb("mx_gain_out", [P, D])
        gain_ffn = sb("mx_gain_ffn", [P, D])
        ident = sb("mx_ident", [P, P])
        eps = sb("mx_eps", [P, 1])
        o = sb("mx_o", [P, 2, D])
        x = sb("mx_x", [P, 2, D])
        x2 = sb("mx_x2", [P, 2, D])
        h = sb("mx_h", [P, 2, D])
        merged = sb("mx_merged", [P, D])
        m_hi = sb("mx_m_hi", [P, 2, DT, P], F32R)
        m_lo = sb("mx_m_lo", [P, 2, DT, P], F32R)
        ht = sb("mx_ht", [P, DT, P])
        junk = sb("mx_junk", [P, D], BF16)
        ss1, rt1, rs1 = (sb(f"mx_{n}1", [P, 2]) for n in ("ss", "rt", "rs"))
        ss2, rt2, rs2 = (sb(f"mx_{n}2", [P, 1]) for n in ("ss", "rt", "rs"))
        tmp1, tmp2 = sb("mx_tmp1", [P, 3, 2]), sb("mx_tmp2", [P, 3, 1])
        neg_top, e_sum, e_inv = (sb(f"mx_{n}", [P, 1]) for n in ("neg_top", "e_sum", "e_inv"))
        e_aff, aff = sb("mx_e_aff", [P, EXPERTS]), sb("mx_aff", [P, 2, EXPERTS])
        bank = [ps(f"mx_ps{i}", [P, 512]) for i in range(8)]

        const_in = sem("mx_const_in")
        w_in = [sem(f"mx_w_in{i}") for i in range(DT)]
        ready = sem("mx_ready")
        o_in = [sem(f"mx_o_in{i}") for i in range(2)]
        x_in = [sem(f"mx_x_in{i}") for i in range(2)]
        hi_w, lo_w = sem("mx_hi_w"), sem("mx_lo_w")
        squared = sem("mx_squared")
        root1, root2 = sem("mx_root1"), sem("mx_root2")
        refined = sem("mx_refined")
        normed1, normed2 = sem("mx_normed1"), sem("mx_normed2")
        turned1, turned2 = sem("mx_turned1"), sem("mx_turned2")
        hi_m, lo_m = sem("mx_hi_m"), sem("mx_lo_m")
        projected = sem("mx_projected")
        summed = sem("mx_summed")
        ht_copied = sem("mx_ht_copied")
        routed = sem("mx_routed")
        topped, exped, inverted, shared = (sem(f"mx_{n}") for n in ("topped", "exped", "inverted", "shared"))
        aff_turned, rowed = sem("mx_aff_turned"), sem("mx_rowed")
        x2_out = [sem(f"mx_x2_out{i}") for i in range(2)]
        h_out = [sem(f"mx_h_out{i}") for i in range(2)]
        block = ctx.enter_context(nc.Block())

        @block.sync
        def _(sp):
            def load(t):
                if t >= 2:
                    sp.wait_ge(normed1, 2 * (t - 1))
                sp.dma_start(o[:, t % 2, :], d["o"][t]).then_inc(o_in[t % 2], 16)
                if t >= 2:
                    sp.wait_ge(summed, 2 * (t - 1))
                sp.dma_start(x[:, t % 2, :], d["x_tiles"][t]).then_inc(x_in[t % 2], 16)

            sp.dma_start(gain_out[:], d["g_out"]).then_inc(const_in, 16)
            sp.dma_start(ident[:], d["ident"]).then_inc(const_in, 16)
            load(0)
            for j in range(DT):
                sp.dma_start(w[:, j, :], d["w_out"][j]).then_inc(w_in[j], 16)
            sp.dma_start(gain_ffn[:], d["g_ffn"]).then_inc(const_in, 16)
            sp.dma_start(w_router[:], d["w_router"]).then_inc(const_in, 16)
            load(1)
            for t in range(TILES):
                if t + 2 < TILES:
                    load(t + 2)
                sp.wait_ge(summed, 2 * (t + 1))
                sp.dma_start(d["acc_tiles"][t], x2[:, t % 2, :]).then_inc(x2_out[t % 2], 16)
                sp.wait_ge(normed2, t + 1)
                sp.dma_start(d["h_tiles"][t], h[:, t % 2, :]).then_inc(h_out[t % 2], 16)
            for i in range(2):
                sp.wait_ge(x2_out[i], 16 * TILES // 2)
                sp.wait_ge(h_out[i], 16 * TILES // 2)

        @block.gpsimd
        def _(pool):
            pool.memset(eps[:], EPS).then_inc(ready, 1)
            pool.memset(route.rows[:, 0, :], -1.0).then_inc(ready, 1)

        @block.scalar
        def _(act):
            squares = 0

            def square(src, dst):
                nonlocal squares
                act.wait_ge(squared, squares)
                act.activation(junk[:, 0:src.shape[-1]], src, ACT.Square, accum_out=dst).then_inc(squared, 1)
                squares += 1

            act.wait_ge(ready, 2)
            for s in range(-1, TILES + 2):
                t = s - 1
                if 0 <= t < TILES:
                    act.wait_ge(summed, 2 * (t + 1))
                    square(x2[:, t % 2, :], ss2[:])
                    act.wait_ge(squared, squares)
                    act.activation(rt2[:], ss2[:], ACT.Sqrt, bias=eps[:], scale=1.0 / D).then_inc(root2, 1)
                t = s + 1
                if t < TILES:
                    act.wait_ge(o_in[t % 2], 16 * (t // 2 + 1))
                    for k in range(2):
                        square(o[:, t % 2, k * HALF:(k + 1) * HALF], ss1[:, k:k + 1])
                    act.wait_ge(squared, squares)
                    act.activation(rt1[:], ss1[:], ACT.Sqrt, bias=eps[:], scale=1.0 / HALF).then_inc(root1, 1)
                if 0 <= s - 2 < TILES:
                    act.wait_ge(topped, s - 1)
                    act.activation(e_aff[:], bank[6][:, 0:EXPERTS], ACT.Exp, bias=neg_top[:],
                                   accum_out=e_sum[:]).then_inc(exped, 1)
                if t < TILES:
                    if t == 0:
                        for j in range(DT):
                            act.wait_ge(w_in[j], 16)
                            act.activation(w_hi[:, j, :], w[:, j, :], ACT.Copy).then_inc(hi_w, 1)
                    for k in range(2):
                        act.wait_ge(turned1, 2 * t + k + 1)
                        if t >= 2:
                            act.wait_ge(projected, t - 1)
                        act.activation(m_hi[:, t % 2, 4 * k:4 * k + 4, :].rearrange("p j c -> p (j c)"),
                                       bank[k][:], ACT.Copy).then_inc(hi_m, 1)
                t = s - 1
                if 0 <= t < TILES:
                    for k in range(2):
                        act.wait_ge(turned2, 2 * t + k + 1)
                        if t >= 1:
                            act.wait_ge(routed, t)
                        act.activation(ht[:, 4 * k:4 * k + 4, :].rearrange("p j c -> p (j c)"),
                                       bank[6 + k][:], ACT.Copy).then_inc(ht_copied, 1)
                t = s - 2
                if 0 <= t < TILES:
                    act.wait_ge(aff_turned, t + 1)
                    row, col = (0, t * P) if t < S_TILES else (PROMPT_AT, (t - S_TILES) * P)
                    act.activation(route.rows[row:row + EXPERTS, 0, col:col + P], bank[7][0:EXPERTS, 0:P],
                                   ACT.Copy).then_inc(rowed, 1)

        @block.vector
        def _(dve):
            refines = 0
            dve.wait_ge(const_in, 64)
            for s in range(-1, TILES + 2):
                t = s - 1
                if 0 <= t < TILES:
                    dve.wait_ge(x_in[t % 2], 16 * (t // 2 + 1))
                    if t >= 2:
                        dve.wait_ge(x2_out[t % 2], 16 * (t // 2))
                    dve.wait_ge(projected, t + 1)
                    for k in range(2):
                        c = slice(k * HALF, (k + 1) * HALF)
                        dve.tensor_tensor(x2[:, t % 2, c], bank[2 + 2 * (t % 2) + k][:], x[:, t % 2, c],
                                          ALU.add).then_inc(summed, 1)
                if 0 <= s - 2 < TILES:
                    dve.wait_ge(routed, s - 1)
                    dve.tensor_reduce(neg_top[:], bank[6][:, 0:EXPERTS], AX.X, ALU.max,
                                      negate=True).then_inc(topped, 1)
                if 0 <= t < TILES:
                    dve.wait_ge(root2, t + 1)
                    inverse_root(dve, refined, refines, ss2[:], rt2[:], [tmp2[:, i, :] for i in range(3)],
                                 rs2[:], 1.0 / D)
                    refines += REFINE
                    if t >= 2:
                        dve.wait_ge(h_out[t % 2], 16 * (t // 2))
                        dve.wait_ge(turned2, 2 * (t - 1))
                    dve.scalar_tensor_tensor(out=h[:, t % 2, :], in0=x2[:, t % 2, :], scalar=rs2[:],
                                             in1=gain_ffn[:], op0=ALU.mult, op1=ALU.mult).then_inc(normed2, 1)
                t = s + 1
                if t < TILES:
                    dve.wait_ge(root1, t + 1)
                    inverse_root(dve, refined, refines, ss1[:], rt1[:], [tmp1[:, i, :] for i in range(3)],
                                 rs1[:], 1.0 / HALF)
                    refines += REFINE
                    for k in range(2):
                        c = slice(k * HALF, (k + 1) * HALF)
                        dve.wait_ge(turned1, 2 * t)
                        dve.scalar_tensor_tensor(out=merged[:, c], in0=o[:, t % 2, c], scalar=rs1[:, k:k + 1],
                                                 in1=gain_out[:, c], op0=ALU.mult,
                                                 op1=ALU.mult).then_inc(normed1, 1)
                    if t == 0:
                        for j in range(DT):
                            dve.wait_ge(hi_w, j + 1)
                            dve.tensor_tensor(w_lo[:, j, :], w[:, j, :], w_hi[:, j, :].bitcast(F32),
                                              ALU.subtract).then_inc(lo_w, 1)
                    for k in range(2):
                        dve.wait_ge(hi_m, 2 * t + k + 1)
                        jj = slice(4 * k, 4 * k + 4)
                        dve.tensor_tensor(m_lo[:, t % 2, jj, :].rearrange("p j c -> p (j c)"), bank[k][:],
                                          m_hi[:, t % 2, jj, :].rearrange("p j c -> p (j c)").bitcast(F32),
                                          ALU.subtract).then_inc(lo_m, 1)
                t = s - 2
                if 0 <= t < TILES:
                    dve.wait_ge(exped, t + 1)
                    dve.reciprocal(e_inv[:], e_sum[:]).then_inc(inverted, 1)
                    dve.wait_ge(inverted, t + 1)
                    if t >= 2:
                        dve.wait_ge(aff_turned, t - 1)
                    dve.tensor_scalar(aff[:, t % 2, :], e_aff[:], e_inv[:], None, ALU.mult).then_inc(shared, 1)

        @block.tensor
        def _(pe):
            pe.wait_ge(const_in, 64)
            for s in range(-1, TILES + 2):
                t = s
                if 0 <= t < TILES:
                    pe.wait_ge(lo_m, 2 * (t + 1))
                    if t >= 2:
                        pe.wait_ge(summed, 2 * (t - 1))
                    for k in range(2):
                        c = slice(k * HALF, (k + 1) * HALF)
                        for j in range(DT):
                            pe.wait_ge(lo_w, j + 1)
                            last = three_pass(nc, bank[2 + 2 * (t % 2) + k][:], (m_hi[:, t % 2, j, :], m_lo[:, t % 2, j, :]),
                                              (w_hi[:, j, c], w_lo[:, j, c]), j == 0, j == DT - 1)
                    last.then_inc(projected, 1)
                t = s + 1
                if t < TILES:
                    for k in range(2):
                        pe.wait_ge(normed1, 2 * t + k + 1)
                        if t >= 1:
                            pe.wait_ge(lo_m, 2 * (t - 1) + k + 1)
                        for j in range(4):
                            c0 = (4 * k + j) * P
                            last = nc.tensor.transpose(bank[k][:, j * P:(j + 1) * P], merged[:, c0:c0 + P],
                                                       ident[:])
                        last.then_inc(turned1, 1)
                t = s - 1
                if 0 <= t < TILES:
                    pe.wait_ge(normed2, t + 1)
                    for k in range(2):
                        if t >= 1 and k == 0:
                            pe.wait_ge(exped, t)
                        if t >= 2 and k == 1:
                            pe.wait_ge(rowed, t - 1)
                        for j in range(4):
                            c0 = (4 * k + j) * P
                            last = nc.tensor.transpose(bank[6 + k][:, j * P:(j + 1) * P], h[:, t % 2, c0:c0 + P],
                                                       ident[:])
                        last.then_inc(turned2, 1)
                    pe.wait_ge(ht_copied, 2 * (t + 1))
                    for j in range(DT):
                        last = nc.tensor.matmul(bank[6][:, 0:EXPERTS], ht[:, j, :], w_router[:, j, :],
                                                start=j == 0, stop=j == DT - 1)
                    last.then_inc(routed, 1)
                t = s - 2
                if 0 <= t < TILES:
                    pe.wait_ge(shared, t + 1)
                    if t >= 1:
                        pe.wait_ge(rowed, t)
                    nc.tensor.transpose(bank[7][0:EXPERTS, 0:P], aff[:, t % 2, :],
                                        ident[:]).then_inc(aff_turned, 1)


def choose(nc, d, route):
    ctx = ExitStack()
    with ctx:
        sb, ps, sem = buffers(nc, ctx)
        ROWS = PROMPT_AT + EXPERTS
        best = sb("ch_best", [ROWS, S_CAP])
        at = sb("ch_at", [ROWS, S_CAP], U32)
        at_f = sb("ch_at_f", [ROWS, S_CAP])
        ident = sb("ch_ident", [P, P])
        bank = [ps(f"ch_ps{i}", [P, 512]) for i in range(2)]
        const_in = sem("ch_const_in")
        found, placed, dropped = sem("ch_found"), sem("ch_placed"), sem("ch_dropped")
        floated, turned, done = sem("ch_floated"), sem("ch_turned"), sem("ch_done")
        block = ctx.enter_context(nc.Block())

        @block.sync
        def _(sp):
            sp.dma_start(ident[:], d["ident"]).then_inc(const_in, 16)

        @block.vector
        def _(dve):
            for r in range(S_CAP // 8):
                rows, other = route.rows[:, r % 2, :], route.rows[:, 1 - r % 2, :]
                c = slice(8 * r, 8 * r + 8)
                dve.wait_ge(dropped, r)
                dve.max(best[:, c], rows).then_inc(found, 1)
                dve.wait_ge(found, r + 1)
                dve.max_index(at[:, c], best[:, c], rows).then_inc(placed, 1)
                dve.match_replace(other, best[:, c], rows, -2.0).then_inc(dropped, 1)
            dve.wait_ge(placed, S_CAP // 8)
            dve.tensor_copy(at_f[:], at[:]).then_inc(floated, 1)
            dve.wait_ge(turned, 2)
            dve.tensor_copy(route.gates[:, 0, :], bank[0][:, 0:EXPERTS]).then_inc(done, 1)
            dve.tensor_copy(route.gates[:, 1, :], bank[0][:, PROMPT_AT:ROWS]).then_inc(done, 1)
            dve.tensor_copy(route.index[:, 0, 0:EXPERTS], bank[1][:, 0:EXPERTS]).then_inc(done, 1)
            dve.tensor_copy(route.index[:, 0, EXPERTS:], bank[1][:, 0:1]).then_inc(done, 1)
            dve.tensor_scalar(route.index[:, 1, 0:EXPERTS], bank[1][:, PROMPT_AT:ROWS], float(S_TOK), None,
                              ALU.add).then_inc(done, 1)
            dve.tensor_scalar(route.index[:, 1, EXPERTS:], bank[1][:, PROMPT_AT:PROMPT_AT + 1], float(S_TOK),
                              None, ALU.add).then_inc(done, 1)

        @block.tensor
        def _(pe):
            pe.wait_ge(const_in, 16)
            pe.wait_ge(found, S_CAP // 8)
            nc.tensor.transpose(bank[0][:, 0:ROWS], best[:], ident[0:ROWS, 0:ROWS]).then_inc(turned, 1)
            pe.wait_ge(floated, 1)
            nc.tensor.transpose(bank[1][:, 0:ROWS], at_f[:], ident[0:ROWS, 0:ROWS]).then_inc(turned, 1)


WIDE = 512
QUARTERS = DF // WIDE
HALVES = D // WIDE
ROWS4 = 4
W_COLS = ROWS4 * WIDE
UP_CHUNKS = 4 * QUARTERS
W_CHUNKS = UP_CHUNKS + HALVES * FT // ROWS4


def experts(nc, d, route):
    ctx = ExitStack()
    with ctx:
        sb, ps, sem = buffers(nc, ctx)
        SLOTS, AHEAD = 4, 3
        w = sb("ex_w", [P, SLOTS, W_COLS])
        w_hi = sb("ex_w_hi", [P, SLOTS, W_COLS], F32R)
        w_lo = sb("ex_w_lo", [P, SLOTS, W_COLS], F32R)
        ident = sb("ex_ident", [P, P])
        x_s = sb("ex_x_s", [S_CAP, D])
        x_p = sb("ex_x_p", [P_CAP, D])
        xs_hi = sb("ex_xs_hi", [P, DT, S_CAP], F32R)
        xs_lo = sb("ex_xs_lo", [P, DT, S_CAP], F32R)
        xp = sb("ex_xp", [P, DT, 2, P_CAP], F32R)
        silu_s = sb("ex_silu_s", [S_CAP, WIDE])
        silu_p = sb("ex_silu_p", [P_CAP, WIDE])
        gate_low = sb("ex_gate_low", [P_CAP, WIDE])
        gate_p_sum = sb("ex_gate_p_sum", [P_CAP, WIDE])
        up_low = sb("ex_up_low", [P_CAP, WIDE])
        up_p_sum = sb("ex_up_p_sum", [P_CAP, WIDE])
        hid_s = sb("ex_hid_s", [S_CAP, WIDE])
        hid_p = sb("ex_hid_p", [P_CAP, WIDE])
        hs_hi = sb("ex_hs_hi", [P, FT, S_CAP], F32R)
        hs_lo = sb("ex_hs_lo", [P, FT, S_CAP], F32R)
        hp = sb("ex_hp", [P, FT, 2, P_CAP], F32R)
        y_low = sb("ex_y_low", [P_CAP, WIDE])
        y_p_sum = sb("ex_y_p_sum", [P_CAP, WIDE])
        y_s = sb("ex_y_s", [S_CAP, D])
        y_p = sb("ex_y_p", [P_CAP, D])
        gather_s = sb("ex_gather_s", [S_CAP, 1], U32)
        gather_p = sb("ex_gather_p", [P_CAP, 1], U32)
        scatter_s = sb("ex_scatter_s", [S_CAP, 1], U32)
        scatter_p = sb("ex_scatter_p", [P_CAP, 1], U32)
        gate_s = sb("ex_gate_s", [S_CAP, 1])
        gate_p = sb("ex_gate_p", [P_CAP, 1])
        gate_ps = [ps(f"ex_gate_ps{i}", [P, WIDE]) for i in range(2)]
        up_ps = [ps(f"ex_up_ps{i}", [P, WIDE]) for i in range(2)]
        down_ps = [ps(f"ex_down_ps{i}", [P, WIDE]) for i in range(2)]
        turn_ps = [ps(f"ex_turn_ps{i}", [P, WIDE]) for i in range(2)]
        y_ps = [down_ps, up_ps]

        const_in = sem("ex_const_in")
        w_in = [sem(f"ex_w_in{i}") for i in range(SLOTS)]
        hi_w = sem("ex_hi_w")
        lo_w = sem("ex_lo_w")
        chunk_done = sem("ex_chunk_done")
        gated_s, gate_lowered, gate_summed, gated_p = (
            sem(f"ex_{n}") for n in ("gated_s", "gate_lowered", "gate_summed", "gated_p"))
        hidden_s, up_lowered, up_summed, hidden_p = (
            sem(f"ex_{n}") for n in ("hidden_s", "up_lowered", "up_summed", "hidden_p"))
        h_turned, hi_h, lo_h = sem("ex_h_turned"), sem("ex_hi_h"), sem("ex_lo_h")
        x_turned, hi_x, lo_x = sem("ex_x_turned"), sem("ex_hi_x"), sem("ex_lo_x")
        y_lowered = sem("ex_y_lowered")
        y_summed = sem("ex_y_summed")
        s_scaled = sem("ex_s_scaled")
        p_scaled = sem("ex_p_scaled")
        columns = sem("ex_columns")
        y_free = sem("ex_y_free")
        released = sem("ex_released")
        pe_released = sem("ex_pe_released")
        gathered = sem("ex_gathered")
        scattered_s, scattered_p = sem("ex_scattered_s"), sem("ex_scattered_p")
        block = ctx.enter_context(nc.Block())
        FILLS = 3
        COPIES, FIRST_COPIES = 6, 2

        @block.sync
        def _(sp):
            sp.dma_start(ident[:], d["ident"]).then_inc(const_in, 16)
            with sp.Fori(0, EXPERTS) as e:
                for c in range(W_CHUNKS):
                    sp.wait_ge(lo_w, e * W_CHUNKS + c + 1)
                    sp.dma_start(w[:, c % SLOTS, :], d["w_experts"][e, c]).then_inc(w_in[c % SLOTS], 16)
            for c in range(AHEAD):
                sp.wait_ge(lo_w, EXPERTS * W_CHUNKS + c + 1)
                sp.dma_start(w[:, c % SLOTS, :], d["w_experts"][0, c]).then_inc(w_in[c % SLOTS], 16)

        @block.gpsimd
        def _(pool):
            def gather(e, copied):
                pool.tensor_copy(gather_s[:], route.index[:, 0, bass.ds(e, 1)]).then_inc(columns, 1)
                pool.tensor_copy(gather_p[:], route.index[0:P_CAP, 1, bass.ds(e, 1)]).then_inc(columns, 1)
                pool.wait_ge(columns, copied)
                pool.sem_inc(released, 1)
                for dst, at in ((x_s, gather_s), (x_p, gather_p)):
                    pool.indirect_dma_start(dst[:], None, d["h"],
                                            bass.IndirectOffsetOnAxis(at[:, 0:1], 0)).then_inc(gathered, 16)

            pool.sem_inc(y_free, START)
            gather(0, FIRST_COPIES)
            with pool.Fori(0, EXPERTS) as e:
                pool.wait_ge(x_turned, (e + 1) * FILLS)
                pool.wait_ge(gathered, (e + 1) * 32)
                gather(e + 1, FIRST_COPIES + e * COPIES + 2)
                pool.tensor_copy(scatter_s[:], route.index[:, 0, bass.ds(e, 1)]).then_inc(columns, 1)
                pool.tensor_copy(scatter_p[:], route.index[0:P_CAP, 1, bass.ds(e, 1)]).then_inc(columns, 1)
                pool.tensor_copy(gate_s[:], route.gates[:, 0, bass.ds(e, 1)]).then_inc(columns, 1)
                pool.tensor_copy(gate_p[:], route.gates[0:P_CAP, 1, bass.ds(e, 1)]).then_inc(columns, 1)
                pool.wait_ge(columns, FIRST_COPIES + (e + 1) * COPIES)
                pool.wait_ge(s_scaled, e * HALVES + HALVES + START)
                pool.sem_inc(released, 1)
                pool.indirect_dma_start(d["acc"], bass.IndirectOffsetOnAxis(scatter_s[:, 0:1], 0), y_s[:],
                                        None, compute_op=ALU.add).then_inc(scattered_s, 16)
                pool.wait_ge(p_scaled, (e + 1) * HALVES)
                pool.sem_inc(released, 1)
                pool.indirect_dma_start(d["acc"], bass.IndirectOffsetOnAxis(scatter_p[:, 0:1], 0), y_p[:],
                                        None, compute_op=ALU.add).then_inc(scattered_p, 16)
                pool.wait_ge(scattered_s, (e + 1) * 16)
                pool.wait_ge(scattered_p, (e + 1) * 16)
                pool.sem_inc(y_free, 1)
            pool.wait_ge(gathered, (EXPERTS + 1) * 32)

        GATE_STEP = [4 * q + 2 for q in range(QUARTERS)]
        UP_STEP = [4 * q + 4 for q in range(QUARTERS)]
        TURN_CHUNK = [4 * q + 5 for q in range(QUARTERS - 1)] + [UP_CHUNKS]
        X_CHUNK = [UP_CHUNKS + 2, UP_CHUNKS + 2, UP_CHUNKS + 4]
        DOWN_STEP = [UP_CHUNKS + 4, W_CHUNKS]

        def x_parts(i):
            if i < 2:
                j = slice(4 * i, 4 * i + 4)
                return (turn_ps[i][:].rearrange("p (j c) -> p j c", j=4), xs_hi[:, j, :], xs_lo[:, j, :])
            return turn_ps[0][:].rearrange("p (j c) -> p j c", j=DT), xp[:, :, 0, :], xp[:, :, 1, :]

        def h_parts(q, group):
            j = slice(4 * q, 4 * q + 4)
            if group == 0:
                return turn_ps[0][:].rearrange("p (j c) -> p j c", j=4), hs_hi[:, j, :], hs_lo[:, j, :]
            return (turn_ps[1][:, 0:4 * P_CAP].rearrange("p (j c) -> p j c", j=4), hp[:, j, 0, :], hp[:, j, 1, :])

        @block.scalar
        def _(act):
            def split(n0, c):
                act.wait_ge(w_in[c % SLOTS], n0 * (16 // SLOTS) + 16 * (c // SLOTS + 1))
                act.activation(w_hi[:, c % SLOTS, :], w[:, c % SLOTS, :], ACT.Copy).then_inc(hi_w, 1)

            def high_x(fills, i):
                src, hi, _ = x_parts(i)
                act.wait_ge(x_turned, fills + i + 1)
                act.activation(hi, src, ACT.Copy).then_inc(hi_x, 1)

            for c in range(AHEAD):
                split(0, c)
            for i in range(FILLS):
                high_x(0, i)
            with act.Fori(0, EXPERTS) as e:
                quarters, halves = e * QUARTERS, e * HALVES

                for c in range(W_CHUNKS + 1):
                    act.wait_ge(chunk_done, e * W_CHUNKS + c + START)
                    if c in GATE_STEP:
                        q = GATE_STEP.index(c)
                        if q:
                            act.wait_ge(hidden_s, quarters + q)
                        act.activation(silu_s[:], gate_ps[0][:], ACT.Silu).then_inc(gated_s, 1)
                        act.activation(gate_low[:], gate_ps[1][P_CAP:P, :], ACT.Copy).then_inc(gate_lowered, 1)
                    if c in UP_STEP:
                        act.activation(up_low[:], up_ps[1][P_CAP:P, :], ACT.Copy).then_inc(up_lowered, 1)
                    if c in DOWN_STEP:
                        k = DOWN_STEP.index(c)
                        if k == 0:
                            act.wait_ge(columns, FIRST_COPIES + (e + 1) * COPIES)
                            act.wait_ge(y_free, e + START)
                        else:
                            act.wait_ge(y_summed, halves + k + START)
                        act.activation(y_low[:], y_ps[k][1][P_CAP:P, :], ACT.Copy).then_inc(y_lowered, 1)
                        act.activation(y_s[:, k * WIDE:(k + 1) * WIDE], y_ps[k][0][:], ACT.Copy,
                                       scale=gate_s[:, 0:1]).then_inc(s_scaled, 1)
                    if c < W_CHUNKS:
                        split(e * W_CHUNKS, c + AHEAD)
                    if c in GATE_STEP:
                        q = GATE_STEP.index(c)
                        if q:
                            act.wait_ge(hidden_p, quarters + q)
                        act.wait_ge(gate_summed, quarters + q + 1)
                        act.activation(silu_p[:], gate_p_sum[:], ACT.Silu).then_inc(gated_p, 1)
                    if c - 1 in TURN_CHUNK:
                        q = TURN_CHUNK.index(c - 1)
                        for group in range(2):
                            src, hi, _ = h_parts(q, group)
                            act.wait_ge(h_turned, quarters * 2 + 2 * q + group + 1)
                            act.activation(hi, src, ACT.Copy).then_inc(hi_h, 1)
                    for i in range(FILLS):
                        if X_CHUNK[i] == c - 1:
                            high_x((e + 1) * FILLS, i)

        @block.vector
        def _(dve):
            def split(n0, c):
                dve.wait_ge(hi_w, n0 + c + 1)
                dve.tensor_tensor(w_lo[:, c % SLOTS, :], w[:, c % SLOTS, :], w_hi[:, c % SLOTS, :].bitcast(F32),
                                  ALU.subtract).then_inc(lo_w, 1)

            def low_x(fills, i):
                src, hi, lo = x_parts(i)
                dve.wait_ge(hi_x, fills + i + 1)
                dve.tensor_tensor(lo, src, hi.bitcast(F32), ALU.subtract).then_inc(lo_x, 1)

            dve.sem_inc(lo_w, SLOTS)
            for c in range(AHEAD):
                split(0, c)
            for i in range(FILLS):
                low_x(0, i)
            with dve.Fori(0, EXPERTS) as e:
                quarters, halves = e * QUARTERS, e * HALVES

                for c in range(W_CHUNKS + 1):
                    if c in GATE_STEP:
                        q = GATE_STEP.index(c)
                        dve.wait_ge(gate_lowered, quarters + q + 1)
                        dve.tensor_tensor(gate_p_sum[:], gate_ps[1][0:P_CAP, :], gate_low[:],
                                          ALU.add).then_inc(gate_summed, 1)
                    if c in UP_STEP:
                        q = UP_STEP.index(c)
                        dve.wait_ge(chunk_done, e * W_CHUNKS + c + START)
                        dve.wait_ge(gated_s, quarters + q + 1)
                        dve.tensor_tensor(hid_s[:], up_ps[0][:], silu_s[:], ALU.mult).then_inc(hidden_s, 1)
                        dve.wait_ge(up_lowered, quarters + q + 1)
                        dve.tensor_tensor(up_p_sum[:], up_ps[1][0:P_CAP, :], up_low[:],
                                          ALU.add).then_inc(up_summed, 1)
                        dve.wait_ge(up_summed, quarters + q + 1)
                        dve.wait_ge(gated_p, quarters + q + 1)
                        dve.tensor_tensor(hid_p[:], up_p_sum[:], silu_p[:], ALU.mult).then_inc(hidden_p, 1)
                    if c in DOWN_STEP:
                        k = DOWN_STEP.index(c)
                        dve.wait_ge(y_lowered, halves + k + 1)
                        dve.tensor_tensor(y_p_sum[:], y_ps[k][1][0:P_CAP, :], y_low[:],
                                          ALU.add).then_inc(y_summed, 1)
                        dve.wait_ge(y_summed, halves + k + 1 + START)
                        if k == 0:
                            dve.wait_ge(columns, FIRST_COPIES + (e + 1) * COPIES)
                            dve.wait_ge(y_free, e + START)
                        dve.tensor_scalar(y_p[:, k * WIDE:(k + 1) * WIDE], y_p_sum[:], gate_p[:, 0:1], None,
                                          ALU.mult).then_inc(p_scaled, 1)
                    if c < W_CHUNKS:
                        split(e * W_CHUNKS, c + AHEAD)
                    if c - 1 in TURN_CHUNK:
                        q = TURN_CHUNK.index(c - 1)
                        for group in range(2):
                            src, hi, lo = h_parts(q, group)
                            dve.wait_ge(hi_h, quarters * 2 + 2 * q + group + 1)
                            dve.tensor_tensor(lo, src, hi.bitcast(F32), ALU.subtract).then_inc(lo_h, 1)
                    for i in range(FILLS):
                        if X_CHUNK[i] == c - 1:
                            low_x((e + 1) * FILLS, i)

        @block.tensor
        def _(pe):
            def turn_x(i):
                for j in range(DT if i == 2 else 4):
                    c = slice((4 * (i % 2) + j) * P, (4 * (i % 2) + j + 1) * P)
                    if i < 2:
                        last = nc.tensor.transpose(turn_ps[i][:, j * P:(j + 1) * P], x_s[:, c], ident[:])
                    else:
                        last = nc.tensor.transpose(turn_ps[0][:, j * P_CAP:(j + 1) * P_CAP], x_p[:, c],
                                                   ident[0:P_CAP, 0:P_CAP])
                last.then_inc(x_turned, 1)

            pe.wait_ge(const_in, 16)
            pe.sem_inc(chunk_done, START)
            pe.sem_inc(s_scaled, START)
            pe.sem_inc(y_summed, START)
            pe.wait_ge(gathered, 32)
            turn_x(0)
            turn_x(1)
            pe.wait_ge(lo_x, 1)
            turn_x(2)
            with pe.Fori(0, EXPERTS) as e:
                quarters, halves = e * QUARTERS, e * HALVES

                def multiply(c, out, sample, prompt, first_row, rows):
                    slot = c % SLOTS
                    for r in range(ROWS4):
                        n = first_row + r
                        hi, lo = (x[:, slot, r * WIDE:(r + 1) * WIDE] for x in (w_hi, w_lo))
                        s_hi, s_lo = (x[:, n, :] for x in sample)
                        both = prompt[:, n, :, :].rearrange("p k c -> p (k c)")
                        start, stop = n == 0, n == rows - 1
                        nc.tensor.matmul(out[0][:], s_hi, hi, start=start, stop=False)
                        nc.tensor.matmul(out[0][:], s_hi, lo, start=False, stop=False)
                        nc.tensor.matmul(out[0][:], s_lo, hi, start=False, stop=stop)
                        nc.tensor.matmul(out[1][:], both, hi, start=start, stop=False)
                        last = nc.tensor.matmul(out[1][:], both, lo, start=False, stop=stop)
                    last.then_inc(chunk_done, 1)

                pe.wait_ge(lo_x, (e + 1) * FILLS)
                for c in range(W_CHUNKS):
                    pe.wait_ge(lo_w, e * W_CHUNKS + c + 1 + SLOTS)
                    if c < UP_CHUNKS:
                        q, kind, half = c // 4, c // 2 % 2, c % 2
                        if half == 0 and q and kind == 0:
                            pe.wait_ge(gated_s, quarters + q)
                            pe.wait_ge(gate_summed, quarters + q)
                        elif half == 0 and q:
                            pe.wait_ge(hidden_s, quarters + q)
                            pe.wait_ge(up_summed, quarters + q)
                        elif half == 0 and kind:
                            pe.wait_ge(s_scaled, halves + START)
                            pe.wait_ge(y_summed, halves + START)
                        multiply(c, up_ps if kind else gate_ps, (xs_hi, xs_lo), xp, ROWS4 * half, DT)
                    else:
                        k, part = divmod(c - UP_CHUNKS, FT // ROWS4)
                        if k == 0:
                            pe.wait_ge(lo_h, quarters * 2 + 2 * (part + 1))
                        multiply(c, y_ps[k], (hs_hi, hs_lo), hp, ROWS4 * part, FT)
                    if c in TURN_CHUNK:
                        q = TURN_CHUNK.index(c)
                        pe.wait_ge(hidden_p, quarters + q + 1)
                        if q:
                            pe.wait_ge(lo_h, quarters * 2 + 2 * q)
                        for group, (hid, rows) in enumerate(((hid_s, S_CAP), (hid_p, P_CAP))):
                            for j in range(4):
                                last = nc.tensor.transpose(turn_ps[group][:, j * rows:(j + 1) * rows],
                                                           hid[:, j * P:(j + 1) * P], ident[0:rows, 0:rows])
                            last.then_inc(h_turned, 1)
                    if c == X_CHUNK[0]:
                        pe.wait_ge(gathered, (e + 2) * 32)
                        pe.wait_ge(lo_h, quarters * 2 + 2 * QUARTERS)
                        turn_x(0)
                        turn_x(1)
                    if c == X_CHUNK[2]:
                        pe.wait_ge(lo_x, (e + 1) * FILLS + 1)
                        pe.sem_inc(pe_released, 1)
                        turn_x(2)


def finish(nc, d):
    ctx = ExitStack()
    with ctx:
        sb, ps, sem = buffers(nc, ctx)
        gain = sb("fi_gain", [P, D])
        eps = sb("fi_eps", [P, 1])
        x = sb("fi_x", [P, G_TILES, D])
        out = sb("fi_out", [P, G_TILES, D])
        junk = sb("fi_junk", [P, D], BF16)
        ss, rt, rs = (sb(f"fi_{n}", [P, G_TILES]) for n in ("ss", "rt", "rs"))
        tmp = sb("fi_tmp", [P, 3])
        const_in, eps_set = sem("fi_const_in"), sem("fi_eps_set")
        x_in = [sem(f"fi_x_in{i}") for i in range(G_TILES)]
        stored = [sem(f"fi_stored{i}") for i in range(G_TILES)]
        squared, root, refined = sem("fi_squared"), sem("fi_root"), sem("fi_refined")
        normed = sem("fi_normed")
        block = ctx.enter_context(nc.Block())

        @block.sync
        def _(sp):
            sp.dma_start(gain[:], d["g_final"]).then_inc(const_in, 16)
            with sp.Fori(0, GROUPS) as g:
                for t in range(G_TILES):
                    sp.wait_ge(normed, g * G_TILES + t + 1)
                    sp.dma_start(x[:, t, :], d["acc_groups"][g, t]).then_inc(x_in[t], 16)
                for t in range(G_TILES):
                    sp.wait_ge(normed, (g + 1) * G_TILES + t + 1)
                    sp.dma_start(d["out_groups"][g, t], out[:, t, :]).then_inc(stored[t], 16)
            for t in range(G_TILES):
                sp.wait_ge(stored[t], 16 * GROUPS + START)

        @block.gpsimd
        def _(pool):
            pool.memset(eps[:], EPS).then_inc(eps_set, 1)

        @block.scalar
        def _(act):
            act.wait_ge(eps_set, 1)
            act.sem_inc(squared, START)
            with act.Fori(0, GROUPS) as g:
                for t in range(G_TILES):
                    act.wait_ge(x_in[t], g * 16 + 16)
                    act.wait_ge(squared, g * G_TILES + t + START)
                    act.activation(junk[:], x[:, t, :], ACT.Square, accum_out=ss[:, t:t + 1]).then_inc(squared, 1)
                    act.wait_ge(squared, g * G_TILES + t + 1 + START)
                    act.activation(rt[:, t:t + 1], ss[:, t:t + 1], ACT.Sqrt, bias=eps[:],
                                   scale=1.0 / D).then_inc(root, 1)

        @block.vector
        def _(dve):
            dve.sem_inc(normed, G_TILES)
            for t in range(G_TILES):
                dve.sem_inc(stored[t], START)
            dve.wait_ge(const_in, 16)
            with dve.Fori(0, GROUPS) as g:
                for t in range(G_TILES):
                    dve.wait_ge(root, g * G_TILES + t + 1)
                    inverse_root(dve, refined, (g * G_TILES + t) * REFINE, ss[:, t:t + 1], rt[:, t:t + 1],
                                 [tmp[:, i:i + 1] for i in range(3)], rs[:, t:t + 1], 1.0 / D)
                    dve.wait_ge(stored[t], g * 16 + START)
                    dve.scalar_tensor_tensor(out=out[:, t, :], in0=x[:, t, :], scalar=rs[:, t:t + 1],
                                             in1=gain[:], op0=ALU.mult, op1=ALU.mult).then_inc(normed, 1)


def program(nc, d):
    d["o"] = nc.dram_tensor("o_scratch", [TILES, P, D], F32, kind="Internal").ap()
    d["h"] = nc.dram_tensor("h_scratch", [TOK, D], F32, kind="Internal").ap()
    d["acc"] = nc.dram_tensor("acc_scratch", [TOK, D], F32, kind="Internal").ap()
    d["x_tiles"] = d["x"].rearrange("g t p e -> (g t) p e")
    d["h_tiles"] = d["h"].rearrange("(t p) e -> t p e", p=P)
    d["acc_tiles"] = d["acc"].rearrange("(t p) e -> t p e", p=P)
    d["acc_groups"] = d["acc"].rearrange("(g t p) e -> g t p e", p=P, t=G_TILES)
    d["out_groups"] = d["out"].rearrange("(g t p) e -> g t p e", p=P, t=G_TILES)
    with ExitStack() as outer:
        sb, _, _ = buffers(nc, outer)
        keep = Heads(
            q=sb("q", [P, QA + QB, TOK]),
            k=sb("k", [P, KA + KB, TOK]),
            v=sb("v", [P, TILES, V_CHUNKS * P]),
        )
        project(nc, d, keep)
        attend(nc, d, keep)
    with ExitStack() as outer:
        sb, _, _ = buffers(nc, outer)
        route = Route(
            rows=sb("rows", [PROMPT_AT + EXPERTS, 2, S_TOK]),
            gates=sb("gates", [P, 2, EXPERTS]),
            index=sb("index", [P, 2, EXPERTS + 1], U32),
        )
        mix(nc, d, route)
        choose(nc, d, route)
        experts(nc, d, route)
    finish(nc, d)


def columns():
    qa0, ka0, va0 = 0, 512, 640
    qb0, kb0, vb0 = 768, 1280, 1792
    span = lambda a, n=P: list(range(a, a + n))
    out = [span(qa0 + HD * c, HD) + span(qa0 + HD * (c + 4), HD) for c in range(QA)]
    out += [span(ka0)]
    out += [span(qb0 + P * c) for c in range(QB)] + [span(kb0 + P * c) for c in range(KB)]
    out += [span(va0)] + [span(vb0 + P * c) for c in range(V_CHUNKS - 1)]
    return np.array(out)


def constants():
    c = {}
    inv = np.float32(500000.0) ** (-(np.arange(ROT_HALF, dtype=np.float32) * np.float32(2.0))
                                   / np.float32(2 * ROT_HALF))
    ang = (np.arange(S_TOK, dtype=np.float32)[:, None] * inv[None, :]).astype(np.float32)
    cos = np.ones((P, S_TOK), np.float32)
    sin = np.zeros((P, S_TOK), np.float32)
    rot = np.zeros((P, P), np.float32)
    for p in range(P):
        dd = p % HD
        if dd < 2 * ROT_HALF:
            cos[p] = np.cos(ang[:, dd % ROT_HALF])
            sin[p] = np.sin(ang[:, dd % ROT_HALF])
            if dd < ROT_HALF:
                rot[p + ROT_HALF, p] = -1.0
            else:
                rot[p - ROT_HALF, p] = 1.0
    c["cos"] = np.stack([cos[:, 0:512], cos[:, 512:1024], cos[:, 0:512]])
    c["sin"] = np.stack([sin[:, 0:512], sin[:, 512:1024], sin[:, 0:512]])
    c["rot"] = rot
    i, j = np.arange(P)[:, None], np.arange(3 * P)[None, :]
    c["band"] = np.where(np.abs(j - P - i) <= P, 0.0, NEG).astype(np.float32)
    qc, kc = np.arange(P)[:, None] % GRID_W, np.arange(GRID_W)[None, :]
    cs = np.clip(qc - 8, 0, GRID_W - 16)
    c["col_mask"] = np.where((kc >= cs) & (kc < cs + 16), 0.0, NEG).astype(np.float32)
    row_mask = np.zeros((P, NEAR_ROWS, GRID_W), np.float32)
    row_mask[GRID_W:, 0] = NEG
    row_mask[:GRID_W, NEAR_ROWS - 1] = NEG
    c["row_mask"] = row_mask.reshape(P, NEAR_KEYS)
    c["ident"] = np.eye(P, dtype=np.float32)
    return c


def layouts(i):
    a = {}
    x = np.concatenate([i["x_sample"][0], i["x_prompt"][0]])
    a["x"] = x.reshape(GROUPS, G_TILES, P, D)
    w = i["w_in"][0].reshape(DT, P, -1)[:, :, columns()]
    a["w_in"] = w.transpose(2, 1, 0, 3).reshape(CHUNKS, P, D)
    pad = np.pad(i["rpb_b"][0], ((0, 0), (0, 0), (GRID_W - 16, GRID_W - 16)))
    a["rpb"] = np.stack([pad[:, :, GRID_W - 1 - c:2 * GRID_W - 1 - c] for c in range(GRID_W)])
    order = [h for c in range(PAIRS) for h in (c, c + PAIRS)]
    a["sink"] = np.broadcast_to(i["sink_a"][0][order], (P, 2 * PAIRS))
    a["w_out"] = i["w_out"][0].reshape(DT, P, D)
    a["w_router"] = i["w_router"][0].reshape(DT, P, EXPERTS).transpose(1, 0, 2)
    up = np.stack([i["w_gate"][0], i["w_up"][0]], axis=1)
    up = up.reshape(EXPERTS, 2, 2, ROWS4, P, QUARTERS, WIDE).transpose(0, 5, 1, 2, 4, 3, 6)
    down = i["w_down"][0].reshape(EXPERTS, FT // ROWS4, ROWS4, P, HALVES, WIDE).transpose(0, 4, 1, 3, 2, 5)
    a["w_experts"] = np.concatenate([up.reshape(EXPERTS, UP_CHUNKS, P, W_COLS),
                                     down.reshape(EXPERTS, W_CHUNKS - UP_CHUNKS, P, W_COLS)], axis=1)
    a["g_out"] = np.broadcast_to(np.concatenate([i["g_out_a"][0], i["g_out_b"][0]]), (P, D))
    a["g_ffn"] = np.broadcast_to(i["g_ffn"][0], (P, D))
    a["g_final"] = np.broadcast_to(i["g_final"], (P, D))
    a["g_attn"] = np.broadcast_to(i["g_attn"][0], (P, D))
    return a


def kernel(**inputs):
    import concourse.bacc as bacc
    from concourse.bass_utils import run_bass_kernel_spmd

    given = {name: np.asarray(value) for name, value in inputs.items()}
    arrays = {**layouts(given), **constants()}
    nc = bacc.Bacc("TRN2", target_bir_lowering=False, num_devices=1)
    feeds, d = {}, {}
    for name, value in arrays.items():
        value = np.ascontiguousarray(value)
        feeds[f"in_{name}"] = value
        d[name] = nc.dram_tensor(f"in_{name}", value.shape, mybir.dt.from_np(value.dtype),
                                 kind="ExternalInput").ap()
    d["out"] = nc.dram_tensor("out_0", [TOK, D], F32, kind="ExternalOutput").ap()
    program(nc, d)
    result = run_bass_kernel_spmd(nc, [feeds], core_ids=[0]).results[0]["out_0"]
    return result[S_TOK:].reshape(1, P_TOK, D), result[:S_TOK].reshape(1, S_TOK, D)
```

```python
import numpy as np
from contextlib import ExitStack
import concourse.bass as bass
from concourse import mybir

F32 = mybir.dt.float32
F32R = mybir.dt.float32r
BF16 = mybir.dt.bfloat16
U32 = mybir.dt.uint32
ACT = mybir.ActivationFunctionType
ALU = mybir.AluOpType
AX = mybir.AxisListType

P = 128
D = 1024
DT = D // P
S_TOK, P_TOK = 1024, 512
TOK = S_TOK + P_TOK
TILES = TOK // P
S_TILES = S_TOK // P
GROUP = 512
G_TILES = GROUP // P
GROUPS = TOK // GROUP
HD = 64
ROT_HALF = 8
GRID_W = 64
KEY_ROWS = 8
QA, KA, QB, KB = 4, 1, 4, 4
V_CHUNKS = 5
ROTATED = QA + KA
CHUNKS = QA + KA + QB + KB + V_CHUNKS
FIRST_V = CHUNKS - V_CHUNKS
AGAIN = [*range(ROTATED), FIRST_V]
EPS = 1e-6
SCALE = float(HD) ** -0.5
NEG = -1e30
EXPERTS = 16
DF = 2048
FT = DF // P
S_CAP, P_CAP = 2 * S_TOK // EXPERTS, 2 * P_TOK // EXPERTS
CAP = S_CAP + P_CAP
PROMPT_AT = 32


class Heads:

    def __init__(self, q, k, v, vt):
        self.q, self.k, self.v, self.vt = q, k, v, vt


class Route:

    def __init__(self, rows, best, at, gates, index):
        self.rows, self.best, self.at, self.gates, self.index = rows, best, at, gates, index


def buffers(nc, ctx):
    def sb(name, shape, dt=F32):
        return ctx.enter_context(nc.sbuf_tensor(name, shape, dt))

    def ps(name, shape, dt=F32):
        return ctx.enter_context(nc.psum_tensor(name, shape, dt))

    def sem(name):
        return ctx.enter_context(nc.semaphore(name))

    return sb, ps, sem


def three_pass(nc, out, stationary, moving, first, last):
    (sh, sl), (mh, ml) = stationary, moving
    nc.tensor.matmul(out, sh, mh, start=first, stop=False)
    nc.tensor.matmul(out, sh, ml, start=False, stop=False)
    return nc.tensor.matmul(out, sl, mh, start=False, stop=last)


START = 1
REFINE = 6


def inverse_root(dve, step, done, ss, rt, tmp, out, scale):
    mean, sq, corr = tmp
    dve.reciprocal(out, rt).then_inc(step, 1)
    dve.tensor_scalar(mean, ss, scale, EPS, ALU.mult, ALU.add).then_inc(step, 1)
    dve.wait_ge(step, done + 2)
    dve.tensor_tensor(sq, out, out, ALU.mult).then_inc(step, 1)
    dve.wait_ge(step, done + 3)
    dve.tensor_tensor(corr, sq, mean, ALU.mult).then_inc(step, 1)
    dve.wait_ge(step, done + 4)
    dve.tensor_scalar(sq, corr, -0.5, 1.5, ALU.mult, ALU.add).then_inc(step, 1)
    dve.wait_ge(step, done + 5)
    dve.tensor_tensor(out, out, sq, ALU.mult).then_inc(step, 1)
    dve.wait_ge(step, done + 6)


def project(nc, d, keep):
    ctx = ExitStack()
    with ctx:
        sb, ps, sem = buffers(nc, ctx)
        X_SLOTS, W_SLOTS, AHEAD = 2, 3, 2
        x = sb("pj_x", [P, X_SLOTS, D])
        xn = sb("pj_xn", [P, D])
        junk = sb("pj_junk", [P, D], BF16)
        gain = sb("pj_gain", [P, D])
        eps = sb("pj_eps", [P, 1])
        ss = sb("pj_ss", [P, G_TILES])
        rt = sb("pj_rt", [P, G_TILES])
        rs = sb("pj_rs", [P, G_TILES])
        tmp = sb("pj_tmp", [P, 3])
        ident = sb("pj_ident", [P, P])
        rot = sb("pj_rot", [P, P])
        x_hi = sb("pj_x_hi", [P, DT, GROUP], F32R)
        x_lo = sb("pj_x_lo", [P, DT, GROUP], F32R)
        w = sb("pj_w", [P, W_SLOTS, D])
        w_hi = sb("pj_w_hi", [P, W_SLOTS, DT, P], F32R)
        w_lo = sb("pj_w_lo", [P, W_SLOTS, DT, P], F32R)
        cos = sb("pj_cos", [P, GROUP])
        sin = sb("pj_sin", [P, GROUP])
        raw = sb("pj_raw", [P, 2, GROUP])
        turned = sb("pj_turned", [P, GROUP])
        bank = [ps(f"pj_ps{i}", [P, 512]) for i in range(8)]

        const_in = sem("pj_const_in")
        eps_set = sem("pj_eps_set")
        x_in = [sem(f"pj_x_in{i}") for i in range(X_SLOTS)]
        w_in = [sem(f"pj_w_in{i}") for i in range(W_SLOTS)]
        table_in = sem("pj_table_in")
        squared = sem("pj_squared")
        root = sem("pj_root")
        refined = sem("pj_refined")
        normed = sem("pj_normed")
        transposed = sem("pj_transposed")
        hi_x = sem("pj_hi_x")
        lo_x = sem("pj_lo_x")
        hi_w = sem("pj_hi_w")
        lo_w = sem("pj_lo_w")
        chunk_done = sem("pj_chunk_done")
        taken = sem("pj_taken")
        swapped = sem("pj_swapped")
        rotated = sem("pj_rotated")
        again_done = sem("pj_again_done")
        block = ctx.enter_context(nc.Block())

        @block.sync
        def _(sp):
            for dst, src in ((gain, d["g_attn"]), (ident, d["ident"]), (rot, d["rot"])):
                sp.dma_start(dst[:], src).then_inc(const_in, 16)
            with sp.Fori(0, GROUPS) as g:
                for t in range(X_SLOTS):
                    sp.wait_ge(normed, g * G_TILES + t + 1)
                    sp.dma_start(x[:, t % X_SLOTS, :], d["x"][g, t]).then_inc(x_in[t % X_SLOTS], 16)
                for n in range(W_SLOTS):
                    sp.wait_ge(lo_w, g * CHUNKS + n + 1)
                    sp.dma_start(w[:, n % W_SLOTS, :], d["w_in"][n]).then_inc(w_in[n % W_SLOTS], 16)
                for t in range(X_SLOTS, G_TILES):
                    sp.wait_ge(normed, g * G_TILES + t + 1)
                    sp.dma_start(x[:, t % X_SLOTS, :], d["x"][g, t]).then_inc(x_in[t % X_SLOTS], 16)
                sp.wait_ge(again_done, g * len(AGAIN) + 2)
                sp.dma_start(cos[:], d["cos"][g]).then_inc(table_in, 16)
                sp.dma_start(sin[:], d["sin"][g]).then_inc(table_in, 16)
                for n in range(W_SLOTS, CHUNKS):
                    sp.wait_ge(lo_w, g * CHUNKS + n + 1)
                    sp.dma_start(w[:, n % W_SLOTS, :], d["w_in"][n]).then_inc(w_in[n % W_SLOTS], 16)

        @block.gpsimd
        def _(pool):
            pool.memset(eps[:], EPS).then_inc(eps_set, 1)

        @block.scalar
        def _(act):
            act.wait_ge(eps_set, 1)
            act.sem_inc(taken, 2)
            act.sem_inc(squared, START)
            with act.Fori(0, GROUPS) as g:
                def split(n):
                    act.wait_ge(w_in[n % W_SLOTS], g * (16 * CHUNKS // W_SLOTS) + 16 * (n // W_SLOTS + 1))
                    act.activation(w_hi[:, n % W_SLOTS, :, :].rearrange("p j c -> p (j c)"),
                                   w[:, n % W_SLOTS, :], ACT.Copy).then_inc(hi_w, 1)

                for t in range(G_TILES):
                    act.wait_ge(x_in[t % X_SLOTS], g * (16 * G_TILES // X_SLOTS) + 16 * (t // X_SLOTS + 1))
                    act.wait_ge(squared, g * G_TILES + t + START)
                    act.activation(junk[:], x[:, t % X_SLOTS, :], ACT.Square,
                                   accum_out=ss[:, t:t + 1]).then_inc(squared, 1)
                    act.wait_ge(squared, g * G_TILES + t + 1 + START)
                    act.activation(rt[:, t:t + 1], ss[:, t:t + 1], ACT.Sqrt, bias=eps[:, 0:1],
                                   scale=1.0 / D).then_inc(root, 1)
                    if t == 1:
                        split(0)
                    if t == 2:
                        split(1)
                for t in range(G_TILES):
                    for h in range(2):
                        act.wait_ge(transposed, g * (2 * G_TILES) + 2 * t + h + 1 + START)
                        act.activation(x_hi[:, 4 * h:4 * h + 4, t * P:(t + 1) * P],
                                       bank[2 * (t % 2) + h][:].rearrange("p (j c) -> p j c", j=4),
                                       ACT.Copy).then_inc(hi_x, 1)
                for n in range(CHUNKS + 1):
                    if n > 0:
                        act.wait_ge(chunk_done, g * CHUNKS + n)
                    if n + AHEAD < CHUNKS and n + AHEAD >= 2:
                        split(n + AHEAD)
                    if n == 0:
                        continue
                    q = n - 1
                    src = bank[4 + q % 2][:]
                    if q in AGAIN:
                        m = AGAIN.index(q)
                        act.wait_ge(again_done, g * len(AGAIN) + m + 1)
                        act.activation(raw[:, m % 2, :], src, ACT.Copy,
                                       scale=SCALE if q < QA else 1.0).then_inc(taken, 1)
                    elif q < ROTATED + QB:
                        dst = keep.q[:, QA + q - ROTATED, bass.ds(g * GROUP, GROUP)]
                        act.activation(dst.rearrange("p (s r c) -> p r s c", s=STRIPS, r=Q_ROWS),
                                       src.rearrange("p (r s c) -> p r s c", s=STRIPS, r=Q_ROWS),
                                       ACT.Copy, scale=SCALE).then_inc(taken, 1)
                    elif q < FIRST_V:
                        act.activation(keep.k[:, KA + q - ROTATED - QB, bass.ds(g * GROUP, GROUP)], src,
                                       ACT.Copy).then_inc(taken, 1)
                    else:
                        act.activation(keep.vt[:, q - FIRST_V - 1, bass.ds(g * GROUP, GROUP)], src,
                                       ACT.Copy).then_inc(taken, 1)

        @block.vector
        def _(dve):
            dve.wait_ge(const_in, 48)
            dve.sem_inc(normed, X_SLOTS)
            dve.sem_inc(lo_w, W_SLOTS)
            dve.sem_inc(again_done, 2)
            dve.sem_inc(transposed, START)
            with dve.Fori(0, GROUPS) as g:
                def split(n):
                    dve.wait_ge(hi_w, g * CHUNKS + n + 1)
                    dve.tensor_tensor(w_lo[:, n % W_SLOTS, :, :].rearrange("p j c -> p (j c)"),
                                      w[:, n % W_SLOTS, :],
                                      w_hi[:, n % W_SLOTS, :, :].rearrange("p j c -> p (j c)").bitcast(F32),
                                      ALU.subtract).then_inc(lo_w, 1)

                def norm(t):
                    dve.wait_ge(root, g * G_TILES + t + 1)
                    inverse_root(dve, refined, (g * G_TILES + t) * REFINE, ss[:, t:t + 1], rt[:, t:t + 1],
                                 [tmp[:, i:i + 1] for i in range(3)], rs[:, t:t + 1], 1.0 / D)
                    dve.wait_ge(transposed, g * (2 * G_TILES) + 2 * t + START)
                    dve.scalar_tensor_tensor(out=xn[:], in0=x[:, t % X_SLOTS, :], scalar=rs[:, t:t + 1],
                                             in1=gain[:], op0=ALU.mult, op1=ALU.mult).then_inc(normed, 1)

                def low(t):
                    for h in range(2):
                        dve.wait_ge(hi_x, g * (2 * G_TILES) + 2 * t + h + 1)
                        dst = x_lo[:, 4 * h:4 * h + 4, t * P:(t + 1) * P]
                        dve.tensor_tensor(dst, bank[2 * (t % 2) + h][:].rearrange("p (j c) -> p j c", j=4),
                                          x_hi[:, 4 * h:4 * h + 4, t * P:(t + 1) * P].bitcast(F32),
                                          ALU.subtract).then_inc(lo_x, 1)

                norm(0)
                norm(1)
                split(0)
                norm(2)
                low(0)
                split(1)
                norm(3)
                for t in range(1, G_TILES):
                    low(t)
                for n in range(CHUNKS + 2):
                    if n + AHEAD < CHUNKS:
                        split(n + AHEAD)
                    q = n - 2
                    if q not in AGAIN:
                        continue
                    m = AGAIN.index(q)
                    again = bank[6 + m % 2][:]
                    if q == 0:
                        dve.wait_ge(table_in, g * 32 + 32)
                    dve.wait_ge(swapped, g * len(AGAIN) + m + 1)
                    if q < ROTATED:
                        dve.tensor_tensor(turned[:], again, sin[:], ALU.mult).then_inc(rotated, 1)
                        dve.tensor_tensor(raw[:, m % 2, :], raw[:, m % 2, :], cos[:],
                                          ALU.mult).then_inc(rotated, 1)
                        dve.wait_ge(rotated, g * (2 * ROTATED) + 2 * q + 2)
                        dst = (keep.q[:, q, bass.ds(g * GROUP, GROUP)] if q < QA
                               else keep.k[:, 0, bass.ds(g * GROUP, GROUP)])
                        dve.tensor_tensor(dst, raw[:, m % 2, :], turned[:], ALU.add).then_inc(again_done, 1)
                        dve.wait_ge(again_done, g * len(AGAIN) + m + 3)
                    else:
                        dve.tensor_copy(keep.v[:, bass.ds(g * G_TILES, G_TILES), :],
                                        again.rearrange("p (t c) -> p t c", t=G_TILES)).then_inc(again_done, 1)

        @block.tensor
        def _(pe):
            pe.wait_ge(const_in, 48)
            with pe.Fori(0, GROUPS) as g:
                for t in range(G_TILES):
                    pe.wait_ge(normed, g * G_TILES + t + 1 + X_SLOTS)
                    for h in range(2):
                        if t >= 2:
                            pe.wait_ge(lo_x, g * (2 * G_TILES) + 2 * (t - 2) + h + 1)
                        for j in range(4):
                            c0 = (4 * h + j) * P
                            last = nc.tensor.transpose(bank[2 * (t % 2) + h][:, j * P:(j + 1) * P],
                                                       xn[:, c0:c0 + P], ident[:])
                        last.then_inc(transposed, 1)
                for n in range(CHUNKS + 1):
                    if n < CHUNKS:
                        pe.wait_ge(lo_w, g * CHUNKS + n + 1 + W_SLOTS)
                        pe.wait_ge(taken, g * CHUNKS + n + 1)
                        if n == 0:
                            pe.wait_ge(lo_x, (g + 1) * (2 * G_TILES))
                        s = n % W_SLOTS
                        for j in range(DT):
                            last = three_pass(nc, bank[4 + n % 2][:], (w_hi[:, s, j, :], w_lo[:, s, j, :]),
                                              (x_hi[:, j, :], x_lo[:, j, :]), j == 0, j == DT - 1)
                        last.then_inc(chunk_done, 1)
                    q = n - 1
                    if q not in AGAIN:
                        continue
                    m = AGAIN.index(q)
                    pe.wait_ge(taken, g * CHUNKS + q + 3)
                    pe.wait_ge(again_done, g * len(AGAIN) + m + 1)
                    if q < ROTATED:
                        last = nc.tensor.matmul(bank[6 + m % 2][:], rot[:], raw[:, m % 2, :], start=True,
                                                stop=True)
                    else:
                        for t in range(G_TILES):
                            c = slice(t * P, (t + 1) * P)
                            last = nc.tensor.transpose(bank[6 + m % 2][:, c], raw[:, m % 2, c], ident[:])
                    last.then_inc(swapped, 1)


WINDOW_KEYS = 3 * P
PAIRS = 4
STRIPS, Q_ROWS, Q_COLS, K_COLS = 4, 8, 16, 32
KEY_COL = [0, 8, 24, 32]
BIAS_STRIPS = [0, 1, 3]
NEAR_KEYS = 12 * K_COLS
V_ROWS = P // K_COLS
NEAR_ROWS = [(0, 0, 12), (8, 4, 12), (0, 0, 8)]
GRID_H = [16, 16, 8]
V_TILES = [(0, V_ROWS * i) for i in range(4)] + [(S_TOK, V_ROWS * i) for i in range(2)]


class Window:

    def __init__(self, tile, first_key, keys, mask_at):
        self.window = True
        self.tile, self.first_key, self.keys, self.mask_at = tile, first_key, keys, mask_at


class Near:

    def __init__(self, number, kind, strip):
        self.window = False
        self.number, self.kind, self.strip = number, kind, strip
        self.group = 0 if kind < 2 else S_TOK
        self.q_row, self.k_row, rows = NEAR_ROWS[kind]
        self.keys = rows * K_COLS
        self.v_tiles = [V_TILES.index((self.group, self.k_row + V_ROWS * i)) for i in range(self.keys // P)]

    def grid(self, x, row, rows, col, cols):
        t0 = self.group + row * GRID_W
        return x[:, t0:t0 + rows * GRID_W].rearrange("p (r c) -> p r c", c=GRID_W)[:, :, col:col + cols]


def attention_blocks():
    window = []
    for first, tiles in ((0, S_TILES), (S_TILES, TILES - S_TILES)):
        for b in range(tiles):
            lo, hi = max(b - 1, 0), min(b + 1, tiles - 1)
            window.append(Window(first + b, first + lo, (hi - lo + 1) * P, (lo - b + 1) * P))
    near = [Near(3 * strip + kind, kind, strip) for strip in range(STRIPS) for kind in range(3)]
    lead = 2
    turns = [b for pair in zip(window[lead:], near) for b in pair]
    return window[:lead] + turns + near[len(window) - lead:]


def attend(nc, d, keep):
    ctx = ExitStack()
    with ctx:
        sb, ps, sem = buffers(nc, ctx)
        blocks = attention_blocks()
        units = [(b, pair, bi) for bi, b in enumerate(blocks) for pair in range(PAIRS)]
        N = len(units)
        window_units = [sum(x[0].window for x in units[:u]) for u in range(N)]
        near_start = {b.number: PAIRS * bi for bi, b in enumerate(blocks) if not b.window}
        PROBS, STATS, FLIPS, OUTS, BIASES, V_SLOTS = 6, 4, 6, 2, 3, 2 * len(V_TILES)

        v_step = {}
        for n in range(STRIPS * len(V_TILES)):
            strip, i = divmod(n, len(V_TILES))
            v_step[near_start[3 * (strip - 1) + i // 2] + 1 + 2 * (i % 2) if strip else n] = n

        bias = sb("at_bias", [P, BIASES, 2 * PAIRS, NEAR_KEYS])
        mask = sb("at_mask", [P, BIASES, NEAR_KEYS])
        band = sb("at_band", [P, WINDOW_KEYS])
        sink = sb("at_sink", [P, 2 * PAIRS])
        neg_sink = sb("at_neg_sink", [P, 2 * PAIRS])
        ident = sb("at_ident", [P, P])
        v_stage = sb("at_v_stage", [P, 2, PAIRS, P])
        v_near = sb("at_v_near", [P, V_SLOTS, PAIRS * P])
        probs = sb("at_probs", [P, PROBS, NEAR_KEYS])
        flipped = sb("at_flipped", [P, FLIPS, NEAR_KEYS])
        o = sb("at_o", [P, 2, 512])
        top, neg_top, at_sink, e_sink, sums, den, rden = (
            sb(f"at_{n}", [P, STATS, 2]) for n in ("top", "neg_top", "at_sink", "e_sink", "sums", "den", "rden"))
        score = [ps(f"at_score{h}", [P, 512]) for h in range(2)]
        flip_ps = [ps(f"at_flip{h}", [P, 512]) for h in range(2)]
        out_ps = [ps(f"at_out{i}", [P, 512]) for i in range(OUTS)]
        v_ps = [ps(f"at_v{i}", [P, 512]) for i in range(2)]

        const_in = sem("at_const_in")
        bias_in = [sem(f"at_bias_in{i}") for i in range(BIASES)]
        negated = sem("at_negated")
        masked = sem("at_masked")
        scored = sem("at_scored")
        added = sem("at_added")
        bounded = sem("at_bounded")
        sink_at = sem("at_sink_at")
        exped = sem("at_exped")
        sink_exped = sem("at_sink_exped")
        summed = sem("at_summed")
        inverted = sem("at_inverted")
        flipped_ps = sem("at_flipped_ps")
        copied = [sem("at_copied_act"), sem("at_copied_dve")]
        v_staged = sem("at_v_staged")
        v_turned = sem("at_v_turned")
        v_copied = sem("at_v_copied")
        weighed = sem("at_weighed")
        scaled = sem("at_scaled")
        stored = [sem(f"at_stored{i}") for i in range(2)]
        block = ctx.enter_context(nc.Block())

        @block.sync
        def _(sp):
            def load_bias(n):
                b = blocks[near_start[n] // PAIRS]
                slot, strip = n % BIASES, BIAS_STRIPS.index(1 if b.strip == 2 else b.strip)
                sp.dma_start(bias[:, slot, :, 0:b.keys],
                             d["near_bias"][b.kind, strip][:, :, 0:b.keys]).then_inc(bias_in[slot], 16)
                sp.dma_start(mask[:, slot, 0:b.keys],
                             d["near_mask"][b.kind, b.strip][:, 0:b.keys]).then_inc(bias_in[slot], 16)

            sp.dma_start(ident[:], d["ident"]).then_inc(const_in, 16)
            sp.dma_start(band[:], d["band"]).then_inc(const_in, 16)
            sp.dma_start(sink[:], d["sink"]).then_inc(const_in, 16)
            for n in range(BIASES):
                load_bias(n)
            for bi, b in enumerate(blocks):
                sp.wait_ge(scaled, PAIRS * (bi + 1))
                if b.window:
                    sp.dma_start(d["o"][b.tile][:, 0:512], o[:, bi % 2, :]).then_inc(stored[bi % 2], 16)
                else:
                    rows = d["o_grid"][(b.group // GRID_W) + b.q_row:(b.group // GRID_W) + b.q_row + Q_ROWS,
                                       b.strip * Q_COLS:(b.strip + 1) * Q_COLS, 512:1024]
                    sp.dma_start(rows, o[:, bi % 2, :]).then_inc(stored[bi % 2], 16)
                    if b.number + BIASES < len(near_start):
                        load_bias(b.number + BIASES)
            for i in range(2):
                sp.wait_ge(stored[i], 16 * len(blocks) // 2)

        @block.gpsimd
        def _(pool):
            def mask_bias(n):
                slot, keys = n % BIASES, blocks[near_start[n] // PAIRS].keys
                pool.wait_ge(bias_in[slot], 32 * (n // BIASES + 1))
                pool.tensor_tensor(bias[:, slot, :, 0:keys], bias[:, slot, :, 0:keys],
                                   mask[:, slot, 0:keys].unsqueeze(1).broadcast_to([P, 2 * PAIRS, keys]),
                                   ALU.add).then_inc(masked, 1)

            def stage_v(n):
                strip, i = divmod(n, len(V_TILES))
                t0 = V_TILES[i][0] + V_TILES[i][1] * GRID_W
                if n >= 2:
                    pool.wait_ge(v_turned, n - 1)
                for c in range(PAIRS):
                    src = keep.vt[:, c, t0:t0 + V_ROWS * GRID_W].rearrange("p (r c) -> p r c", c=GRID_W)
                    pool.tensor_copy(v_stage[:, n % 2, c, :].rearrange("p (r c) -> p r c", c=K_COLS),
                                     src[:, :, KEY_COL[strip]:KEY_COL[strip] + K_COLS]).then_inc(v_staged, 1)

            step_of = {n: u for u, n in v_step.items()}
            for u in range(N):
                for n in step_of:
                    if u == (step_of[n - 2] + 1 if n >= 2 else 0):
                        stage_v(n)
                for n in near_start:
                    if u == (near_start[n - BIASES] + PAIRS + 2 if n >= BIASES else len(V_TILES)):
                        mask_bias(n)

        def v_slots_free(eng, n):
            if n >= V_SLOTS:
                last_block = 3 * (n // len(V_TILES) - 1) - 1
                eng.wait_ge(weighed, near_start[last_block] + PAIRS)

        @block.scalar
        def _(act):
            for u in range(N + 1):
                if u < N:
                    b, r = units[u][0], u % STATS
                    act.wait_ge(bounded, u + 1)
                    for h in range(2):
                        p = probs[:, (2 * u + h) % PROBS, 0:b.keys]
                        act.activation(p, p, ACT.Exp, bias=neg_top[:, r, h:h + 1],
                                       accum_out=sums[:, r, h:h + 1]).then_inc(exped, 1)
                    if b.window:
                        act.wait_ge(sink_at, window_units[u] + 1)
                        act.activation(e_sink[:, r, :], at_sink[:, r, :], ACT.Exp).then_inc(sink_exped, 1)
                if u >= 1:
                    v = u - 1
                    keys = units[v][0].keys
                    act.wait_ge(flipped_ps, 2 * v + 1)
                    if 2 * v >= FLIPS:
                        act.wait_ge(weighed, v - FLIPS // 2 + 1)
                    act.activation(flipped[:, 2 * v % FLIPS, 0:keys], flip_ps[0][:, 0:keys],
                                   ACT.Copy).then_inc(copied[0], 1)
                if u in v_step:
                    n = v_step[u]
                    act.wait_ge(v_turned, n + 1)
                    v_slots_free(act, n)
                    act.activation(v_near[:, n % V_SLOTS, :], v_ps[n % 2][:], ACT.Copy).then_inc(v_copied, 1)

        @block.vector
        def _(dve):
            dve.wait_ge(const_in, 48)
            dve.tensor_scalar(neg_sink[:], sink[:], -1.0, None, ALU.mult).then_inc(negated, 1)
            dve.wait_ge(negated, 1)
            for u in range(N + 2):
                if u < N:
                    b, pair, bi = units[u]
                    r = u % STATS
                    if not b.window and pair == 0:
                        dve.wait_ge(masked, b.number + 1)
                    for h in range(2):
                        dve.wait_ge(scored, 2 * u + h + 1)
                        if 2 * u + h >= PROBS:
                            dve.wait_ge(flipped_ps, 2 * (u - PROBS // 2 + 1))
                        if b.window:
                            add = band[:, b.mask_at:b.mask_at + b.keys]
                        else:
                            add = bias[:, b.number % BIASES, 2 * pair + h, 0:b.keys]
                        dve.tensor_tensor_reduce(out=probs[:, (2 * u + h) % PROBS, 0:b.keys],
                                                 in0=score[h][:, 0:b.keys], in1=add, scale=1.0, scalar=-3.0e38,
                                                 op0=ALU.add, op1=ALU.max,
                                                 accum_out=top[:, r, h:h + 1]).then_inc(added, 1)
                    dve.wait_ge(added, 2 * u + 2)
                    if b.window:
                        mine = neg_sink[:, 2 * pair:2 * pair + 2]
                        dve.scalar_tensor_tensor(out=neg_top[:, r, :], in0=top[:, r, :], scalar=-1.0, in1=mine,
                                                 op0=ALU.mult, op1=ALU.min).then_inc(bounded, 1)
                        dve.wait_ge(bounded, u + 1)
                        dve.tensor_tensor(at_sink[:, r, :], neg_top[:, r, :], mine,
                                          ALU.subtract).then_inc(sink_at, 1)
                    else:
                        dve.tensor_scalar(neg_top[:, r, :], top[:, r, :], -1.0, None,
                                          ALU.mult).then_inc(bounded, 1)
                if 1 <= u < N + 1:
                    v, r = u - 1, (u - 1) % STATS
                    dve.wait_ge(exped, 2 * v + 2)
                    total = sums
                    if units[v][0].window:
                        dve.wait_ge(sink_exped, window_units[v] + 1)
                        dve.tensor_tensor(den[:, r, :], sums[:, r, :], e_sink[:, r, :],
                                          ALU.add).then_inc(summed, 1)
                        dve.wait_ge(summed, window_units[v] + 1)
                        total = den
                    dve.reciprocal(rden[:, r, :], total[:, r, :]).then_inc(inverted, 1)
                    keys = units[v][0].keys
                    dve.wait_ge(flipped_ps, 2 * v + 2)
                    if 2 * v >= FLIPS:
                        dve.wait_ge(weighed, v - FLIPS // 2 + 1)
                    dve.tensor_copy(flipped[:, (2 * v + 1) % FLIPS, 0:keys],
                                    flip_ps[1][:, 0:keys]).then_inc(copied[1], 1)
                if u >= 2:
                    v, r = u - 2, (u - 2) % STATS
                    b, pair, bi = units[v]
                    dve.wait_ge(weighed, v + 1)
                    dve.wait_ge(inverted, v + 1)
                    if pair == 0 and bi >= 2:
                        dve.wait_ge(stored[bi % 2], 16 * (bi // 2))
                    if b.window:
                        dst = o[:, bi % 2, :].rearrange("p (h c e) -> p h c e", h=2, c=PAIRS)[:, :, pair, :]
                    else:
                        dst = o[:, bi % 2, pair * P:(pair + 1) * P].rearrange("p (h e) -> p h e", h=2)
                    own = out_ps[v % OUTS][:, 0:2 * (P + HD)].rearrange("p (h x) -> p h x", h=2)[:, :, 0:HD]
                    dve.tensor_tensor(dst, own,
                                      rden[:, r, :].unsqueeze(2).broadcast_to([P, 2, HD]),
                                      ALU.mult).then_inc(scaled, 1)

        @block.tensor
        def _(pe):
            pe.wait_ge(const_in, 48)

            for u in range(N + 2):
                if u < N:
                    b, pair, bi = units[u]
                    for h in range(2):
                        if u >= 1:
                            pe.wait_ge(added, 2 * (u - 1) + h + 1)
                        rows = slice(h * HD, (h + 1) * HD)
                        if b.window:
                            q = keep.q[rows, pair, b.tile * P:(b.tile + 1) * P]
                            k = keep.k[rows, 0, b.first_key * P:b.first_key * P + b.keys]
                        else:
                            q0 = b.kind * GROUP + b.strip * P
                            q = keep.q[rows, QA + pair, q0:q0 + P]
                            k = b.grid(keep.k[rows, KA + pair, :], b.k_row, b.keys // K_COLS,
                                       KEY_COL[b.strip], K_COLS)
                        nc.tensor.matmul(score[h][:, 0:b.keys], q, k, start=True, stop=True).then_inc(scored, 1)
                if 1 <= u < N + 1:
                    v = u - 1
                    for h in range(2):
                        pe.wait_ge(exped, 2 * v + h + 1)
                        if v >= 1:
                            pe.wait_ge(copied[h], v)
                        for c in range(0, units[v][0].keys, P):
                            last = nc.tensor.transpose(flip_ps[h][:, c:c + P],
                                                       probs[:, (2 * v + h) % PROBS, c:c + P], ident[:])
                        last.then_inc(flipped_ps, 1)
                if u >= 2:
                    v = u - 2
                    b, pair, bi = units[v]
                    if not b.window and pair == 0:
                        pe.wait_ge(v_copied, len(V_TILES) * (b.strip + 1))
                    if v >= OUTS:
                        pe.wait_ge(scaled, v - OUTS + 1)
                    for h in range(2):
                        pe.wait_ge(copied[h], v + 1)
                        tiles = b.keys // P
                        for i in range(tiles):
                            if b.window:
                                values = keep.v[:, b.first_key + i, :]
                            else:
                                slot = (len(V_TILES) * b.strip + b.v_tiles[i]) % V_SLOTS
                                values = v_near[:, slot, pair * P:(pair + 1) * P]
                            last = nc.tensor.matmul(out_ps[v % OUTS][:, h * P:(h + 1) * P],
                                                    flipped[:, (2 * v + h) % FLIPS, i * P:(i + 1) * P],
                                                    values, start=i == 0, stop=i == tiles - 1)
                    last.then_inc(weighed, 1)
                if u in v_step:
                    n = v_step[u]
                    if n >= 2:
                        pe.wait_ge(v_copied, n - 1)
                    pe.wait_ge(v_staged, PAIRS * (n + 1))
                    for c in range(PAIRS):
                        last = nc.tensor.transpose(v_ps[n % 2][:, c * P:(c + 1) * P], v_stage[:, n % 2, c, :],
                                                   ident[:])
                    last.then_inc(v_turned, 1)


EARLY_ROUNDS = {TILES - 2: 2, TILES - 1: 3, TILES: 2}


def take_best(dve, route, steps, done, prompt, r):
    found, placed, dropped = steps
    first, width = (PROMPT_AT, P_TOK) if prompt else (0, S_TOK)
    part, c = slice(first, first + EXPERTS), slice(8 * r, 8 * r + 8)
    rows, other = (route.rows[part, i, 0:width] for i in (r % 2, 1 - r % 2))
    if done:
        dve.wait_ge(dropped, done)
    dve.max(route.best[part, c], rows).then_inc(found, 1)
    dve.wait_ge(found, done + 1)
    dve.max_index(route.at[part, c], route.best[part, c], rows).then_inc(placed, 1)
    dve.match_replace(other, route.best[part, c], rows, -2.0).then_inc(dropped, 1)


def mix(nc, d, route):
    ctx = ExitStack()
    with ctx:
        sb, ps, sem = buffers(nc, ctx)
        HALF = D // 2
        w = sb("mx_w", [P, DT, D])
        w_hi = sb("mx_w_hi", [P, DT, D], F32R)
        w_lo = sb("mx_w_lo", [P, DT, D], F32R)
        w_router = sb("mx_w_router", [P, DT, EXPERTS])
        gain_out = sb("mx_gain_out", [P, D])
        gain_ffn = sb("mx_gain_ffn", [P, D])
        ident = sb("mx_ident", [P, P])
        eps = sb("mx_eps", [P, 1])
        o = sb("mx_o", [P, 2, D])
        x = sb("mx_x", [P, 2, D])
        x2 = sb("mx_x2", [P, 2, D])
        h = sb("mx_h", [P, 2, D])
        merged = sb("mx_merged", [P, D])
        m_hi = sb("mx_m_hi", [P, 2, DT, P], F32R)
        m_lo = sb("mx_m_lo", [P, 2, DT, P], F32R)
        ht = sb("mx_ht", [P, DT, P])
        junk = sb("mx_junk", [P, D], BF16)
        ss1, rt1, rs1 = (sb(f"mx_{n}1", [P, 2]) for n in ("ss", "rt", "rs"))
        ss2, rt2, rs2 = (sb(f"mx_{n}2", [P, 1]) for n in ("ss", "rt", "rs"))
        tmp1, tmp2 = sb("mx_tmp1", [P, 3, 2]), sb("mx_tmp2", [P, 3, 1])
        neg_top, e_sum, e_inv = (sb(f"mx_{n}", [P, 1]) for n in ("neg_top", "e_sum", "e_inv"))
        e_aff, aff = sb("mx_e_aff", [P, EXPERTS]), sb("mx_aff", [P, 2, EXPERTS])
        bank = [ps(f"mx_ps{i}", [P, 512]) for i in range(8)]

        const_in = sem("mx_const_in")
        late_in = sem("mx_late_in")
        w_in = [sem(f"mx_w_in{i}") for i in range(DT)]
        ready = sem("mx_ready")
        o_in = [sem(f"mx_o_in{i}") for i in range(2)]
        x_in = [sem(f"mx_x_in{i}") for i in range(2)]
        hi_w, lo_w = sem("mx_hi_w"), sem("mx_lo_w")
        squared = sem("mx_squared")
        root1, root2 = sem("mx_root1"), sem("mx_root2")
        refined = sem("mx_refined")
        normed1, normed2 = sem("mx_normed1"), sem("mx_normed2")
        turned1, turned2 = sem("mx_turned1"), sem("mx_turned2")
        hi_m, lo_m = sem("mx_hi_m"), sem("mx_lo_m")
        projected = sem("mx_projected")
        summed = sem("mx_summed")
        ht_copied = sem("mx_ht_copied")
        routed = sem("mx_routed")
        topped, exped, inverted, shared = (sem(f"mx_{n}") for n in ("topped", "exped", "inverted", "shared"))
        aff_turned, rowed = sem("mx_aff_turned"), sem("mx_rowed")
        choice = [sem(f"mx_{n}") for n in ("found", "placed", "dropped")]
        x2_out = [sem(f"mx_x2_out{i}") for i in range(2)]
        h_out = [sem(f"mx_h_out{i}") for i in range(2)]
        block = ctx.enter_context(nc.Block())

        @block.sync
        def _(sp):
            def load(t):
                sp.wait_ge(normed1, 2 * (t - 1))
                sp.dma_start(o[:, t % 2, :], d["o"][t]).then_inc(o_in[t % 2], 16)
                sp.wait_ge(summed, 2 * (t - 1))
                sp.dma_start(x[:, t % 2, :], d["x_tiles"][t]).then_inc(x_in[t % 2], 16)

            sp.dma_start(o[:, 0, :], d["o"][0]).then_inc(o_in[0], 16)
            sp.dma_start(gain_out[:], d["g_out"]).then_inc(const_in, 16)
            sp.dma_start(ident[:], d["ident"]).then_inc(const_in, 16)
            for j in range(DT):
                sp.dma_start(w[:, j, :], d["w_out"][j]).then_inc(w_in[j], 16)
                if j == 3:
                    sp.dma_start(o[:, 1, :], d["o"][1]).then_inc(o_in[1], 16)
            for t in range(2):
                sp.dma_start(x[:, t, :], d["x_tiles"][t]).then_inc(x_in[t], 16)
            sp.dma_start(gain_ffn[:], d["g_ffn"]).then_inc(late_in, 16)
            sp.dma_start(w_router[:], d["w_router"]).then_inc(late_in, 16)
            for t in range(TILES):
                if t + 2 < TILES:
                    load(t + 2)
                sp.wait_ge(summed, 2 * (t + 1))
                sp.dma_start(d["acc_tiles"][t], x2[:, t % 2, :]).then_inc(x2_out[t % 2], 16)
                sp.wait_ge(normed2, t + 1)
                sp.dma_start(d["h_tiles"][t], h[:, t % 2, :]).then_inc(h_out[t % 2], 16)
            for i in range(2):
                sp.wait_ge(x2_out[i], 16 * TILES // 2)
                sp.wait_ge(h_out[i], 16 * TILES // 2)

        @block.gpsimd
        def _(pool):
            pool.memset(eps[:], EPS).then_inc(ready, 1)
            pool.memset(route.best[:], 0.0).then_inc(ready, 1)
            pool.memset(route.at[:], 0).then_inc(ready, 1)

        @block.scalar
        def _(act):
            squares = 0

            def square(src, dst):
                nonlocal squares
                act.wait_ge(squared, squares)
                act.activation(junk[:, 0:src.shape[-1]], src, ACT.Square, accum_out=dst).then_inc(squared, 1)
                squares += 1

            act.wait_ge(ready, 1)
            for s in range(-1, TILES + 2):
                t = s - 1
                if 0 <= t < TILES:
                    act.wait_ge(summed, 2 * (t + 1))
                    square(x2[:, t % 2, :], ss2[:])
                    act.wait_ge(squared, squares)
                    act.activation(rt2[:], ss2[:], ACT.Sqrt, bias=eps[:], scale=1.0 / D).then_inc(root2, 1)
                t = s + 1
                if t < TILES:
                    act.wait_ge(o_in[t % 2], 16 * (t // 2 + 1))
                    for k in range(2):
                        square(o[:, t % 2, k * HALF:(k + 1) * HALF], ss1[:, k:k + 1])
                    act.wait_ge(squared, squares)
                    act.activation(rt1[:], ss1[:], ACT.Sqrt, bias=eps[:], scale=1.0 / HALF).then_inc(root1, 1)
                if 0 <= s - 2 < TILES:
                    act.wait_ge(topped, s - 1)
                    act.activation(e_aff[:], bank[6][:, 0:EXPERTS], ACT.Exp, bias=neg_top[:],
                                   accum_out=e_sum[:]).then_inc(exped, 1)
                t = s - 1
                if 0 <= t < TILES:
                    for k in range(2):
                        act.wait_ge(turned2, 2 * t + k + 1)
                        if t >= 1:
                            act.wait_ge(routed, t)
                        act.activation(ht[:, 4 * k:4 * k + 4, :].rearrange("p j c -> p (j c)"),
                                       bank[6 + k][:], ACT.Copy).then_inc(ht_copied, 1)
                t = s + 1
                if t < TILES:
                    for k in range(2):
                        act.wait_ge(turned1, 2 * t + k + 1)
                        if t >= 2:
                            act.wait_ge(projected, t - 1)
                        act.activation(m_hi[:, t % 2, 4 * k:4 * k + 4, :].rearrange("p j c -> p (j c)"),
                                       bank[k][:], ACT.Copy).then_inc(hi_m, 1)
                    if t == 0:
                        for j in range(DT):
                            act.wait_ge(w_in[j], 16)
                            act.activation(w_hi[:, j, :], w[:, j, :], ACT.Copy).then_inc(hi_w, 1)
                t = s - 2
                if 0 <= t < TILES:
                    act.wait_ge(aff_turned, t + 1)
                    row, col = (0, t * P) if t < S_TILES else (PROMPT_AT, (t - S_TILES) * P)
                    act.activation(route.rows[row:row + EXPERTS, 0, col:col + P], bank[7][0:EXPERTS, 0:P],
                                   ACT.Copy).then_inc(rowed, 1)

        @block.vector
        def _(dve):
            refines = rounds = 0
            dve.wait_ge(const_in, 32)
            for s in range(-1, TILES + 2):
                t = s - 1
                if 0 <= t < TILES:
                    dve.wait_ge(x_in[t % 2], 16 * (t // 2 + 1))
                    if t >= 2:
                        dve.wait_ge(x2_out[t % 2], 16 * (t // 2))
                    dve.wait_ge(projected, t + 1)
                    if t == 0:
                        dve.wait_ge(late_in, 32)
                    for k in range(2):
                        c = slice(k * HALF, (k + 1) * HALF)
                        dve.tensor_tensor(x2[:, t % 2, c], bank[2 + 2 * (t % 2) + k][:], x[:, t % 2, c],
                                          ALU.add).then_inc(summed, 1)
                if 0 <= s - 2 < TILES:
                    dve.wait_ge(routed, s - 1)
                    dve.tensor_reduce(neg_top[:], bank[6][:, 0:EXPERTS], AX.X, ALU.max,
                                      negate=True).then_inc(topped, 1)
                if 0 <= t < TILES:
                    dve.wait_ge(root2, t + 1)
                    inverse_root(dve, refined, refines, ss2[:], rt2[:], [tmp2[:, i, :] for i in range(3)],
                                 rs2[:], 1.0 / D)
                    refines += REFINE
                    if t >= 2:
                        dve.wait_ge(h_out[t % 2], 16 * (t // 2))
                        dve.wait_ge(turned2, 2 * (t - 1))
                    dve.scalar_tensor_tensor(out=h[:, t % 2, :], in0=x2[:, t % 2, :], scalar=rs2[:],
                                             in1=gain_ffn[:], op0=ALU.mult, op1=ALU.mult).then_inc(normed2, 1)
                t = s + 1
                if t < TILES:
                    dve.wait_ge(root1, t + 1)
                    inverse_root(dve, refined, refines, ss1[:], rt1[:], [tmp1[:, i, :] for i in range(3)],
                                 rs1[:], 1.0 / HALF)
                    refines += REFINE
                    for k in range(2):
                        c = slice(k * HALF, (k + 1) * HALF)
                        dve.wait_ge(turned1, 2 * t)
                        dve.scalar_tensor_tensor(out=merged[:, c], in0=o[:, t % 2, c], scalar=rs1[:, k:k + 1],
                                                 in1=gain_out[:, c], op0=ALU.mult,
                                                 op1=ALU.mult).then_inc(normed1, 1)
                for _ in range(EARLY_ROUNDS.get(s, 0)):
                    if rounds == 0:
                        dve.wait_ge(ready, 3)
                        dve.wait_ge(rowed, S_TILES)
                    take_best(dve, route, choice, rounds, False, rounds)
                    rounds += 1
                if t < TILES:
                    for k in range(2):
                        dve.wait_ge(hi_m, 2 * t + k + 1)
                        jj = slice(4 * k, 4 * k + 4)
                        dve.tensor_tensor(m_lo[:, t % 2, jj, :].rearrange("p j c -> p (j c)"), bank[k][:],
                                          m_hi[:, t % 2, jj, :].rearrange("p j c -> p (j c)").bitcast(F32),
                                          ALU.subtract).then_inc(lo_m, 1)
                    if t == 0:
                        for j in range(DT):
                            dve.wait_ge(hi_w, j + 1)
                            dve.tensor_tensor(w_lo[:, j, :], w[:, j, :], w_hi[:, j, :].bitcast(F32),
                                              ALU.subtract).then_inc(lo_w, 1)
                t = s - 2
                if 0 <= t < TILES:
                    dve.wait_ge(exped, t + 1)
                    dve.reciprocal(e_inv[:], e_sum[:]).then_inc(inverted, 1)
                    dve.wait_ge(inverted, t + 1)
                    if t >= 2:
                        dve.wait_ge(aff_turned, t - 1)
                    dve.tensor_scalar(aff[:, t % 2, :], e_aff[:], e_inv[:], None, ALU.mult).then_inc(shared, 1)

        @block.tensor
        def _(pe):
            pe.wait_ge(const_in, 32)

            def project(t, k, tiles=range(DT)):
                c = slice(k * HALF, (k + 1) * HALF)
                for j in tiles:
                    if t == 0:
                        pe.wait_ge(lo_w, j + 1)
                    last = three_pass(nc, bank[2 + 2 * (t % 2) + k][:], (m_hi[:, t % 2, j, :], m_lo[:, t % 2, j, :]),
                                      (w_hi[:, j, c], w_lo[:, j, c]), j == 0, j == DT - 1)
                return last

            for s in range(-1, TILES + 2):
                if 0 <= s < TILES:
                    pe.wait_ge(lo_m, 2 * (s + 1))
                    if s >= 2:
                        pe.wait_ge(summed, 2 * (s - 1))
                    if s == 0:
                        for j in range(3):
                            project(s, 0, [j])
                            project(s, 1, [j])
                    else:
                        project(s, 0)
                        project(s, 1, range(0, 3))
                t = s - 1
                if 0 <= t < TILES:
                    pe.wait_ge(normed2, t + 1)
                    for k in range(2):
                        if t >= 1 and k == 0:
                            pe.wait_ge(exped, t)
                        if t >= 2 and k == 1:
                            pe.wait_ge(rowed, t - 1)
                        for j in range(4):
                            c0 = (4 * k + j) * P
                            last = nc.tensor.transpose(bank[6 + k][:, j * P:(j + 1) * P], h[:, t % 2, c0:c0 + P],
                                                       ident[:])
                        last.then_inc(turned2, 1)
                if 0 <= s < TILES:
                    for j in range(3, 7):
                        if s == 0:
                            project(s, 0, [j])
                        project(s, 1, [j])
                t = s + 1
                if t < TILES:
                    for k in range(2):
                        pe.wait_ge(normed1, 2 * t + k + 1)
                        if t >= 1:
                            pe.wait_ge(lo_m, 2 * (t - 1) + k + 1)
                        for j in range(4):
                            c0 = (4 * k + j) * P
                            last = nc.tensor.transpose(bank[k][:, j * P:(j + 1) * P], merged[:, c0:c0 + P],
                                                       ident[:])
                        last.then_inc(turned1, 1)
                if 0 <= s < TILES:
                    if s == 0:
                        project(s, 0, [DT - 1])
                    project(s, 1, [DT - 1]).then_inc(projected, 1)
                t = s - 1
                if 0 <= t < TILES:
                    pe.wait_ge(ht_copied, 2 * (t + 1))
                    for j in range(DT):
                        last = nc.tensor.matmul(bank[6][:, 0:EXPERTS], ht[:, j, :], w_router[:, j, :],
                                                start=j == 0, stop=j == DT - 1)
                    last.then_inc(routed, 1)
                t = s - 2
                if 0 <= t < TILES:
                    pe.wait_ge(shared, t + 1)
                    if t >= 1:
                        pe.wait_ge(rowed, t)
                    nc.tensor.transpose(bank[7][0:EXPERTS, 0:P], aff[:, t % 2, :],
                                        ident[:]).then_inc(aff_turned, 1)


ROWS = PROMPT_AT + EXPERTS
LATE_ROUNDS = (S_CAP + P_CAP) // 8 - sum(EARLY_ROUNDS.values())


class Choice:

    def __init__(self, sem, at_f, bank):
        self.steps = [sem(f"ch_{n}") for n in ("found", "placed", "dropped")]
        self.floated, self.turned, self.done = sem("ch_floated"), sem("ch_turned"), sem("ch_done")
        self.at_f, self.bank = at_f, bank

    READY = 6


def choose(dve, route, ch):
    early = sum(EARLY_ROUNDS.values())
    for r in range(early, S_CAP // 8):
        take_best(dve, route, ch.steps, r - early, False, r)
    for r in range(P_CAP // 8):
        take_best(dve, route, ch.steps, S_CAP // 8 - early + r, True, r)
    dve.wait_ge(ch.steps[1], LATE_ROUNDS)
    dve.tensor_copy(ch.at_f[:], route.at[:]).then_inc(ch.floated, 1)
    dve.wait_ge(ch.turned, 2)
    at, best = ch.bank
    dve.tensor_copy(route.index[:, 0, 0:EXPERTS], at[:, 0:EXPERTS]).then_inc(ch.done, 1)
    dve.tensor_copy(route.index[:, 0, EXPERTS:], at[:, 0:1]).then_inc(ch.done, 1)
    dve.tensor_scalar(route.index[:, 1, 0:EXPERTS], at[:, PROMPT_AT:ROWS], float(S_TOK), None,
                      ALU.add).then_inc(ch.done, 1)
    dve.tensor_scalar(route.index[:, 1, EXPERTS:], at[:, PROMPT_AT:PROMPT_AT + 1], float(S_TOK),
                      None, ALU.add).then_inc(ch.done, 1)
    dve.tensor_copy(route.gates[:, 0, :], best[:, 0:EXPERTS]).then_inc(ch.done, 1)
    dve.tensor_copy(route.gates[:, 1, :], best[:, PROMPT_AT:ROWS]).then_inc(ch.done, 1)


def turn_choice(nc, pe, route, ch, ident):
    at, best = ch.bank
    pe.wait_ge(ch.steps[0], LATE_ROUNDS)
    nc.tensor.transpose(best[:, 0:ROWS], route.best[:], ident[0:ROWS, 0:ROWS]).then_inc(ch.turned, 1)
    pe.wait_ge(ch.floated, 1)
    nc.tensor.transpose(at[:, 0:ROWS], ch.at_f[:], ident[0:ROWS, 0:ROWS]).then_inc(ch.turned, 1)


WIDE = 512
QUARTERS = DF // WIDE
HALVES = D // WIDE
ROWS4 = 4
W_COLS = ROWS4 * WIDE
UP_CHUNKS = 4 * QUARTERS
W_CHUNKS = UP_CHUNKS + HALVES * FT // ROWS4


def experts(nc, d, route):
    ctx = ExitStack()
    with ctx:
        sb, ps, sem = buffers(nc, ctx)
        SLOTS, AHEAD = 4, 3
        w = sb("ex_w", [P, SLOTS, W_COLS])
        w_hi = sb("ex_w_hi", [P, SLOTS, W_COLS], F32R)
        w_lo = sb("ex_w_lo", [P, SLOTS, W_COLS], F32R)
        ident = sb("ex_ident", [P, P])
        x_s = sb("ex_x_s", [S_CAP, D])
        x_p = sb("ex_x_p", [P_CAP, D])
        xs_hi = sb("ex_xs_hi", [P, DT, S_CAP], F32R)
        xs_lo = sb("ex_xs_lo", [P, DT, S_CAP], F32R)
        xp = sb("ex_xp", [P, DT, 2, P_CAP], F32R)
        silu_s = sb("ex_silu_s", [S_CAP, WIDE])
        silu_p = sb("ex_silu_p", [P_CAP, WIDE])
        gate_low = sb("ex_gate_low", [P_CAP, WIDE])
        gate_p_sum = sb("ex_gate_p_sum", [P_CAP, WIDE])
        up_low = sb("ex_up_low", [P_CAP, WIDE])
        up_p_sum = sb("ex_up_p_sum", [P_CAP, WIDE])
        hid_s = sb("ex_hid_s", [S_CAP, WIDE])
        hid_p = sb("ex_hid_p", [P_CAP, WIDE])
        hs_hi = sb("ex_hs_hi", [P, FT, S_CAP], F32R)
        hs_lo = sb("ex_hs_lo", [P, FT, S_CAP], F32R)
        hp = sb("ex_hp", [P, FT, 2, P_CAP], F32R)
        y_low = sb("ex_y_low", [P_CAP, WIDE])
        y_p_sum = sb("ex_y_p_sum", [P_CAP, WIDE])
        y_s = sb("ex_y_s", [S_CAP, D])
        y_p = sb("ex_y_p", [P_CAP, D])
        gather_s = sb("ex_gather_s", [S_CAP, 1], U32)
        gather_p = sb("ex_gather_p", [P_CAP, 1], U32)
        scatter_s = sb("ex_scatter_s", [S_CAP, 1], U32)
        scatter_p = sb("ex_scatter_p", [P_CAP, 1], U32)
        gate_s = sb("ex_gate_s", [S_CAP, 1])
        gate_p = sb("ex_gate_p", [P_CAP, 1])
        gate_ps = [ps(f"ex_gate_ps{i}", [P, WIDE]) for i in range(2)]
        up_ps = [ps(f"ex_up_ps{i}", [P, WIDE]) for i in range(2)]
        down_ps = [ps(f"ex_down_ps{i}", [P, WIDE]) for i in range(2)]
        turn_ps = [ps(f"ex_turn_ps{i}", [P, WIDE]) for i in range(2)]
        y_ps = [down_ps, up_ps]

        ch = Choice(sem, sb("ch_at_f", [ROWS, S_CAP]), [down_ps[0], down_ps[1]])
        const_in = sem("ex_const_in")
        w_in = [sem(f"ex_w_in{i}") for i in range(SLOTS)]
        hi_w = sem("ex_hi_w")
        lo_w = sem("ex_lo_w")
        chunk_done = sem("ex_chunk_done")
        gated_s, gate_lowered, gate_summed, gated_p = (
            sem(f"ex_{n}") for n in ("gated_s", "gate_lowered", "gate_summed", "gated_p"))
        hidden_s, up_lowered, up_summed, hidden_p = (
            sem(f"ex_{n}") for n in ("hidden_s", "up_lowered", "up_summed", "hidden_p"))
        h_turned, hi_h, lo_h = sem("ex_h_turned"), sem("ex_hi_h"), sem("ex_lo_h")
        x_turned, hi_x, lo_x = sem("ex_x_turned"), sem("ex_hi_x"), sem("ex_lo_x")
        y_lowered = sem("ex_y_lowered")
        y_summed = sem("ex_y_summed")
        s_scaled = sem("ex_s_scaled")
        p_scaled = sem("ex_p_scaled")
        columns = sem("ex_columns")
        y_free = sem("ex_y_free")
        released = sem("ex_released")
        pe_released = sem("ex_pe_released")
        gathered = sem("ex_gathered")
        scattered_s, scattered_p = sem("ex_scattered_s"), sem("ex_scattered_p")
        block = ctx.enter_context(nc.Block())
        FILLS = 3
        COPIES, FIRST_COPIES = 6, 2

        @block.sync
        def _(sp):
            sp.dma_start(ident[:], d["ident"]).then_inc(const_in, 16)
            with sp.Fori(0, EXPERTS) as e:
                for c in range(W_CHUNKS):
                    sp.wait_ge(lo_w, e * W_CHUNKS + c + 1)
                    sp.dma_start(w[:, c % SLOTS, :], d["w_experts"][e, c]).then_inc(w_in[c % SLOTS], 16)
            for c in range(AHEAD):
                sp.wait_ge(lo_w, EXPERTS * W_CHUNKS + c + 1)
                sp.dma_start(w[:, c % SLOTS, :], d["w_experts"][0, c]).then_inc(w_in[c % SLOTS], 16)

        @block.gpsimd
        def _(pool):
            def gather(e, copied):
                pool.tensor_copy(gather_s[:], route.index[:, 0, bass.ds(e, 1)]).then_inc(columns, 1)
                pool.tensor_copy(gather_p[:], route.index[0:P_CAP, 1, bass.ds(e, 1)]).then_inc(columns, 1)
                pool.wait_ge(columns, copied)
                pool.sem_inc(released, 1)
                for dst, at in ((x_s, gather_s), (x_p, gather_p)):
                    pool.indirect_dma_start(dst[:], None, d["h"],
                                            bass.IndirectOffsetOnAxis(at[:, 0:1], 0)).then_inc(gathered, 16)

            pool.sem_inc(y_free, START)
            pool.wait_ge(ch.done, ch.READY)
            gather(0, FIRST_COPIES)
            with pool.Fori(0, EXPERTS) as e:
                pool.wait_ge(x_turned, (e + 1) * FILLS)
                pool.wait_ge(gathered, (e + 1) * 32)
                gather(e + 1, FIRST_COPIES + e * COPIES + 2)
                pool.tensor_copy(scatter_s[:], route.index[:, 0, bass.ds(e, 1)]).then_inc(columns, 1)
                pool.tensor_copy(scatter_p[:], route.index[0:P_CAP, 1, bass.ds(e, 1)]).then_inc(columns, 1)
                pool.tensor_copy(gate_s[:], route.gates[:, 0, bass.ds(e, 1)]).then_inc(columns, 1)
                pool.tensor_copy(gate_p[:], route.gates[0:P_CAP, 1, bass.ds(e, 1)]).then_inc(columns, 1)
                pool.wait_ge(columns, FIRST_COPIES + (e + 1) * COPIES)
                pool.wait_ge(s_scaled, e * HALVES + HALVES + START)
                pool.sem_inc(released, 1)
                pool.indirect_dma_start(d["acc"], bass.IndirectOffsetOnAxis(scatter_s[:, 0:1], 0), y_s[:],
                                        None, compute_op=ALU.add).then_inc(scattered_s, 16)
                pool.wait_ge(p_scaled, (e + 1) * HALVES)
                pool.sem_inc(released, 1)
                pool.indirect_dma_start(d["acc"], bass.IndirectOffsetOnAxis(scatter_p[:, 0:1], 0), y_p[:],
                                        None, compute_op=ALU.add).then_inc(scattered_p, 16)
                pool.wait_ge(scattered_s, (e + 1) * 16)
                pool.wait_ge(scattered_p, (e + 1) * 16)
                pool.sem_inc(y_free, 1)
            pool.wait_ge(gathered, (EXPERTS + 1) * 32)

        GATE_STEP = [4 * q + 2 for q in range(QUARTERS)]
        UP_STEP = [4 * q + 4 for q in range(QUARTERS)]
        TURN_CHUNK = [4 * q + 5 for q in range(QUARTERS - 1)] + [UP_CHUNKS]
        X_CHUNK = [UP_CHUNKS + 2, UP_CHUNKS + 2, UP_CHUNKS + 4]
        DOWN_STEP = [UP_CHUNKS + 4, W_CHUNKS]

        def x_parts(i):
            if i < 2:
                j = slice(4 * i, 4 * i + 4)
                return (turn_ps[i][:].rearrange("p (j c) -> p j c", j=4), xs_hi[:, j, :], xs_lo[:, j, :])
            return turn_ps[0][:].rearrange("p (j c) -> p j c", j=DT), xp[:, :, 0, :], xp[:, :, 1, :]

        def h_parts(q, group):
            j = slice(4 * q, 4 * q + 4)
            if group == 0:
                return turn_ps[0][:].rearrange("p (j c) -> p j c", j=4), hs_hi[:, j, :], hs_lo[:, j, :]
            return (turn_ps[1][:, 0:4 * P_CAP].rearrange("p (j c) -> p j c", j=4), hp[:, j, 0, :], hp[:, j, 1, :])

        @block.scalar
        def _(act):
            def split(n0, c):
                act.wait_ge(w_in[c % SLOTS], n0 * (16 // SLOTS) + 16 * (c // SLOTS + 1))
                act.activation(w_hi[:, c % SLOTS, :], w[:, c % SLOTS, :], ACT.Copy).then_inc(hi_w, 1)

            def high_x(fills, i):
                src, hi, _ = x_parts(i)
                act.wait_ge(x_turned, fills + i + 1)
                act.activation(hi, src, ACT.Copy).then_inc(hi_x, 1)

            for c in range(AHEAD):
                split(0, c)
            for i in range(FILLS):
                high_x(0, i)
            with act.Fori(0, EXPERTS) as e:
                quarters, halves = e * QUARTERS, e * HALVES

                for c in range(W_CHUNKS + 1):
                    act.wait_ge(chunk_done, e * W_CHUNKS + c + START)
                    if c in GATE_STEP:
                        q = GATE_STEP.index(c)
                        if q:
                            act.wait_ge(hidden_s, quarters + q)
                        act.activation(silu_s[:], gate_ps[0][:], ACT.Silu).then_inc(gated_s, 1)
                        act.activation(gate_low[:], gate_ps[1][P_CAP:P, :], ACT.Copy).then_inc(gate_lowered, 1)
                    if c in UP_STEP:
                        act.activation(up_low[:], up_ps[1][P_CAP:P, :], ACT.Copy).then_inc(up_lowered, 1)
                    if c in DOWN_STEP:
                        k = DOWN_STEP.index(c)
                        if k == 0:
                            act.wait_ge(columns, FIRST_COPIES + (e + 1) * COPIES)
                            act.wait_ge(y_free, e + START)
                        else:
                            act.wait_ge(y_summed, halves + k + START)
                        act.activation(y_low[:], y_ps[k][1][P_CAP:P, :], ACT.Copy).then_inc(y_lowered, 1)
                        act.activation(y_s[:, k * WIDE:(k + 1) * WIDE], y_ps[k][0][:], ACT.Copy,
                                       scale=gate_s[:, 0:1]).then_inc(s_scaled, 1)
                    if c < W_CHUNKS:
                        split(e * W_CHUNKS, c + AHEAD)
                    if c in GATE_STEP:
                        q = GATE_STEP.index(c)
                        if q:
                            act.wait_ge(hidden_p, quarters + q)
                        act.wait_ge(gate_summed, quarters + q + 1)
                        act.activation(silu_p[:], gate_p_sum[:], ACT.Silu).then_inc(gated_p, 1)
                    if c - 1 in TURN_CHUNK:
                        q = TURN_CHUNK.index(c - 1)
                        for group in range(2):
                            src, hi, _ = h_parts(q, group)
                            act.wait_ge(h_turned, quarters * 2 + 2 * q + group + 1)
                            act.activation(hi, src, ACT.Copy).then_inc(hi_h, 1)
                    for i in range(FILLS):
                        if X_CHUNK[i] == c - 1:
                            high_x((e + 1) * FILLS, i)

        @block.vector
        def _(dve):
            def split(n0, c):
                dve.wait_ge(hi_w, n0 + c + 1)
                dve.tensor_tensor(w_lo[:, c % SLOTS, :], w[:, c % SLOTS, :], w_hi[:, c % SLOTS, :].bitcast(F32),
                                  ALU.subtract).then_inc(lo_w, 1)

            def low_x(fills, i):
                src, hi, lo = x_parts(i)
                dve.wait_ge(hi_x, fills + i + 1)
                dve.tensor_tensor(lo, src, hi.bitcast(F32), ALU.subtract).then_inc(lo_x, 1)

            dve.sem_inc(lo_w, SLOTS)
            choose(dve, route, ch)
            for c in range(AHEAD):
                split(0, c)
            for i in range(FILLS):
                low_x(0, i)
            with dve.Fori(0, EXPERTS) as e:
                quarters, halves = e * QUARTERS, e * HALVES

                for c in range(W_CHUNKS + 1):
                    if c in GATE_STEP:
                        q = GATE_STEP.index(c)
                        dve.wait_ge(gate_lowered, quarters + q + 1)
                        dve.tensor_tensor(gate_p_sum[:], gate_ps[1][0:P_CAP, :], gate_low[:],
                                          ALU.add).then_inc(gate_summed, 1)
                    if c in UP_STEP:
                        q = UP_STEP.index(c)
                        dve.wait_ge(chunk_done, e * W_CHUNKS + c + START)
                        dve.wait_ge(gated_s, quarters + q + 1)
                        dve.tensor_tensor(hid_s[:], up_ps[0][:], silu_s[:], ALU.mult).then_inc(hidden_s, 1)
                        dve.wait_ge(up_lowered, quarters + q + 1)
                        dve.tensor_tensor(up_p_sum[:], up_ps[1][0:P_CAP, :], up_low[:],
                                          ALU.add).then_inc(up_summed, 1)
                        dve.wait_ge(up_summed, quarters + q + 1)
                        dve.wait_ge(gated_p, quarters + q + 1)
                        dve.tensor_tensor(hid_p[:], up_p_sum[:], silu_p[:], ALU.mult).then_inc(hidden_p, 1)
                    if c in DOWN_STEP:
                        k = DOWN_STEP.index(c)
                        dve.wait_ge(y_lowered, halves + k + 1)
                        dve.tensor_tensor(y_p_sum[:], y_ps[k][1][0:P_CAP, :], y_low[:],
                                          ALU.add).then_inc(y_summed, 1)
                        dve.wait_ge(y_summed, halves + k + 1 + START)
                        if k == 0:
                            dve.wait_ge(columns, FIRST_COPIES + (e + 1) * COPIES)
                            dve.wait_ge(y_free, e + START)
                        dve.tensor_scalar(y_p[:, k * WIDE:(k + 1) * WIDE], y_p_sum[:], gate_p[:, 0:1], None,
                                          ALU.mult).then_inc(p_scaled, 1)
                    if c < W_CHUNKS:
                        split(e * W_CHUNKS, c + AHEAD)
                    if c - 1 in TURN_CHUNK:
                        q = TURN_CHUNK.index(c - 1)
                        for group in range(2):
                            src, hi, lo = h_parts(q, group)
                            dve.wait_ge(hi_h, quarters * 2 + 2 * q + group + 1)
                            dve.tensor_tensor(lo, src, hi.bitcast(F32), ALU.subtract).then_inc(lo_h, 1)
                    for i in range(FILLS):
                        if X_CHUNK[i] == c - 1:
                            low_x((e + 1) * FILLS, i)

        @block.tensor
        def _(pe):
            def turn_x(i):
                for j in range(DT if i == 2 else 4):
                    c = slice((4 * (i % 2) + j) * P, (4 * (i % 2) + j + 1) * P)
                    if i < 2:
                        last = nc.tensor.transpose(turn_ps[i][:, j * P:(j + 1) * P], x_s[:, c], ident[:])
                    else:
                        last = nc.tensor.transpose(turn_ps[0][:, j * P_CAP:(j + 1) * P_CAP], x_p[:, c],
                                                   ident[0:P_CAP, 0:P_CAP])
                last.then_inc(x_turned, 1)

            pe.wait_ge(const_in, 16)
            pe.sem_inc(chunk_done, START)
            pe.sem_inc(s_scaled, START)
            pe.sem_inc(y_summed, START)
            turn_choice(nc, pe, route, ch, ident)
            pe.wait_ge(gathered, 32)
            turn_x(0)
            turn_x(1)
            pe.wait_ge(lo_x, 1)
            turn_x(2)
            with pe.Fori(0, EXPERTS) as e:
                quarters, halves = e * QUARTERS, e * HALVES

                def multiply(c, out, sample, prompt, first_row, rows):
                    slot = c % SLOTS
                    for r in range(ROWS4):
                        n = first_row + r
                        hi, lo = (x[:, slot, r * WIDE:(r + 1) * WIDE] for x in (w_hi, w_lo))
                        s_hi, s_lo = (x[:, n, :] for x in sample)
                        both = prompt[:, n, :, :].rearrange("p k c -> p (k c)")
                        start, stop = n == 0, n == rows - 1
                        nc.tensor.matmul(out[0][:], s_hi, hi, start=start, stop=False)
                        nc.tensor.matmul(out[0][:], s_hi, lo, start=False, stop=False)
                        nc.tensor.matmul(out[0][:], s_lo, hi, start=False, stop=stop)
                        nc.tensor.matmul(out[1][:], both, hi, start=start, stop=False)
                        last = nc.tensor.matmul(out[1][:], both, lo, start=False, stop=stop)
                    last.then_inc(chunk_done, 1)

                pe.wait_ge(lo_x, (e + 1) * FILLS)
                for c in range(W_CHUNKS):
                    pe.wait_ge(lo_w, e * W_CHUNKS + c + 1 + SLOTS)
                    if c < UP_CHUNKS:
                        q, kind, half = c // 4, c // 2 % 2, c % 2
                        if half == 0 and q and kind == 0:
                            pe.wait_ge(gated_s, quarters + q)
                            pe.wait_ge(gate_summed, quarters + q)
                        elif half == 0 and q:
                            pe.wait_ge(hidden_s, quarters + q)
                            pe.wait_ge(up_summed, quarters + q)
                        elif half == 0 and kind:
                            pe.wait_ge(s_scaled, halves + START)
                            pe.wait_ge(y_summed, halves + START)
                        multiply(c, up_ps if kind else gate_ps, (xs_hi, xs_lo), xp, ROWS4 * half, DT)
                    else:
                        k, part = divmod(c - UP_CHUNKS, FT // ROWS4)
                        if k == 0:
                            pe.wait_ge(lo_h, quarters * 2 + 2 * (part + 1))
                        multiply(c, y_ps[k], (hs_hi, hs_lo), hp, ROWS4 * part, FT)
                    if c in TURN_CHUNK:
                        q = TURN_CHUNK.index(c)
                        pe.wait_ge(hidden_p, quarters + q + 1)
                        if q:
                            pe.wait_ge(lo_h, quarters * 2 + 2 * q)
                        for group, (hid, rows) in enumerate(((hid_s, S_CAP), (hid_p, P_CAP))):
                            for j in range(4):
                                last = nc.tensor.transpose(turn_ps[group][:, j * rows:(j + 1) * rows],
                                                           hid[:, j * P:(j + 1) * P], ident[0:rows, 0:rows])
                            last.then_inc(h_turned, 1)
                    if c == X_CHUNK[0]:
                        pe.wait_ge(gathered, (e + 2) * 32)
                        pe.wait_ge(lo_h, quarters * 2 + 2 * QUARTERS)
                        turn_x(0)
                        turn_x(1)
                    if c == X_CHUNK[2]:
                        pe.wait_ge(lo_x, (e + 1) * FILLS + 1)
                        pe.sem_inc(pe_released, 1)
                        turn_x(2)


def finish(nc, d):
    ctx = ExitStack()
    with ctx:
        sb, ps, sem = buffers(nc, ctx)
        gain = sb("fi_gain", [P, D])
        eps = sb("fi_eps", [P, 1])
        x = sb("fi_x", [P, TILES, D])
        junk = sb("fi_junk", [P, D], BF16)
        ss, rt, rs = (sb(f"fi_{n}", [P, TILES]) for n in ("ss", "rt", "rs"))
        tmp = sb("fi_tmp", [P, 3])
        const_in, eps_set = sem("fi_const_in"), sem("fi_eps_set")
        x_in = [sem(f"fi_x_in{t}") for t in range(TILES)]
        stored = sem("fi_stored")
        squared, root, refined, normed = sem("fi_squared"), sem("fi_root"), sem("fi_refined"), sem("fi_normed")
        block = ctx.enter_context(nc.Block())

        @block.sync
        def _(sp):
            sp.dma_start(x[:, 0, :], d["acc_tiles"][0]).then_inc(x_in[0], 16)
            sp.dma_start(gain[:], d["g_final"]).then_inc(const_in, 16)
            for t in range(1, TILES):
                sp.dma_start(x[:, t, :], d["acc_tiles"][t]).then_inc(x_in[t], 16)
            for t in range(TILES):
                sp.wait_ge(normed, t + 1)
                sp.dma_start(d["out_tiles"][t], x[:, t, :]).then_inc(stored, 16)
            sp.wait_ge(stored, 16 * TILES)

        @block.gpsimd
        def _(pool):
            pool.memset(eps[:], EPS).then_inc(eps_set, 1)

        @block.scalar
        def _(act):
            act.wait_ge(eps_set, 1)
            for t in range(TILES):
                act.wait_ge(x_in[t], 16)
                act.wait_ge(squared, t)
                act.activation(junk[:], x[:, t, :], ACT.Square, accum_out=ss[:, t:t + 1]).then_inc(squared, 1)
                act.wait_ge(squared, t + 1)
                act.activation(rt[:, t:t + 1], ss[:, t:t + 1], ACT.Sqrt, bias=eps[:],
                               scale=1.0 / D).then_inc(root, 1)

        @block.vector
        def _(dve):
            dve.wait_ge(const_in, 16)
            for t in range(TILES):
                dve.wait_ge(root, t + 1)
                inverse_root(dve, refined, t * REFINE, ss[:, t:t + 1], rt[:, t:t + 1],
                             [tmp[:, i:i + 1] for i in range(3)], rs[:, t:t + 1], 1.0 / D)
                dve.scalar_tensor_tensor(out=x[:, t, :], in0=x[:, t, :], scalar=rs[:, t:t + 1],
                                         in1=gain[:], op0=ALU.mult, op1=ALU.mult).then_inc(normed, 1)


def program(nc, d):
    d["o"] = nc.dram_tensor("o_scratch", [TILES, P, D], F32, kind="Internal").ap()
    d["o_grid"] = d["o"].rearrange("t (r c) e -> (t r) c e", c=GRID_W)
    d["h"] = nc.dram_tensor("h_scratch", [TOK, D], F32, kind="Internal").ap()
    d["acc"] = nc.dram_tensor("acc_scratch", [TOK, D], F32, kind="Internal").ap()
    d["x_tiles"] = d["x"].rearrange("g t p e -> (g t) p e")
    d["h_tiles"] = d["h"].rearrange("(t p) e -> t p e", p=P)
    d["acc_tiles"] = d["acc"].rearrange("(t p) e -> t p e", p=P)
    d["out_tiles"] = d["out"].rearrange("(t p) e -> t p e", p=P)
    with ExitStack() as outer:
        sb, _, _ = buffers(nc, outer)
        keep = Heads(
            q=sb("q", [P, QA + QB, TOK]),
            k=sb("k", [P, KA + KB, TOK]),
            v=sb("v", [P, TILES, P]),
            vt=sb("vt", [P, V_CHUNKS - 1, TOK]),
        )
        project(nc, d, keep)
        attend(nc, d, keep)
    with ExitStack() as outer:
        sb, _, _ = buffers(nc, outer)
        route = Route(
            rows=sb("rows", [PROMPT_AT + EXPERTS, 2, S_TOK]),
            best=sb("best", [PROMPT_AT + EXPERTS, S_CAP]),
            at=sb("best_at", [PROMPT_AT + EXPERTS, S_CAP], U32),
            gates=sb("gates", [P, 2, EXPERTS]),
            index=sb("index", [P, 2, EXPERTS + 1], U32),
        )
        mix(nc, d, route)
        experts(nc, d, route)
    finish(nc, d)


def columns():
    qa0, ka0, va0 = 0, 512, 640
    qb0, kb0, vb0 = 768, 1280, 1792
    span = lambda a, n=P: list(range(a, a + n))
    out = [span(qa0 + HD * c, HD) + span(qa0 + HD * (c + 4), HD) for c in range(QA)]
    out += [span(ka0)]
    out += [span(qb0 + P * c) for c in range(QB)] + [span(kb0 + P * c) for c in range(KB)]
    out += [span(va0)] + [span(vb0 + P * c) for c in range(V_CHUNKS - 1)]
    return np.array(out)


def near_positions(kind, strip):
    q0, k0, _ = NEAR_ROWS[kind]
    q, k = np.arange(P)[:, None], np.arange(NEAR_KEYS)[None, :]
    return q0 + q // Q_COLS, Q_COLS * strip + q % Q_COLS, k0 + k // K_COLS, KEY_COL[strip] + k % K_COLS


def constants():
    c = {}
    inv = np.float32(500000.0) ** (-(np.arange(ROT_HALF, dtype=np.float32) * np.float32(2.0))
                                   / np.float32(2 * ROT_HALF))
    ang = (np.arange(S_TOK, dtype=np.float32)[:, None] * inv[None, :]).astype(np.float32)
    cos = np.ones((P, S_TOK), np.float32)
    sin = np.zeros((P, S_TOK), np.float32)
    rot = np.zeros((P, P), np.float32)
    for p in range(P):
        dd = p % HD
        if dd < 2 * ROT_HALF:
            cos[p] = np.cos(ang[:, dd % ROT_HALF])
            sin[p] = np.sin(ang[:, dd % ROT_HALF])
            if dd < ROT_HALF:
                rot[p + ROT_HALF, p] = -1.0
            else:
                rot[p - ROT_HALF, p] = 1.0
    c["cos"] = np.stack([cos[:, 0:512], cos[:, 512:1024], cos[:, 0:512]])
    c["sin"] = np.stack([sin[:, 0:512], sin[:, 512:1024], sin[:, 0:512]])
    c["rot"] = rot
    i, j = np.arange(P)[:, None], np.arange(3 * P)[None, :]
    c["band"] = np.where(np.abs(j - P - i) <= P, 0.0, NEG).astype(np.float32)
    masks = []
    for kind in range(len(NEAR_ROWS)):
        rows = GRID_H[kind]
        for strip in range(STRIPS):
            qr, qc, kr, kc = near_positions(kind, strip)
            rs, cs = np.clip(qr - 4, 0, rows - KEY_ROWS), np.clip(qc - 8, 0, GRID_W - 16)
            ok = (kr >= rs) & (kr < rs + KEY_ROWS) & (kc >= cs) & (kc < cs + 16)
            masks.append(np.where(ok, 0.0, NEG).astype(np.float32))
    c["near_mask"] = np.stack(masks).reshape(len(NEAR_ROWS), STRIPS, P, NEAR_KEYS)
    c["ident"] = np.eye(P, dtype=np.float32)
    return c


def layouts(i):
    a = {}
    x = np.concatenate([i["x_sample"][0], i["x_prompt"][0]])
    a["x"] = x.reshape(GROUPS, G_TILES, P, D)
    w = i["w_in"][0].reshape(DT, P, -1)[:, :, columns()]
    a["w_in"] = w.transpose(2, 1, 0, 3).reshape(CHUNKS, P, D)
    bias = []
    for kind in range(len(NEAR_ROWS)):
        for strip in BIAS_STRIPS:
            qr, qc, kr, kc = near_positions(kind, strip)
            ridx = np.clip(kr - qr + KEY_ROWS - 1, 0, 2 * KEY_ROWS - 2)
            cidx = np.clip(kc - qc + 15, 0, 30)
            bias.append(i["rpb_b"][0][:, ridx, cidx].transpose(1, 0, 2))
    a["near_bias"] = np.stack(bias).reshape(len(NEAR_ROWS), len(BIAS_STRIPS), P, 2 * PAIRS, NEAR_KEYS)
    order = [h for c in range(PAIRS) for h in (c, c + PAIRS)]
    a["sink"] = np.broadcast_to(i["sink_a"][0][order], (P, 2 * PAIRS))
    a["w_out"] = i["w_out"][0].reshape(DT, P, D)
    a["w_router"] = i["w_router"][0].reshape(DT, P, EXPERTS).transpose(1, 0, 2)
    up = np.stack([i["w_gate"][0], i["w_up"][0]], axis=1)
    up = up.reshape(EXPERTS, 2, 2, ROWS4, P, QUARTERS, WIDE).transpose(0, 5, 1, 2, 4, 3, 6)
    down = i["w_down"][0].reshape(EXPERTS, FT // ROWS4, ROWS4, P, HALVES, WIDE).transpose(0, 4, 1, 3, 2, 5)
    a["w_experts"] = np.concatenate([up.reshape(EXPERTS, UP_CHUNKS, P, W_COLS),
                                     down.reshape(EXPERTS, W_CHUNKS - UP_CHUNKS, P, W_COLS)], axis=1)
    a["g_out"] = np.broadcast_to(np.concatenate([i["g_out_a"][0], i["g_out_b"][0]]), (P, D))
    a["g_ffn"] = np.broadcast_to(i["g_ffn"][0], (P, D))
    a["g_final"] = np.broadcast_to(i["g_final"], (P, D))
    a["g_attn"] = np.broadcast_to(i["g_attn"][0], (P, D))
    return a


def kernel(**inputs):
    import concourse.bacc as bacc
    from concourse.bass_utils import run_bass_kernel_spmd

    given = {name: np.asarray(value) for name, value in inputs.items()}
    arrays = {**layouts(given), **constants()}
    nc = bacc.Bacc("TRN2", target_bir_lowering=False, num_devices=1)
    feeds, d = {}, {}
    for name, value in arrays.items():
        value = np.ascontiguousarray(value)
        feeds[f"in_{name}"] = value
        d[name] = nc.dram_tensor(f"in_{name}", value.shape, mybir.dt.from_np(value.dtype),
                                 kind="ExternalInput").ap()
    d["out"] = nc.dram_tensor("out_0", [TOK, D], F32, kind="ExternalOutput").ap()
    program(nc, d)
    result = run_bass_kernel_spmd(nc, [feeds], core_ids=[0]).results[0]["out_0"]
    return result[S_TOK:].reshape(1, P_TOK, D), result[:S_TOK].reshape(1, S_TOK, D)
```
